# Optimizing a Trainium2 kernel written in Bass

```python
import math
import jax, jax.numpy as jnp
from jax import lax
import numpy as np

D_MODEL = 1024
BATCH = 1
SEQ = 256
DEPTH = 2

HEAD_DIM = 64
BLOCK = 128
ROPE_THETA = 10000.0
EPS = 1e-6
NEG = -1e30
N_BRANCH = 3
BRANCH_WIDTH = D_MODEL // 4

SB_HEADS = BRANCH_WIDTH // HEAD_DIM

MLA_HEADS = 4
MLA_V = BRANCH_WIDTH // MLA_HEADS
MLA_NOPE = 64
MLA_ROPE = 32
MLA_Q_LORA = D_MODEL // 4
MLA_KV_LORA = D_MODEL // 8

DIL_CONFIGS = ((128, 1), (512, 4), (2048, 16))
DIL_HEADS = BRANCH_WIDTH // HEAD_DIM

SB_COLS = 3 * SB_HEADS * HEAD_DIM
MLA_COLS = MLA_Q_LORA + MLA_KV_LORA + MLA_ROPE
DIL_COLS = len(DIL_CONFIGS) * 3 * DIL_HEADS * HEAD_DIM
GATE_COLS = N_BRANCH * D_MODEL
IN_COLS = SB_COLS + MLA_COLS + DIL_COLS + GATE_COLS

N_GROUPS = 4
EXPERTS_PER_GROUP = 4
N_EXPERTS = N_GROUPS * EXPERTS_PER_GROUP
TOP_K = 2
D_EXPERT = D_MODEL // 4

kernel_name = "hybrid_sb_mla_dilated_hmoe"

def rmsnorm(x, g):
    xf = x.astype(jnp.float32)
    y = xf * lax.rsqrt(jnp.mean(xf * xf, axis=-1, keepdims=True) + EPS)
    return (y * g.astype(jnp.float32)).astype(x.dtype)

def apply_rope(x, pos):
    dim = x.shape[-1]
    inv_freq = ROPE_THETA ** (-jnp.arange(0, dim, 2, dtype=jnp.float32) / dim)
    ang = pos.astype(jnp.float32)[:, :, None, None] * inv_freq
    cos, sin = jnp.cos(ang), jnp.sin(ang)
    x1, x2 = jnp.split(x.astype(jnp.float32), 2, axis=-1)
    return jnp.concatenate([x1 * cos - x2 * sin, x1 * sin + x2 * cos], axis=-1).astype(x.dtype)

def query_blocks(t):
    b, s, h, d = t.shape
    return t.reshape(b, s // BLOCK, BLOCK, h, d).transpose(1, 0, 2, 3, 4)

def merge_blocks(t):
    nb, b, q, h, d = t.shape
    return t.transpose(1, 0, 2, 3, 4).reshape(b, nb * q, h, d)

def stick_breaking_attention(q, k, v):
    b, s, h, dh = q.shape
    scale = dh ** -0.5
    key_pos = jnp.arange(s)
    starts = jnp.arange(s // BLOCK) * BLOCK

    def one_block(args):
        q_blk, start = args
        z = jnp.einsum('bqhd,bkhd->bhqk', q_blk, k, preferred_element_type=jnp.float32) * scale
        qpos = start + jnp.arange(BLOCK)
        strict = key_pos[None, :] < qpos[:, None]
        log_beta = jax.nn.log_sigmoid(z)
        log_one_minus = jnp.where(strict, jax.nn.log_sigmoid(-z), 0.0)
        after = lax.cumsum(log_one_minus, axis=3, reverse=True) - log_one_minus
        w = jnp.where(strict, jnp.exp(log_beta + after), 0.0)
        return jnp.einsum('bhqk,bkhd->bqhd', w.astype(v.dtype), v)

    return merge_blocks(lax.map(one_block, (query_blocks(q), starts)))

def mla_attention(c_q, c_kv, k_rope_raw, pos, g_q_lat, w_uq, g_kv_lat, w_ukv):
    b, s, _ = c_q.shape
    q = (rmsnorm(c_q, g_q_lat) @ w_uq).reshape(b, s, MLA_HEADS, MLA_NOPE + MLA_ROPE)
    q_nope = q[..., :MLA_NOPE]
    q_rope = apply_rope(q[..., MLA_NOPE:], pos)
    kv = (rmsnorm(c_kv, g_kv_lat) @ w_ukv).reshape(b, s, MLA_HEADS, MLA_NOPE + MLA_V)
    k_nope, v = kv[..., :MLA_NOPE], kv[..., MLA_NOPE:]
    k_rope = apply_rope(k_rope_raw[:, :, None, :], pos)[:, :, 0]
    scale = (MLA_NOPE + MLA_ROPE) ** -0.5
    key_pos = jnp.arange(s)
    starts = jnp.arange(s // BLOCK) * BLOCK

    def one_block(args):
        qn, qr, start = args
        sc = (jnp.einsum('bqhd,bkhd->bhqk', qn, k_nope, preferred_element_type=jnp.float32)
              + jnp.einsum('bqhd,bkd->bhqk', qr, k_rope, preferred_element_type=jnp.float32)) * scale
        qpos = start + jnp.arange(BLOCK)
        causal = key_pos[None, :] <= qpos[:, None]
        p = jax.nn.softmax(jnp.where(causal, sc, NEG), axis=-1)
        return jnp.einsum('bhqk,bkhd->bqhd', p.astype(v.dtype), v)

    return merge_blocks(lax.map(one_block, (query_blocks(q_nope), query_blocks(q_rope), starts)))

def dilated_group_attention(q, k, v, window, dilation):
    b, s, h, dh = q.shape
    L = window // dilation
    s_pad = -(-s // window) * window
    n = s_pad // dilation
    nb = n // L

    def strided_blocks(t):
        t = jnp.pad(t, ((0, 0), (0, s_pad - s), (0, 0), (0, 0)))
        t = t.reshape(b, n, dilation, h, dh).transpose(0, 2, 1, 3, 4)
        return t.reshape(b, dilation, nb, L, h, dh)

    qb, kb, vb = strided_blocks(q), strided_blocks(k), strided_blocks(v)
    prev = lambda t: jnp.pad(t, ((0, 0), (0, 0), (1, 0), (0, 0), (0, 0), (0, 0)))[:, :, :-1]
    kw = jnp.concatenate([prev(kb), kb], axis=3)
    vw = jnp.concatenate([prev(vb), vb], axis=3)
    sc = jnp.einsum('brnqhd,brnkhd->brnhqk', qb, kw, preferred_element_type=jnp.float32) * (dh ** -0.5)
    a = jnp.arange(L)[:, None]
    c = jnp.arange(2 * L)[None, :]
    band = (c >= a) & (c <= a + L)
    has_prev = jnp.arange(nb) > 0
    valid = band[None] & ((c >= L)[None] | has_prev[:, None, None])
    sc = jnp.where(valid[None, None, :, None], sc, NEG)
    lse = jax.nn.logsumexp(sc, axis=-1)
    p = jnp.exp(sc - lse[..., None])
    o = jnp.einsum('brnhqk,brnkhd->brnqhd', p.astype(v.dtype), vw)
    o = o.reshape(b, dilation, n, h, dh).transpose(0, 2, 1, 3, 4).reshape(b, s_pad, h, dh)[:, :s]
    lse = lse.transpose(0, 1, 2, 4, 3).reshape(b, dilation, n, h).transpose(0, 2, 1, 3).reshape(b, s_pad, h)[:, :s]
    return o, lse

def hybrid_mixer(h, pos, w_in, g_q_lat, w_uq, g_kv_lat, w_ukv, w_branch, w_out):
    b, s, _ = h.shape
    proj = h @ w_in
    sb, mla, dil, gate_logits = jnp.split(
        proj, [SB_COLS, SB_COLS + MLA_COLS, SB_COLS + MLA_COLS + DIL_COLS], axis=-1)

    sb = sb.reshape(b, s, 3, SB_HEADS, HEAD_DIM)
    o_a = stick_breaking_attention(sb[:, :, 0], sb[:, :, 1], sb[:, :, 2])

    c_q, c_kv, k_rope_raw = jnp.split(mla, [MLA_Q_LORA, MLA_Q_LORA + MLA_KV_LORA], axis=-1)
    o_b = mla_attention(c_q, c_kv, k_rope_raw, pos, g_q_lat, w_uq, g_kv_lat, w_ukv)

    dil = dil.reshape(b, s, len(DIL_CONFIGS), 3, DIL_HEADS, HEAD_DIM)
    outs, lses = [], []
    for gi, (window, dilation) in enumerate(DIL_CONFIGS):
        qg = apply_rope(dil[:, :, gi, 0], pos)
        kg = apply_rope(dil[:, :, gi, 1], pos)
        o_g, lse_g = dilated_group_attention(qg, kg, dil[:, :, gi, 2], window, dilation)
        outs.append(o_g)
        lses.append(lse_g)
    alpha = jax.nn.softmax(jnp.stack(lses, axis=0), axis=0)
    o_c = jnp.sum(alpha[..., None] * jnp.stack(outs, axis=0).astype(jnp.float32), axis=0).astype(h.dtype)

    branches = jnp.stack([o_a.reshape(b, s, BRANCH_WIDTH),
                          o_b.reshape(b, s, BRANCH_WIDTH),
                          o_c.reshape(b, s, BRANCH_WIDTH)], axis=2)
    branch_d = jnp.einsum('bsnc,ncd->bsnd', branches, w_branch)
    gates = jax.nn.sigmoid(gate_logits.reshape(b, s, N_BRANCH, D_MODEL).astype(jnp.float32)).astype(h.dtype)
    merged = jnp.sum(gates * branch_d, axis=2)
    return merged @ w_out

def hierarchical_moe(h, w_group_router, b_group_router, w_expert_router, b_expert_router,
                     w_gate, w_up, w_down):
    b, s, d = h.shape
    t = h.reshape(b * s, d)
    group_logits = (t @ w_group_router).astype(jnp.float32) + b_group_router.astype(jnp.float32)
    group_prob = jax.nn.softmax(group_logits, axis=-1)
    g_top = jnp.argmax(group_logits, axis=-1)
    p_group = jnp.take_along_axis(group_prob, g_top[:, None], axis=-1)
    expert_logits = ((t @ w_expert_router).astype(jnp.float32)
                     + b_expert_router.astype(jnp.float32)).reshape(-1, N_GROUPS, EXPERTS_PER_GROUP)
    in_group = jnp.take_along_axis(expert_logits, g_top[:, None, None], axis=1)[:, 0]
    top_logit, top_i = lax.top_k(in_group, TOP_K)
    top_p = jax.nn.softmax(top_logit, axis=-1)
    expert_ids = g_top[:, None] * EXPERTS_PER_GROUP + top_i
    weights = p_group * top_p
    combine = jnp.sum(jax.nn.one_hot(expert_ids, N_EXPERTS, dtype=jnp.float32) * weights[..., None], axis=1)
    hid = jax.nn.silu(jnp.einsum('td,edf->tef', t, w_gate)) * jnp.einsum('td,edf->tef', t, w_up)
    out = jnp.einsum('tef,efd->td', hid * combine[:, :, None].astype(hid.dtype), w_down)
    return out.reshape(b, s, d)

def setup_inputs(seed: int = 0) -> dict:
    key = jax.random.key(seed)
    ks = jax.random.split(key, 24)
    f32 = jnp.float32

    def nrm(k, shape, fan_in):
        return jax.random.normal(k, shape, f32) * (fan_in ** -0.5)

    def gain(k, shape):
        return 1.0 + 0.02 * jax.random.normal(k, shape, f32)

    x = jax.random.normal(ks[0], (BATCH, SEQ, D_MODEL), f32)
    offset = jax.random.randint(ks[1], (BATCH, 1), 0, 4096, dtype=jnp.int32)
    positions = offset + jnp.arange(SEQ, dtype=jnp.int32)[None, :]
    return {
        "x": x,
        "positions": positions,
        "g_mix": gain(ks[2], (DEPTH, D_MODEL)),
        "w_in": nrm(ks[3], (DEPTH, D_MODEL, IN_COLS), D_MODEL),
        "g_q_lat": gain(ks[4], (DEPTH, MLA_Q_LORA)),
        "w_uq": nrm(ks[5], (DEPTH, MLA_Q_LORA, MLA_HEADS * (MLA_NOPE + MLA_ROPE)), MLA_Q_LORA),
        "g_kv_lat": gain(ks[6], (DEPTH, MLA_KV_LORA)),
        "w_ukv": nrm(ks[7], (DEPTH, MLA_KV_LORA, MLA_HEADS * (MLA_NOPE + MLA_V)), MLA_KV_LORA),
        "w_branch": nrm(ks[8], (DEPTH, N_BRANCH, BRANCH_WIDTH, D_MODEL), BRANCH_WIDTH),
        "w_out": nrm(ks[9], (DEPTH, D_MODEL, D_MODEL), D_MODEL),
        "g_ffn": gain(ks[10], (DEPTH, D_MODEL)),
        "w_group_router": nrm(ks[11], (DEPTH, D_MODEL, N_GROUPS), D_MODEL),
        "b_group_router": 0.01 * jax.random.normal(ks[12], (DEPTH, N_GROUPS), f32),
        "w_expert_router": nrm(ks[13], (DEPTH, D_MODEL, N_EXPERTS), D_MODEL),
        "b_expert_router": 0.01 * jax.random.normal(ks[14], (DEPTH, N_EXPERTS), f32),
        "w_gate": nrm(ks[15], (DEPTH, N_EXPERTS, D_MODEL, D_EXPERT), D_MODEL),
        "w_up": nrm(ks[16], (DEPTH, N_EXPERTS, D_MODEL, D_EXPERT), D_MODEL),
        "w_down": nrm(ks[17], (DEPTH, N_EXPERTS, D_EXPERT, D_MODEL), D_EXPERT),
        "g_final": gain(ks[18], (D_MODEL,)),
    }

def reference(x, positions, g_mix, w_in, g_q_lat, w_uq, g_kv_lat, w_ukv, w_branch, w_out, g_ffn,
              w_group_router, b_group_router, w_expert_router, b_expert_router,
              w_gate, w_up, w_down, g_final):
    for l in range(DEPTH):
        h = rmsnorm(x, g_mix[l])
        x = x + hybrid_mixer(h, positions, w_in[l], g_q_lat[l], w_uq[l], g_kv_lat[l], w_ukv[l],
                             w_branch[l], w_out[l])
        h = rmsnorm(x, g_ffn[l])
        x = x + hierarchical_moe(h, w_group_router[l], b_group_router[l], w_expert_router[l],
                                 b_expert_router[l], w_gate[l], w_up[l], w_down[l])
    return rmsnorm(x, g_final)


_drawn_inputs = setup_inputs


def setup_inputs(seed=0):
    import zlib

    import numpy as np

    out = dict(_drawn_inputs(seed))
    spreads = {}
    factors = {'g_q_lat': 8.0,
     'g_kv_lat': 6.711,
     'b_group_router': 3.814,
     'b_expert_router': 4.615,
     'g_final': 2.904}
    for name, (base, spread) in spreads.items():
        noise = np.random.default_rng([zlib.crc32(name.encode()), seed]).standard_normal(out[name].shape)
        drawn = base * np.exp(spread * noise) if base else spread * noise
        out[name] = __import__('jax').numpy.asarray(drawn.astype(out[name].dtype))
    for name, factor in factors.items():
        out[name] = (out[name] * factor).astype(out[name].dtype)
    return out
```

```python
import numpy as np

D_MODEL = 1024
SEQ = 256
DEPTH = 2
HEAD = 64
THETA = 10000.0
EPS = 1e-6
NEG = -1e30
P = 128
TILES = SEQ // P
CHUNKS = D_MODEL // P
BRANCHES = 3
WIDTH = D_MODEL // 4
HEADS = WIDTH // HEAD
NOPE, ROPE = 64, 32
MLA_QK = NOPE + ROPE
GROUPS, PER_GROUP = 4, 4
EXPERTS = GROUPS * PER_GROUP
DIL = ((128, 1), (512, 4), (2048, 16))

UNIT = CHUNKS * WIDTH
RAW_SLOTS = 4
SPLIT_SLOTS = 3

MIX = ["sbq", "sbk", "sbv", "cq", "ckv", "kr", "d0q", "d0k", "d0v", "uq", "ukv",
       "d1q", "d1k", "d1v", "d2q", "d2k", "d2v"]
MIX += [f"gate{i}" for i in range(12)] + [f"branch{n}" for n in range(3)] + [f"out{i}" for i in range(4)]
FILL = {"ckv": CHUNKS * 128, "kr": CHUNKS * MLA_QK, "uq": 2 * HEADS * MLA_QK, "ukv": 512}
MIX_UNITS = len(MIX)
MOE = ["A0", "B0", "A1", "B1", "D0", "A2", "B2", "D1", "A3", "B3", "D2", "D3"]
GROUP_UNITS = len(MOE)
MOE_UNITS = GROUPS * GROUP_UNITS
assert MIX_UNITS % RAW_SLOTS == MIX_UNITS % SPLIT_SLOTS == 0
assert GROUP_UNITS % RAW_SLOTS == GROUP_UNITS % SPLIT_SLOTS == 0

PJ = [(f"norm{c}", "dve") for c in range(4)]
PJ += [(n, "act") for n in ("sbq", "sbk", "sbv", "cq", "ckv", "kr", "d0q")]
PJ += [("sw_kr", "dve"), ("d0k", "act"), ("d0v", "act"), ("sw_d0q", "dve"), ("sw_d0k", "dve"),
       ("uq0", "act"), ("uq1", "act"), ("ukv0", "act"), ("ukv1", "act"), ("ukvv", "act"),
       ("sw_mq0", "dve"), ("sw_mq1", "dve"), ("d1q", "act"), ("d1k", "act"), ("d1v", "act"),
       ("sw_d1q", "dve"), ("d2q", "act"), ("sw_d1k", "dve"), ("d2k", "act"), ("d2v", "act"),
       ("sw_d2q", "dve"), ("gate0", "act"), ("sw_d2k", "dve")]
PJ += [(f"gate{i}", "act") for i in range(1, 12)]
PJ += [(f"branch{n}_{j}", "dve") for n in range(3) for j in range(4)]
PJ += [(f"moe_norm{c}", "dve") for c in range(4)] + [("logits", "dve"), ("rank", "dve")]
PJ_INDEX = {name: i for i, (name, _) in enumerate(PJ)}
PJ_BANKS = 3
PJ_TOTAL = {who: sum(w == who for _, w in PJ) for who in ("act", "dve")}

LAST_FILL = [{"uq": "uq1", "ukv": "ukvv"}.get(name, f"{name}_3" if name[:6] == "branch" else name)
             for name in MIX[:-4]]

ROTATIONS = ["sw_kr", "sw_d0q", "sw_d0k", "sw_mq0", "sw_mq1", "sw_d1q", "sw_d1k", "sw_d2q", "sw_d2k"]

JOBS = [("mla", h, None) for h in range(HEADS)] + [("dil", h, b) for h in range(HEADS) for b in range(2)]

CONST = {}
_at = 0
for _name, _n in (("ident", 128), ("before", 128), ("later", 128), ("ones", 128), ("swap64", 128),
                  ("swap96", 128), ("iota", 128), ("sb_mask", 256), ("mla_mask", 384),
                  ("dil_mask0", 384), ("dil_mask1", 768), ("freq64", 1), ("freq96", 1),
                  ("first4", 4), ("first16", 16), ("minus_half", 2)):
    CONST[_name] = (_at, _at + _n)
    _at += _n
CONST_COLS = _at
PARAM = {"g_mix": (0, 8), "g_ffn": (8, 16), "g_q": (16, 18), "g_kv": (18, 19), "router": (19, 179),
         "bias": (179, 199)}
PARAM_COLS = 199

DVE_LAYER_STEPS = 74
DVE_GROUP_STEPS = 4
ACT_LAYER_STEPS = 2


def build(nc, x, positions, mix_weights, moe_weights, params, g_final, constants, out):
    import concourse.bass as bass
    from concourse import mybir
    from contextlib import ExitStack

    F32, F32R, I32 = mybir.dt.float32, mybir.dt.float32r, mybir.dt.int32
    ALU, ACT, AX = mybir.AluOpType, mybir.ActivationFunctionType, mybir.AxisListType

    cursor = [(nc.sbuf_base + 63) // 64 * 64]

    def place(name, shape, dtype=F32, at=None):
        size = 4 * int(np.prod(shape[1:]))
        if at is None:
            at = cursor[0]
            cursor[0] += (size + 31) // 32 * 32
        return nc.alloc_sbuf_tensor_at(name, shape, dtype, offset=at), at

    raw, _ = place("raw", [P, RAW_SLOTS, UNIT])
    w_hi, _ = place("w_hi", [P, SPLIT_SLOTS, UNIT], F32R)
    w_lo, _ = place("w_lo", [P, SPLIT_SLOTS, UNIT], F32R)
    xt, _ = place("xt", [P, TILES, D_MODEL])
    hn, hn_at = place("hn", [P, TILES, D_MODEL])
    o_hi, o_lo = [None] * 3, [None] * 3
    for n in (1, 2):
        o_hi[n], _ = place(f"o_hi{n}", [P, 2, SEQ], F32R, hn_at + (n - 1) * 4096)
        o_lo[n], _ = place(f"o_lo{n}", [P, 2, SEQ], F32R, hn_at + (n - 1) * 4096 + 2048)
    hTf, hTf_at = place("hTf", [P, CHUNKS, SEQ])
    lat, _ = place("lat", [P, 3, SEQ], F32, hTf_at)
    lat_sq, _ = place("lat_sq", [P, 3, SEQ], F32, hTf_at + 3072)
    lat_rs, _ = place("lat_rs", [P, 2, SEQ], F32, hTf_at + 6144)
    merged, _ = place("merged", [P, CHUNKS, SEQ], F32, hTf_at)
    hT_hi, hh_at = place("hT_hi", [P, CHUNKS, SEQ], F32R)
    hT_lo, hl_at = place("hT_lo", [P, CHUNKS, SEQ], F32R)
    m_hi, _ = place("m_hi", [P, CHUNKS, SEQ], F32R, hh_at)
    m_lo, _ = place("m_lo", [P, CHUNKS, SEQ], F32R, hl_at)
    cst, _ = place("cst", [P, CONST_COLS])
    all_params, _ = place("all_params", [P, DEPTH, PARAM_COLS])
    par, _ = place("par", [P, PARAM_COLS])
    gfin, _ = place("gfin", [P, D_MODEL])
    rope = {k: place(f"rope_{k}", [P, SEQ])[0] for k in ("cos64", "sin64", "cos96", "sin96")}
    stat, _ = place("stat", [P, 64])
    rounds_f, _ = place("rounds_f", [1, 1])
    rounds, _ = place("rounds", [1, 1], I32)
    region = cursor[0]
    gates, gates_at = place("gates", [P, BRANCHES, CHUNKS, SEQ])
    sb_a, _ = place("sb_a", [P, 1536], F32, gates_at)
    sb_b, _ = place("sb_b", [P, 1536], F32, gates_at + 6144)
    sb_c, _ = place("sb_c", [P, 1536], F32, gates_at + 12288)
    lat_hi, _ = place("lat_hi", [P, 3, SEQ], F32R, gates_at + 18432)
    lat_lo, _ = place("lat_lo", [P, 3, SEQ], F32R, gates_at + 21504)
    dq, dk, dv = ([place(f"d{g}{c}", [P, 2, SEQ])[0] for g in range(3)] for c in "qkv")
    mq, _ = place("mq", [P, HEADS, SEQ])
    mk, _ = place("mk", [P, HEADS, SEQ])
    mv, _ = place("mv", [P, TILES, WIDTH])
    o_hi[0], _ = place("o_hi0", [P, 2, SEQ], F32R)
    o_lo[0], _ = place("o_lo0", [P, 2, SEQ], F32R)
    sbq, sbq_at = place("sbq", [P, 2, SEQ])
    sbk, _ = place("sbk", [P, 2, SEQ])
    sbv, _ = place("sbv", [P, TILES, WIDTH])
    probs, _ = place("probs", [P, 2, 768], F32, sbq_at)
    pT, pT_at = place("pT", [P, 6, P])
    kr, _ = place("kr", [P, SEQ], F32, pT_at)
    rope_tmp, _ = place("rope_tmp", [P, 2, SEQ], F32, pT_at + 1024)
    pos_i, _ = place("pos_i", [P, SEQ], I32, gates_at)
    pos_f, _ = place("pos_f", [P, SEQ], F32, gates_at + 1024)
    angle, _ = place("angle", [P, SEQ], F32, gates_at + 2048)
    turns, _ = place("turns", [P, SEQ], F32, gates_at + 3072)
    end_mix = cursor[0]
    cursor[0] = region
    xgf, _ = place("xgf", [P, CHUNKS, P])
    xg_hi, _ = place("xg_hi", [P, CHUNKS, P], F32R)
    xg_lo, _ = place("xg_lo", [P, CHUNKS, P], F32R)
    sel, _ = place("sel", [P, TILES, P])
    selT, _ = place("selT", [P, TILES, P], F32R)
    th, _ = place("th", [P, 2, WIDTH])
    hid, _ = place("hid", [P, 2, WIDTH])
    hidT_hi, _ = place("hidT_hi", [P, 2, 2, P], F32R)
    hidT_lo, _ = place("hidT_lo", [P, 2, 2, P], F32R)
    y_hi, _ = place("y_hi", [P, D_MODEL], F32R)
    y_lo, _ = place("y_lo", [P, D_MODEL], F32R)
    comb, _ = place("comb", [P, TILES, EXPERTS])
    gcomb, _ = place("gcomb", [P, TILES, PER_GROUP])
    scomb, _ = place("scomb", [P, PER_GROUP])
    slot_of, _ = place("slot_of", [P, TILES * GROUPS])
    gl, _ = place("gl", [P, TILES, GROUPS])
    el, _ = place("el", [P, TILES, EXPERTS])
    r1, _ = place("r1", [P, TILES, EXPERTS])
    r2, _ = place("r2", [P, TILES, EXPERTS])
    hot1, _ = place("hot1", [P, TILES, EXPERTS])
    hot2, _ = place("hot2", [P, TILES, EXPERTS])
    ghot, _ = place("ghot", [P, TILES, GROUPS])
    g1, _ = place("g1", [P, TILES, GROUPS])
    assert max(end_mix, cursor[0]) <= nc.sbuf_usable_end, (end_mix, cursor[0], nc.sbuf_usable_end)

    def const(name, rows=P):
        a, b = CONST[name]
        return cst[0:rows, a:b]

    def param(name):
        a, b = PARAM[name]
        return par[:, a:b]

    ctx = ExitStack()
    with ctx:
        ps = ctx.enter_context(nc.psum_tensor("ps", [P, 8, 512], F32))

        def sem(name):
            return ctx.enter_context(nc.semaphore(name))

        OV = ps[:, 3, :]
        SC = ps[:, 4:6, :].rearrange("p b n -> p (b n)")
        TR = ps[:, 6:8, :].rearrange("p b n -> p (b n)")
        GU = [ps[:, 0, :], ps[:, 1, :]]
        GU2 = ps[:, 0:2, :].rearrange("p b n -> p (b n)")
        HT = [ps[:, 2, 0:256], ps[:, 3, 0:256]]

        TR2 = ps[:, 6:8, 0:256]

        def alone(eng, sem_, value):
            eng.wait_ge(sem_, value)
            eng.sem_inc(waits_carried, 1)

        def two(ap):
            return ap.rearrange("p (b n) -> p b n", b=2)

        def pj(name):
            return ps[:, PJ_INDEX[name] % PJ_BANKS, :]

        weights_landed = [sem(f"weights_landed{s}") for s in range(RAW_SLOTS)]
        x_landed, const_landed, params_landed = sem("x_landed"), sem("const_landed"), sem("params_landed")
        pos_landed, gfin_landed, out_stored = sem("pos_landed"), sem("gfin_landed"), sem("out_stored")
        split_hi, split_lo = sem("split_hi"), sem("split_lo")
        out_used, a_used, d_used = sem("out_used"), sem("a_used"), sem("d_used")
        pj_full, pj_act, pj_dve = sem("pj_full"), sem("pj_act"), sem("pj_dve")
        dve_chain, dve_gchain, dve_pchain = sem("dve_chain"), sem("dve_gchain"), sem("dve_pchain")
        act_chain = sem("act_chain")
        setup_chain, sin_done, tables_ready, angle_ready = (sem("setup_chain"), sem("sin_done"),
                                                            sem("tables_ready"), sem("angle_ready"))
        params_ready = sem("params_ready")
        squares_ready, rstd_ready, hn_ready, pool_chain = (sem("squares_ready"), sem("rstd_ready"),
                                                           sem("hn_ready"), sem("pool_chain"))
        hT_hi_ready, hT_ready = sem("hT_hi_ready"), sem("hT_ready")
        z_full, softplus_ready, strict_ready, after_full = (sem("z_full"), sem("softplus_ready"),
                                                            sem("strict_ready"), sem("after_full"))
        logw_ready, wexp_ready, w_ready = sem("logw_ready"), sem("wexp_ready"), sem("w_ready")
        lat_sq_ready, lat_full, lat_var, lat_rstd = (sem("lat_sq_ready"), sem("lat_full"),
                                                     sem("lat_var"), sem("lat_rstd"))
        lat_normed, lat_hi_ready, lat_ready = sem("lat_normed"), sem("lat_hi_ready"), sem("lat_ready")
        roped = sem("roped")
        sc_full, max_ready, exp_ready, probs_ready = (sem("sc_full"), sem("max_ready"),
                                                      sem("exp_ready"), sem("probs_ready"))
        tr_full, pT_ready = sem("tr_full"), sem("pT_ready")
        av_done = sem("av_done")
        ov_full, o_hi_ready, o_ready = sem("ov_full"), sem("o_hi_ready"), sem("o_ready")
        merged_done, m_hi_ready, m_ready = sem("merged_done"), sem("m_hi_ready"), sem("m_ready")
        mix_full, x_mixed = sem("mix_full"), sem("x_mixed")
        route_max, route_exp, ghot_ready, routed = (sem("route_max"), sem("route_exp"),
                                                    sem("ghot_ready"), sem("routed"))
        sel_ready, gather_full, selT_ready, xgf_ready = (sem("sel_ready"), sem("gather_full"),
                                                         sem("selT_ready"), sem("xgf_ready"))
        xg_hi_ready, xg_ready = sem("xg_hi_ready"), sem("xg_ready")
        gu_full, th_ready, hid_ready, ht_full = sem("gu_full"), sem("th_ready"), sem("hid_ready"), sem("ht_full")
        hidT_hi_ready, hidT_ready = sem("hidT_hi_ready"), sem("hidT_ready")
        y_full, y_hi_ready, y_ready, scatter_full, x_moe = (sem("y_full"), sem("y_hi_ready"), sem("y_ready"),
                                                            sem("scatter_full"), sem("x_moe"))
        out_ready, waits_carried = sem("out_ready"), sem("waits_carried")

        block = ctx.enter_context(nc.Block())

        def slot_width(n):
            return FILL.get(MIX[n], UNIT) if n < MIX_UNITS else UNIT

        def pj_emptied(name):
            i = PJ_INDEX[name]
            who = PJ[i][1]
            return who, sum(w == who for _, w in PJ[:i + 1])

        def spans(h, b, kind):
            if kind == "mla":
                return [(0, 0, 128, None), (1, 128, 256, None)]
            w = 128 * (b + 1)
            return [(b, g * w, w, g) for g in range(3)]

        @block.sync
        def _(sp):
            def load(n, slot, src, width):
                sp.wait_ge(split_lo, n + 1)
                sp.dma_start(raw[:, slot, 0:width], src).then_inc(weights_landed[slot], 16)

            sp.sem_inc(split_lo, RAW_SLOTS)
            with sp.Fori(0, DEPTH) as layer:
                alone(sp, routed, layer + 1)
                before = sp.value_load(rounds[0:1, 0:1], min_val=0, max_val=2 * DEPTH)
                first = sp.snap(layer * MIX_UNITS + before * MOE_UNITS)
                for u in range(MIX_UNITS):
                    load(first + u, u % RAW_SLOTS, mix_weights[layer, u, :, 0:slot_width(u)], slot_width(u))
                first = sp.snap((layer + 1) * MIX_UNITS + before * MOE_UNITS)
                for u in range(GROUP_UNITS):
                    load(first + u, u % RAW_SLOTS, moe_weights[layer, 0, u], UNIT)
                with sp.Fori(1, GROUPS) as g:
                    base = sp.snap(first + g * GROUP_UNITS)
                    for u in range(GROUP_UNITS):
                        load(base + u, u % RAW_SLOTS, moe_weights[layer, g, u], UNIT)
                alone(sp, routed, layer + 2)
                end = sp.value_load(rounds[0:1, 0:1], min_val=0, max_val=2 * DEPTH)
                with sp.If(end - before - 1):
                    with sp.Fori(0, GROUPS) as g:
                        base = sp.snap(first + MOE_UNITS + g * GROUP_UNITS)
                        for u in range(GROUP_UNITS):
                            load(base + u, u % RAW_SLOTS, moe_weights[layer, g, u], UNIT)
            end = sp.value_load(rounds[0:1, 0:1], min_val=0, max_val=2 * DEPTH)
            last = sp.snap(DEPTH * MIX_UNITS + end * MOE_UNITS)
            for u in range(SPLIT_SLOTS):
                load(last + u, u, mix_weights[0, u, :, 0:16], 16)
            sp.wait_ge(out_ready, 1)
            sp.dma_start(out.rearrange("(t p) d -> p t d", p=P), hn[:, :, :]).then_inc(out_stored, 16)
            sp.wait_ge(out_stored, 16)
            for s in range(RAW_SLOTS):
                sp.wait_ge(weights_landed[s], 16)

        @block.scalar
        def _(act):
            def split(u, width=UNIT):
                slot, out_slot = u % RAW_SLOTS, u % SPLIT_SLOTS
                act.wait_ge(weights_landed[slot], 16 * (landed + u // RAW_SLOTS + 1))
                act.activation(w_hi[:, out_slot, 0:width], raw[:, slot, 0:width], ACT.Copy).then_inc(split_hi, 1)

            act.dma_start(xt[:, :, :], x.rearrange("(t p) d -> p t d", p=P)).then_inc(x_landed, 16)
            act.dma_start(cst[:, :], constants).then_inc(const_landed, 16)
            act.dma_start(pos_i[:, :], positions.broadcast_to([P, SEQ])).then_inc(pos_landed, 16)
            act.dma_start(all_params[:, :, :], params.rearrange("l p n -> p l n")).then_inc(params_landed, 16)
            act.dma_start(gfin[:, :], g_final.broadcast_to([P, D_MODEL])).then_inc(gfin_landed, 16)
            for i, name in enumerate(("sin64", "cos64", "sin96", "cos96")):
                act.wait_ge(angle_ready, i + 1)
                act.activation(rope[name][:, :], turns[:, :], ACT.Sin).then_inc(sin_done, 1)
            landed = 0
            for u in range(SPLIT_SLOTS):
                split(u)

            def squares():
                for t in range(TILES):
                    act.activation(hn[:, t, :], xt[:, t, :], ACT.Square,
                                   accum_out=stat[:, t:t + 1]).then_inc(squares_ready, 1)

            act.wait_ge(x_landed, 16)
            act.sem_inc(x_moe, 1)
            with act.Fori(0, DEPTH) as layer:
                alone(act, routed, layer + 1)
                before = act.value_load(rounds[0:1, 0:1], min_val=0, max_val=2 * DEPTH)
                landed = act.snap(layer * (MIX_UNITS // RAW_SLOTS) + before * (MOE_UNITS // RAW_SLOTS))

                def full(name):
                    act.wait_ge(pj_full, layer * len(PJ) + PJ_INDEX[name] + 1)

                def after(u):
                    if u < MIX_UNITS - 4:
                        full(LAST_FILL[u])
                    elif u < MIX_UNITS - 1:
                        act.wait_ge(out_used, layer * 3 + u - (MIX_UNITS - 4) + 1)
                    else:
                        act.wait_ge(mix_full, layer + 1)
                    split(u + SPLIT_SLOTS, slot_width(u + SPLIT_SLOTS))

                def copy(name, dst, src=None):
                    full(name)
                    act.activation(dst, pj(name) if src is None else src, ACT.Copy).then_inc(pj_act, 1)

                act.wait_ge(x_moe, before * GROUPS + 1)
                squares()
                for c in range(4):
                    act.wait_ge(pj_dve, layer * PJ_TOTAL["dve"] + c + 1)
                    act.activation(hT_hi[:, 2 * c:2 * c + 2, :], hTf[:, 2 * c:2 * c + 2, :],
                                   ACT.Copy).then_inc(hT_hi_ready, 1)
                after(0)
                copy("sbq", sbq[:, :, :])
                after(1)
                copy("sbk", sbk[:, :, :])
                after(2)
                copy("sbv", sbv[:, :, :])
                act.wait_ge(z_full, layer + 1)
                act.activation(sb_a[:, 0:1024], SC[:, :], ACT.Abs, scale=HEAD ** -0.5)
                act.activation(two(sb_a[:, 1024:1536]), TR2, ACT.Abs, scale=HEAD ** -0.5).then_inc(act_chain, 1)
                act.wait_ge(act_chain, layer * ACT_LAYER_STEPS + 1)
                act.activation(sb_a[:, :], sb_a[:, :], ACT.Exp, scale=-1.0).then_inc(act_chain, 1)
                act.wait_ge(act_chain, layer * ACT_LAYER_STEPS + 2)
                act.activation(sb_a[:, :], sb_a[:, :], ACT.Ln, bias=1.0).then_inc(softplus_ready, 1)
                after(3)
                full("cq")
                act.activation(lat_sq[:, 0:2, :], pj("cq"), ACT.Square)
                copy("cq", lat[:, 0:2, :])
                after(4)
                full("ckv")
                act.activation(lat_sq[:, 2, :], pj("ckv")[:, 0:SEQ], ACT.Square).then_inc(lat_sq_ready, 1)
                copy("ckv", lat[:, 2, :], pj("ckv")[:, 0:SEQ])
                after(5)
                copy("kr", kr[0:MLA_QK, :], pj("kr")[0:MLA_QK, 0:SEQ])
                after(6)
                copy("d0q", dq[0][:, :, :])
                act.wait_ge(lat_normed, layer + 1)
                act.activation(lat_hi[:, :, :], lat[:, :, :], ACT.Copy).then_inc(lat_hi_ready, 1)
                after(7)
                copy("d0k", dk[0][:, :, :])
                act.wait_ge(logw_ready, layer + 1)
                act.activation(sb_b[:, :], sb_b[:, :], ACT.Exp).then_inc(wexp_ready, 1)
                after(8)
                copy("d0v", dv[0][:, :, :])
                after(9)
                for i in range(2):
                    copy(f"uq{i}", mq[0:MLA_QK, 2 * i:2 * i + 2, :], pj(f"uq{i}")[0:MLA_QK, :])
                act.wait_ge(ov_full, layer * BRANCHES + 1)
                act.activation(o_hi[0][:, :, :], OV, ACT.Copy).then_inc(o_hi_ready, 1)
                after(10)
                for i in range(2):
                    copy(f"ukv{i}", mk[0:NOPE, 2 * i:2 * i + 2, :], pj(f"ukv{i}")[0:NOPE, :])
                copy("ukvv", mv[:, :, :])
                for u, name, dst in ((11, "d1q", dq[1]), (12, "d1k", dk[1]), (13, "d1v", dv[1]),
                                     (14, "d2q", dq[2]), (15, "d2k", dk[2]), (16, "d2v", dv[2])):
                    after(u)
                    copy(name, dst[:, :, :])

                def exps(j):
                    kind, h, b = JOBS[j]
                    act.wait_ge(max_ready, layer * len(JOBS) + j + 1)
                    rows = ((0, 128), (128, 384)) if kind == "mla" else ((0, 384 * (b + 1)),)
                    for i, (lo, hi) in enumerate(rows):
                        ins = act.activation(probs[:, j % 2, lo:hi], probs[:, j % 2, lo:hi], ACT.Exp,
                                             bias=stat[:, 8 + 4 * (j % 2) + i:9 + 4 * (j % 2) + i],
                                             accum_out=stat[:, 16 + 4 * (j % 2) + i:17 + 4 * (j % 2) + i])
                    ins.then_inc(exp_ready, 1)

                def out_of_transposes(j):
                    kind, h, b = JOBS[j]
                    n = 6 if b == 1 else 3
                    act.wait_ge(tr_full, layer * len(JOBS) + j + 1)
                    if j == HEADS:
                        act.wait_ge(ov_full, layer * BRANCHES + 2)
                    elif j >= 1:
                        act.wait_ge(av_done, layer * (len(JOBS) - 2) + j - (j > HEADS))
                    act.activation(pT[:, 0:n, :], TR[:, 0:128 * n], ACT.Copy).then_inc(pT_ready, 1)

                for i in range(12):
                    if i == 6:
                        act.wait_ge(ov_full, layer * BRANCHES + 2)
                        act.activation(o_hi[1][:, :, :], OV, ACT.Copy).then_inc(o_hi_ready, 1)
                    if i >= 1:
                        exps(i - 1)
                    after(17 + i)
                    full(f"gate{i}")
                    act.activation(gates[:, i // 4, 2 * (i % 4):2 * (i % 4) + 2, :], pj(f"gate{i}"), ACT.Tanh,
                                   scale=0.5).then_inc(pj_act, 1)
                    if i >= 1:
                        out_of_transposes(i - 1)
                exps(11)
                after(29)
                out_of_transposes(11)
                after(30)
                act.wait_ge(ov_full, layer * BRANCHES + 3)
                act.activation(o_hi[2][:, :, :], OV, ACT.Copy).then_inc(o_hi_ready, 1)
                after(31)
                for j in range(4):
                    act.wait_ge(merged_done, layer * 4 + j + 1)
                    act.activation(m_hi[:, 2 * j:2 * j + 2, :], merged[:, 2 * j:2 * j + 2, :], ACT.Copy,
                                   scale=0.5).then_inc(m_hi_ready, 1)
                for u in range(32, 36):
                    after(u)

                act.wait_ge(x_mixed, layer + 1)
                squares()
                act.wait_ge(route_max, layer + 1)
                ins = act.activation(g1[:, :, :], g1[:, :, :], ACT.Exp)
                act.activation(stat[:, 36:38], stat[:, 36:38], ACT.Exp).then_inc(route_exp, 1)
                alone(act, routed, layer + 2)
                end = act.value_load(rounds[0:1, 0:1], min_val=0, max_val=2 * DEPTH)
                with act.Fori(before, end) as r:
                    with act.Fori(0, GROUPS) as g:
                        q = act.snap(r * GROUPS + g)
                        landed = act.snap((layer + 1) * (MIX_UNITS // RAW_SLOTS) + q * (GROUP_UNITS // RAW_SLOTS))
                        act.wait_ge(gather_full, q + 1)
                        act.activation(selT[:, :, :], SC[:, 0:256], ACT.Copy).then_inc(selT_ready, 1)
                        act.wait_ge(xgf_ready, q + 1)
                        act.activation(xg_hi[:, :, :], xgf[:, :, :], ACT.Copy).then_inc(xg_hi_ready, 1)

                        def tanh(e):
                            act.wait_ge(gu_full, q * PER_GROUP + e + 1)
                            act.activation(th[:, e % 2, :], GU[e % 2][:, 0:WIDTH], ACT.Tanh,
                                           scale=0.5).then_inc(th_ready, 1)

                        def hidT(e):
                            act.wait_ge(ht_full, q * PER_GROUP + e + 1)
                            act.activation(hidT_hi[:, e % 2, :, :], HT[e % 2], ACT.Copy).then_inc(hidT_hi_ready, 1)

                        for u, name in enumerate(MOE):
                            if name[0] == "B":
                                tanh(int(name[1]))
                            if name[0] == "D":
                                hidT(int(name[1]))
                            e = int(name[1])
                            if name[0] == "A":
                                act.wait_ge(a_used, q * PER_GROUP + e + 1)
                            elif name[0] == "B":
                                act.wait_ge(gu_full, q * PER_GROUP + e + 1)
                            elif e < 3:
                                act.wait_ge(d_used, q * 3 + e + 1)
                            else:
                                act.wait_ge(y_full, q + 1)
                            split(u + SPLIT_SLOTS)
                        act.wait_ge(y_full, q + 1)
                        act.activation(y_hi[:, :], SC[:, :], ACT.Copy).then_inc(y_hi_ready, 1)
            act.wait_ge(x_moe, end * GROUPS + 1)
            squares()

        @block.gpsimd
        def _(pool):
            def rsqrt(out_, in_, exponent):
                return pool.tensor_tensor(out_, in_, exponent, ALU.pow)

            def norm_rstd(n):
                alone(pool, squares_ready, TILES * (n + 1))
                pool.tensor_scalar(stat[:, 2:4], stat[:, 0:2], 1.0 / D_MODEL, EPS, ALU.mult,
                                   ALU.add).then_inc(pool_chain, 1)
                pool.wait_ge(pool_chain, n + 1)
                rsqrt(stat[:, 4:6], stat[:, 2:4], const("minus_half")).then_inc(rstd_ready, 1)

            pool.wait_ge(const_landed, 16)
            with pool.Fori(0, DEPTH) as layer:
                norm_rstd(layer * 2)
                pool.wait_ge(lat_var, layer + 1)
                half = const("minus_half")[:, 0:1].broadcast_to([P, SEQ])
                rsqrt(lat_rs[:, 0, :], lat_rs[:, 0, :], half)
                rsqrt(lat_rs[:, 1, :], lat_rs[:, 1, :], half).then_inc(lat_rstd, 1)
                norm_rstd(layer * 2 + 1)
            norm_rstd(2 * DEPTH)

        @block.vector
        def _(dve):
            steps = {"layer": 0, "group": 0, "pass": 0}

            def link(ins, base):
                steps["layer"] += 1
                ins.then_inc(dve_chain, 1)
                dve.wait_ge(dve_chain, base + steps["layer"])

            def glink(ins):
                steps["group"] += 1
                ins.then_inc(dve_gchain, 1)
                dve.wait_ge(dve_gchain, q * DVE_GROUP_STEPS + steps["group"])

            setup = [0]

            def slink(ins):
                setup[0] += 1
                ins.then_inc(setup_chain, 1)
                dve.wait_ge(setup_chain, setup[0])

            def split(n, u, width=UNIT):
                dve.wait_ge(split_hi, n + 1)
                slot = u % SPLIT_SLOTS
                dve.tensor_tensor(w_lo[:, slot, 0:width], raw[:, u % RAW_SLOTS, 0:width],
                                  w_hi[:, slot, 0:width].bitcast(F32), ALU.subtract).then_inc(split_lo, 1)

            slink(dve.memset(rounds_f[:, :], 0.0))
            dve.tensor_copy(rounds[:, :], rounds_f[:, :]).then_inc(routed, 1)
            dve.wait_ge(pos_landed, 16)
            dve.wait_ge(const_landed, 16)
            slink(dve.tensor_copy(pos_f[:, :], pos_i[:, :]))
            two_pi = 2 * np.pi
            parts = [6.25, 0.033203125]
            parts.append(float(np.float32(two_pi - sum(parts))))
            for i, (name, freq, lead) in enumerate((("sin64", "freq64", 0.0), ("cos64", "freq64", 0.25),
                                                    ("sin96", "freq96", 0.0), ("cos96", "freq96", 0.25))):
                slink(dve.tensor_scalar(angle[:, :], pos_f[:, :], const(freq), None, ALU.mult))
                if i >= 1:
                    dve.wait_ge(sin_done, i)
                slink(dve.tensor_scalar(turns[:, :], angle[:, :], 1.0 / two_pi, lead, ALU.mult, ALU.add))
                slink(dve.tensor_scalar(turns[:, :], turns[:, :], 12582912.0, None, ALU.add))
                slink(dve.tensor_scalar(turns[:, :], turns[:, :], 12582912.0, None, ALU.subtract))
                for part in parts:
                    slink(dve.scalar_tensor_tensor(out=angle[:, :], in0=turns[:, :], scalar=-part,
                                                   in1=angle[:, :], op0=ALU.mult, op1=ALU.add))
                slink(dve.tensor_scalar(turns[:, :], angle[:, :], lead * two_pi, None, ALU.add))
                dve.tensor_scalar(turns[:, :], turns[:, :], 3.1415925, -3.1415925, ALU.min,
                                  ALU.max).then_inc(angle_ready, 1)
            for u in range(SPLIT_SLOTS):
                split(u, u)
            dve.wait_ge(params_landed, 16)
            dve.wait_ge(sin_done, 4)

            def normed(n):
                dve.wait_ge(rstd_ready, n + 1)
                for t in range(TILES):
                    ins = dve.tensor_scalar(hn[:, t, :], xt[:, t, :], stat[:, 4 + t:5 + t], None, ALU.mult)
                return ins

            with dve.Fori(0, DEPTH) as layer:
                steps["layer"] = 0
                alone(dve, routed, layer + 1)
                before = dve.value_load(rounds[0:1, 0:1], min_val=0, max_val=2 * DEPTH)
                first = dve.snap(layer * MIX_UNITS + before * MOE_UNITS)
                base = dve.snap(layer * DVE_LAYER_STEPS)

                def chain(ins):
                    link(ins, base)

                def full(name):
                    dve.wait_ge(pj_full, layer * len(PJ) + PJ_INDEX[name] + 1)

                def after(u):
                    split(first + u + SPLIT_SLOTS, u + SPLIT_SLOTS, slot_width(u + SPLIT_SLOTS))

                def scaled_transposes(prefix, gain, c):
                    full(f"{prefix}{c}")
                    g = param(gain)[:, 2 * c:2 * c + 2].unsqueeze(2).broadcast_to([P, 2, SEQ])
                    dve.tensor_tensor(hTf[:, 2 * c:2 * c + 2, :],
                                      pj(f"{prefix}{c}").rearrange("p (c t) -> p c t", c=2), g,
                                      ALU.mult).then_inc(pj_dve, 1)

                def rotate(name, dst, rows, width, cos, sin):
                    full(name)
                    if name != ROTATIONS[0]:
                        dve.wait_ge(roped, layer * len(ROTATIONS) + ROTATIONS.index(name))
                    swapped = pj(name)[rows, 0:width].rearrange("p (h t) -> p h t", t=SEQ)
                    h = width // SEQ
                    table = lambda k: rope[k][rows, :].unsqueeze(1).broadcast_to([dst.shape[0], h, SEQ])
                    dve.tensor_tensor(rope_tmp[rows, 0:h, :], swapped, table(sin), ALU.mult).then_inc(pj_dve, 1)
                    chain(dve.tensor_tensor(dst, dst, table(cos), ALU.mult))
                    return dve.tensor_tensor(dst, dst, rope_tmp[rows, 0:h, :], ALU.add)

                chain(dve.tensor_copy(par[:, :], all_params[:, layer, :]))
                normed(layer * 2).then_inc(hn_ready, 1)

                def low_hT(c):
                    dve.wait_ge(hT_hi_ready, layer * 4 + c + 1)
                    dve.tensor_tensor(hT_lo[:, 2 * c:2 * c + 2, :], hTf[:, 2 * c:2 * c + 2, :],
                                      hT_hi[:, 2 * c:2 * c + 2, :].bitcast(F32), ALU.subtract).then_inc(hT_ready, 1)

                for c in range(4):
                    scaled_transposes("norm", "g_mix", c)
                    if c >= 1:
                        low_hT(c - 1)
                low_hT(3)
                for u in range(4):
                    after(u)
                scale = HEAD ** -0.5
                blocks = ((ps[:, 4:6, :], 0, 1024, 256), (TR2, 1024, 1536, 128))
                dve.wait_ge(z_full, layer + 1)
                for z, lo, hi, _ in blocks:
                    ins = dve.tensor_scalar(two(sb_b[:, lo:hi]), z, scale, 0.0, ALU.mult, ALU.min)
                chain(ins)
                dve.wait_ge(softplus_ready, layer + 1)
                chain(dve.tensor_tensor(sb_b[:, :], sb_b[:, :], sb_a[:, :], ALU.subtract))
                for z, lo, hi, _ in blocks:
                    ins = dve.scalar_tensor_tensor(out=two(sb_c[:, lo:hi]), in0=z, scalar=-scale, in1=two(sb_b[:, lo:hi]),
                                                   op0=ALU.mult, op1=ALU.add)
                chain(ins)

                def strict(buf, lo, hi, w):
                    view = buf[:, lo:hi].rearrange("p (h t) -> p h t", t=w)
                    mask = const("sb_mask")[:, 0:w].unsqueeze(1).broadcast_to([P, HEADS, w])
                    return dve.tensor_tensor(view, view, mask, ALU.mult)

                for z, lo, hi, w in blocks:
                    ins = strict(sb_c, lo, hi, w)
                ins.then_inc(strict_ready, 1)
                after(4)
                after(5)
                dve.wait_ge(lat_full, layer + 1)
                dve.tensor_scalar(lat_rs[:, 0, :], OV[:, 0:SEQ], 1.0 / WIDTH, EPS, ALU.mult, ALU.add)
                dve.tensor_scalar(lat_rs[:, 1, :], OV[:, SEQ:2 * SEQ], 1.0 / P, EPS, ALU.mult,
                                  ALU.add).then_inc(lat_var, 1)
                after(6)
                rows = slice(0, MLA_QK)
                chain(rotate("sw_kr", kr[rows, :].unsqueeze(1), rows, SEQ, "cos96", "sin96"))
                dve.tensor_copy(mk[NOPE:MLA_QK, :, :],
                                kr[NOPE:MLA_QK, :].unsqueeze(1).broadcast_to([ROPE, HEADS, SEQ])).then_inc(roped, 1)
                dve.wait_ge(lat_rstd, layer + 1)
                for c in range(3):
                    gain = param("g_q")[:, c:c + 1] if c < 2 else param("g_kv")
                    ins = dve.scalar_tensor_tensor(out=lat[:, c, :], in0=lat[:, c, :], scalar=gain,
                                                   in1=lat_rs[:, c // 2, :], op0=ALU.mult, op1=ALU.mult)
                ins.then_inc(lat_normed, 1)
                dve.wait_ge(lat_hi_ready, layer + 1)
                dve.tensor_tensor(lat_lo[:, :, :], lat[:, :, :], lat_hi[:, :, :].bitcast(F32),
                                  ALU.subtract).then_inc(lat_ready, 1)
                after(7)
                dve.wait_ge(after_full, layer + 1)
                for z, lo, hi, _ in blocks:
                    ins = dve.tensor_tensor(two(sb_b[:, lo:hi]), z, two(sb_b[:, lo:hi]), ALU.add)
                ins.then_inc(logw_ready, 1)
                after(8)
                rows = slice(0, P)
                rotate("sw_d0q", dq[0][:, :, :], rows, 512, "cos64", "sin64").then_inc(roped, 1)
                dve.wait_ge(wexp_ready, layer + 1)
                for z, lo, hi, w in blocks:
                    ins = strict(sb_b, lo, hi, w)
                ins.then_inc(w_ready, 1)
                rotate("sw_d0k", dk[0][:, :, :], rows, 512, "cos64", "sin64").then_inc(roped, 1)
                after(9)

                def low_o(n):
                    dve.wait_ge(o_hi_ready, layer * BRANCHES + n + 1)
                    dve.tensor_tensor(o_lo[n][:, :, :], OV.rearrange("p (c t) -> p c t", c=2),
                                      o_hi[n][:, :, :].bitcast(F32), ALU.subtract).then_inc(o_ready, 1)

                low_o(0)
                after(10)
                rows = slice(0, MLA_QK)
                for i in range(2):
                    rotate(f"sw_mq{i}", mq[rows, 2 * i:2 * i + 2, :], rows, 512, "cos96", "sin96").then_inc(roped, 1)
                rows = slice(0, P)
                after(11)
                after(12)
                after(13)
                rotate("sw_d1q", dq[1][:, :, :], rows, 512, "cos64", "sin64").then_inc(roped, 1)
                after(14)
                rotate("sw_d1k", dk[1][:, :, :], rows, 512, "cos64", "sin64").then_inc(roped, 1)
                after(15)
                after(16)
                rotate("sw_d2q", dq[2][:, :, :], rows, 512, "cos64", "sin64").then_inc(roped, 1)

                def masked(j):
                    kind, h, b = JOBS[j]
                    dve.wait_ge(sc_full, layer * len(JOBS) + j + 1)
                    w = 768 if b == 1 else 384
                    mask = const("mla_mask" if kind == "mla" else f"dil_mask{b}")
                    chain(dve.scalar_tensor_tensor(out=probs[:, j % 2, 0:w], in0=SC[:, 0:w], scalar=
                                                   (MLA_QK if kind == "mla" else HEAD) ** -0.5, in1=mask,
                                                   op0=ALU.mult, op1=ALU.add))
                    rows = ((0, 128), (128, 384)) if kind == "mla" else ((0, w),)
                    for i, (lo, hi) in enumerate(rows):
                        ins = dve.tensor_reduce(stat[:, 8 + 4 * (j % 2) + i:9 + 4 * (j % 2) + i],
                                                probs[:, j % 2, lo:hi], AX.X, ALU.max, negate=True)
                    ins.then_inc(max_ready, 1)

                def normalised(j):
                    kind, h, b = JOBS[j]
                    dve.wait_ge(exp_ready, layer * len(JOBS) + j + 1)
                    w = 768 if b == 1 else 384
                    rows = ((0, 128), (128, 384)) if kind == "mla" else ((0, w),)
                    s, r = 16 + 4 * (j % 2), 24 + 4 * (j % 2)
                    chain(dve.reciprocal(stat[:, r:r + len(rows)], stat[:, s:s + len(rows)]))
                    for i, (lo, hi) in enumerate(rows):
                        ins = dve.tensor_scalar(probs[:, j % 2, lo:hi], probs[:, j % 2, lo:hi],
                                                stat[:, r + i:r + i + 1], None, ALU.mult)
                    ins.then_inc(probs_ready, 1)

                for i in range(12):
                    if i == 6:
                        low_o(1)
                    if i >= 1:
                        normalised(i - 1)
                    after(17 + i)
                    if i == 0:
                        rotate("sw_d2k", dk[2][:, :, :], rows, 512, "cos64", "sin64").then_inc(roped, 1)
                    masked(i)
                normalised(11)

                def merge(n, j):
                    full(f"branch{n}_{j}")
                    dst = (merged if n == 0 else gates[:, n])[:, 2 * j:2 * j + 2, :]
                    ins = dve.scalar_tensor_tensor(out=dst, in0=gates[:, n, 2 * j:2 * j + 2, :], scalar=1.0,
                                                   in1=pj(f"branch{n}_{j}").rearrange("p (c t) -> p c t", c=2),
                                                   op0=ALU.add, op1=ALU.mult)
                    ins.then_inc(pj_dve, 1)
                    if n > 0:
                        who, count = pj_emptied(f"branch{n}_{j}")
                        dve.wait_ge(pj_dve, layer * PJ_TOTAL["dve"] + count)
                        m = merged[:, 2 * j:2 * j + 2, :]
                        ins = dve.tensor_tensor(m, m, dst, ALU.add)
                        if n == 1:
                            chain(ins)
                        else:
                            ins.then_inc(merged_done, 1)

                for n in range(BRANCHES):
                    if n == 2:
                        low_o(2)
                    for j in range(4):
                        merge(n, j)
                    after(29 + n)
                for j in range(4):
                    dve.wait_ge(m_hi_ready, layer * 4 + j + 1)
                    dve.scalar_tensor_tensor(out=m_lo[:, 2 * j:2 * j + 2, :], in0=merged[:, 2 * j:2 * j + 2, :],
                                             scalar=0.5, in1=m_hi[:, 2 * j:2 * j + 2, :].bitcast(F32),
                                             op0=ALU.mult, op1=ALU.subtract).then_inc(m_ready, 1)
                for u in range(32, 36):
                    after(u)
                dve.wait_ge(mix_full, layer + 1)
                dve.tensor_tensor(xt[:, 0, :], xt[:, 0, :], SC, ALU.add)
                dve.tensor_tensor(xt[:, 1, :], xt[:, 1, :], TR, ALU.add).then_inc(x_mixed, 1)

                normed(layer * 2 + 1).then_inc(hn_ready, 1)
                for c in range(4):
                    scaled_transposes("moe_norm", "g_ffn", c)
                full("logits")
                logits = pj("logits")[:, 0:2 * 20].rearrange("p (t n) -> p t n", n=20)
                bias = param("bias").unsqueeze(1).broadcast_to([P, TILES, 20])
                chain(dve.tensor_tensor(gl[:, :, :], logits[:, :, 0:GROUPS], bias[:, :, 0:GROUPS], ALU.add))
                ins = dve.tensor_tensor(el[:, :, :], logits[:, :, GROUPS:20], bias[:, :, GROUPS:20], ALU.add)
                ins.then_inc(pj_dve, 1)

                def over(col, n):
                    return stat[:, col:col + 2].unsqueeze(2).broadcast_to([P, TILES, n])

                def first_largest(hot, values, top, tmp, n):
                    chain(dve.tensor_reduce(stat[:, top:top + 2], values, AX.X, ALU.max))
                    chain(dve.tensor_tensor(tmp, values, over(top, n), ALU.is_equal))
                    order = const(f"first{n}").unsqueeze(1).broadcast_to([P, TILES, n])
                    chain(dve.tensor_tensor(tmp, tmp, order, ALU.mult))
                    chain(dve.tensor_reduce(stat[:, 34:36], tmp, AX.X, ALU.max))
                    return dve.tensor_tensor(hot, tmp, over(34, n), ALU.is_equal)

                first_largest(ghot[:, :, :], gl[:, :, :], 32, g1[:, :, :], GROUPS).then_inc(ghot_ready, 1)
                dve.wait_ge(ghot_ready, layer + 1)
                chain(dve.tensor_tensor(g1[:, :, :], gl[:, :, :], over(32, GROUPS), ALU.subtract))
                el8 = el[:, :, :].rearrange("p t (g e) -> p (t g) e", e=PER_GROUP)
                gh8 = ghot[:, :, :].rearrange("p t g -> p (t g)")
                r8 = r1[:, :, :].rearrange("p t (g e) -> p (t g) e", e=PER_GROUP)
                wide = lambda a: a.unsqueeze(2).broadcast_to([P, TILES * GROUPS, PER_GROUP])
                chain(dve.tensor_tensor(r8, el8, wide(gh8), ALU.mult))
                chain(dve.tensor_scalar(slot_of[:, :], gh8, -NEG, NEG, ALU.mult, ALU.add))
                chain(dve.tensor_tensor(el8, r8, wide(slot_of[:, :]), ALU.add))
                chain(first_largest(hot1[:, :, :], el[:, :, :], 40, r1[:, :, :], EXPERTS))
                chain(dve.scalar_tensor_tensor(out=el[:, :, :], in0=hot1[:, :, :], scalar=2 * NEG, in1=el[:, :, :],
                                               op0=ALU.mult, op1=ALU.add))
                chain(first_largest(hot2[:, :, :], el[:, :, :], 42, r1[:, :, :], EXPERTS))
                dve.tensor_tensor(stat[:, 36:38], stat[:, 42:44], stat[:, 40:42], ALU.subtract).then_inc(route_max, 1)
                full("rank")
                rank = pj("rank")[:, 0:TILES * GROUPS]
                chain(dve.scalar_tensor_tensor(out=slot_of[:, :], in0=rank, scalar=1.0, in1=gh8,
                                               op0=ALU.add, op1=ALU.mult))
                chain(dve.tensor_scalar(slot_of[:, :], slot_of[:, :], -1.0, None, ALU.add))
                chain(dve.tensor_reduce(stat[:, 44:45], pj("rank")[:, 8:12], AX.X, ALU.max))
                ins = dve.tensor_scalar(stat[:, 45:46], stat[:, 44:45], float(P), 1.0, ALU.is_gt, ALU.add)
                ins.then_inc(pj_dve, 1)
                who, count = pj_emptied("rank")
                dve.wait_ge(pj_dve, layer * PJ_TOTAL["dve"] + count)
                chain(dve.tensor_tensor(rounds_f[:, :], rounds_f[:, :], stat[0:1, 45:46], ALU.add))
                dve.tensor_copy(rounds[:, :], rounds_f[:, :]).then_inc(routed, 1)
                dve.wait_ge(route_exp, layer + 1)
                chain(dve.tensor_reduce(stat[:, 46:48], g1[:, :, :], AX.X, ALU.add))
                chain(dve.tensor_scalar(stat[:, 48:50], stat[:, 36:38], 1.0, 2.0, ALU.add, ALU.mult))
                chain(dve.tensor_tensor(stat[:, 50:52], stat[:, 48:50], stat[:, 46:48], ALU.mult))
                chain(dve.reciprocal(stat[:, 52:54], stat[:, 50:52]))
                chain(dve.tensor_tensor(stat[:, 54:56], stat[:, 52:54], stat[:, 36:38], ALU.mult))
                chain(dve.tensor_tensor(hot1[:, :, :], hot1[:, :, :], over(52, EXPERTS), ALU.mult))
                chain(dve.tensor_tensor(hot2[:, :, :], hot2[:, :, :], over(54, EXPERTS), ALU.mult))
                chain(dve.tensor_tensor(comb[:, :, :], hot1[:, :, :], hot2[:, :, :], ALU.add))
                assert steps["layer"] == DVE_LAYER_STEPS, steps
                alone(dve, routed, layer + 2)
                end = dve.value_load(rounds[0:1, 0:1], min_val=0, max_val=2 * DEPTH)
                with dve.Fori(before, end) as r:
                    with dve.Fori(0, GROUPS) as g:
                        steps["group"] = 0
                        q = dve.snap(r * GROUPS + g)
                        first = dve.snap((layer + 1) * MIX_UNITS + q * GROUP_UNITS)
                        for t in range(TILES):
                            dve.tensor_scalar(sel[:, t, :], const("iota"), slot_of[:, bass.ds(g + t * GROUPS, 1)],
                                              None, ALU.is_equal)
                        dve.tensor_copy(gcomb[:, :, :], comb[:, :, bass.ds(g * PER_GROUP, PER_GROUP)]).then_inc(sel_ready, 1)
                        dve.wait_ge(gather_full, q + 1)
                        dve.tensor_copy(scomb[:, :], SC[:, 512:512 + PER_GROUP])
                        gain = param("g_ffn").unsqueeze(2).broadcast_to([P, CHUNKS, P])
                        dve.tensor_tensor(xgf[:, :, :], TR.rearrange("p (c s) -> p c s", s=P), gain,
                                          ALU.mult).then_inc(xgf_ready, 1)
                        dve.wait_ge(xg_hi_ready, q + 1)
                        dve.tensor_tensor(xg_lo[:, :, :], xgf[:, :, :], xg_hi[:, :, :].bitcast(F32),
                                          ALU.subtract).then_inc(xg_ready, 1)

                        def hidden(e):
                            dve.wait_ge(th_ready, q * PER_GROUP + e + 1)
                            glink(dve.scalar_tensor_tensor(out=hid[:, e % 2, :], in0=th[:, e % 2, :], scalar=1.0,
                                                           in1=GU[e % 2][:, 0:WIDTH], op0=ALU.add, op1=ALU.mult))
                            dve.scalar_tensor_tensor(out=hid[:, e % 2, :], in0=hid[:, e % 2, :],
                                                     scalar=scomb[:, e:e + 1], in1=GU[e % 2][:, WIDTH:2 * WIDTH],
                                                     op0=ALU.mult, op1=ALU.mult).then_inc(hid_ready, 1)

                        def low_hidT(e):
                            dve.wait_ge(hidT_hi_ready, q * PER_GROUP + e + 1)
                            dve.tensor_tensor(hidT_lo[:, e % 2, :, :], HT[e % 2].rearrange("p (c s) -> p c s", s=P),
                                              hidT_hi[:, e % 2, :, :].bitcast(F32), ALU.subtract).then_inc(hidT_ready, 1)

                        for u, name in enumerate(MOE):
                            if name[0] == "B":
                                hidden(int(name[1]))
                            if name[0] == "D":
                                low_hidT(int(name[1]))
                            split(first + u + SPLIT_SLOTS, u + SPLIT_SLOTS)
                        dve.wait_ge(y_hi_ready, q + 1)
                        dve.tensor_tensor(y_lo[:, :], SC, y_hi[:, :].bitcast(F32), ALU.subtract).then_inc(y_ready, 1)
                        dve.wait_ge(scatter_full, q + 1)
                        dve.tensor_tensor(xt[:, 0, :], xt[:, 0, :], TR, ALU.add)
                        dve.tensor_tensor(xt[:, 1, :], xt[:, 1, :], GU2, ALU.add).then_inc(x_moe, 1)
                        assert steps["group"] == DVE_GROUP_STEPS, steps
                    dve.tensor_scalar(slot_of[:, :], slot_of[:, :], -float(P), None, ALU.add).then_inc(dve_pchain, 1)
                    dve.wait_ge(dve_pchain, r + 1)

            dve.wait_ge(rstd_ready, 2 * DEPTH + 1)
            dve.wait_ge(gfin_landed, 16)
            for t in range(TILES):
                ins = dve.scalar_tensor_tensor(out=hn[:, t, :], in0=xt[:, t, :], scalar=stat[:, 4 + t:5 + t],
                                               in1=gfin[:, :], op0=ALU.mult, op1=ALU.mult)
            ins.then_inc(out_ready, 1)

        @block.tensor
        def _(pe):
            def product(out_, lhs, rhs, start, stop, **kw):
                pe.matmul(out_, lhs[1], rhs[0], start=start, stop=False, **kw)
                pe.matmul(out_, lhs[0], rhs[1], start=False, stop=False, **kw)
                return pe.matmul(out_, lhs[0], rhs[0], start=False, stop=stop, **kw)

            def weights(u, width, cols):
                slot = u % SPLIT_SLOTS
                return tuple(w[:, slot, 0:width].rearrange("p (k n) -> p k n", n=cols) for w in (w_hi, w_lo))

            def at(pair, *index):
                return tuple(w[(slice(None), *index)] for w in pair)

            def use(n):
                pe.wait_ge(split_lo, RAW_SLOTS + n + 1)

            pe.wait_ge(const_landed, 16)
            hT, o, m = (hT_hi, hT_lo), list(zip(o_hi, o_lo)), (m_hi, m_lo)
            with pe.Fori(0, DEPTH) as layer:
                alone(pe, routed, layer + 1)
                before = pe.value_load(rounds[0:1, 0:1], min_val=0, max_val=2 * DEPTH)
                first = pe.snap(layer * MIX_UNITS + before * MOE_UNITS)

                def bank(name):
                    i = PJ_INDEX[name]
                    if i >= PJ_BANKS:
                        who, count = pj_emptied(PJ[i - PJ_BANKS][0])
                        pe.wait_ge({"act": pj_act, "dve": pj_dve}[who], layer * PJ_TOTAL[who] + count)
                    return pj(name)

                def transposes(prefix):
                    for c2 in range(4):
                        b = bank(f"{prefix}{c2}")
                        for c in range(2):
                            for t in range(TILES):
                                ins = pe.transpose(b[:, c * SEQ + t * P:c * SEQ + (t + 1) * P],
                                                   hn[:, t, (2 * c2 + c) * P:(2 * c2 + c + 1) * P], const("ident"))
                        ins.then_inc(pj_full, 1)


                def project(u, fills, cols, act_in=hT, chunks=CHUNKS, wait=None):
                    w = weights(u, chunks * cols, cols)
                    use(first + u)
                    for name, parts in fills:
                        b = bank(name)
                        for col, n, to in parts:
                            for k in range(chunks):
                                if wait is not None and (col, k % 2) == (0, 0):
                                    wait(k)
                                ins = product(b[0:n, to:to + SEQ], at(w, k, slice(col, col + n)),
                                              at(act_in, k), k == 0, k == chunks - 1)
                        ins.then_inc(pj_full, 1)

                def features(name, wait=None):
                    project(MIX.index(name), [(name, [(0, P, 0), (P, P, SEQ)])], WIDTH, wait=wait)

                def tokens(name):
                    u = MIX.index(name)
                    w = weights(u, UNIT, WIDTH)
                    use(first + u)
                    b = bank(name)
                    for t in range(TILES):
                        for k in range(CHUNKS):
                            ins = product(b[:, t * WIDTH:(t + 1) * WIDTH], at(hT, k, slice(t * P, (t + 1) * P)),
                                          at(w, k), k == 0, k == CHUNKS - 1)
                    ins.then_inc(pj_full, 1)

                def act_has(name):
                    pe.wait_ge(pj_act, layer * PJ_TOTAL["act"] + pj_emptied(name)[1])

                def swap(name, src, rows, perm):
                    act_has(name)
                    b = bank(f"sw_{SWAPS[name]}")
                    pe.matmul(b[0:rows, 0:int(np.prod(src.shape[1:]))], const(perm, rows)[:, 0:rows], src,
                              start=True, stop=True).then_inc(pj_full, 1)

                SWAPS = {"kr": "kr", "d0q": "d0q", "d0k": "d0k", "uq0": "mq0", "uq1": "mq1",
                         "d1q": "d1q", "d1k": "d1k", "d2q": "d2q", "d2k": "d2k"}

                def place_of(h):
                    return 2 * (h % 2) + h // 2

                def half(h):
                    return slice(HEAD * (h % 2), HEAD * (h % 2) + HEAD)

                pe.wait_ge(hn_ready, layer * 2 + 1)
                transposes("norm")
                features("sbq", wait=lambda k: pe.wait_ge(hT_ready, layer * 4 + k // 2 + 1))
                features("sbk")
                tokens("sbv")
                features("cq")
                act_has("sbk")
                for h in range(HEADS):
                    pe.matmul(SC[:, place_of(h) * SEQ:(place_of(h) + 1) * SEQ], sbk[half(h), h // 2, 0:P],
                              sbq[half(h), h // 2, :], start=True, stop=True)
                for h in range(HEADS):
                    ins = pe.matmul(TR[:, 512 * (h % 2) + (h // 2) * P:512 * (h % 2) + (h // 2 + 1) * P],
                                    sbk[half(h), h // 2, P:SEQ], sbq[half(h), h // 2, P:SEQ], start=True, stop=True)
                ins.then_inc(z_full, 1)
                project(MIX.index("ckv"), [("ckv", [(0, P, 0)])], P)
                project(MIX.index("kr"), [("kr", [(0, MLA_QK, 0)])], MLA_QK)
                pe.wait_ge(lat_sq_ready, layer + 1)
                for c in range(3):
                    ins = pe.matmul(OV[:, (c // 2) * SEQ:(c // 2 + 1) * SEQ], const("ones"), lat_sq[:, c, :],
                                    start=c != 1, stop=c != 0)
                ins.then_inc(lat_full, 1)
                features("d0q")
                swap("kr", kr[0:MLA_QK, :], MLA_QK, "swap96")
                features("d0k")
                pe.wait_ge(strict_ready, layer + 1)
                near, far = sb_c[:, 0:1024], sb_c[:, 1024:1536]
                for i in range(2):
                    pe.matmul(SC[:, i * 512:(i + 1) * 512], const("later"), near[:, i * 512:(i + 1) * 512],
                              start=True, stop=False)
                    pe.matmul(SC[:, i * 512:(i + 1) * 512].rearrange("p (h t) -> p h t", t=SEQ)[:, :, P:SEQ],
                              const("ones"), far[:, i * 256:(i + 1) * 256].rearrange("p (h t) -> p h t", t=P),
                              start=False, stop=True)
                for i in range(2):
                    ins = pe.matmul(TR[:, 512 * i:512 * i + 256], const("later"), far[:, i * 256:(i + 1) * 256],
                                    start=True, stop=True)
                ins.then_inc(after_full, 1)
                tokens("d0v")
                swap("d0q", dq[0][:, :, :], P, "swap64")
                swap("d0k", dk[0][:, :, :], P, "swap64")
                pe.wait_ge(lat_ready, layer + 1)
                latq = (lat_hi[:, 0:2, :], lat_lo[:, 0:2, :])
                project(MIX.index("uq"), [(f"uq{i}", [((2 * i + h) * MLA_QK, MLA_QK, h * SEQ) for h in range(2)])
                                          for i in range(2)], HEADS * MLA_QK, act_in=latq, chunks=2)
                pe.wait_ge(w_ready, layer + 1)
                for h in range(HEADS):
                    to = OV[half(h), (h // 2) * SEQ:(h // 2 + 1) * SEQ]
                    cols = slice(h * HEAD, (h + 1) * HEAD)
                    i = place_of(h)
                    pe.matmul(to, sbv[:, 0, cols], sb_b[:, i * SEQ:(i + 1) * SEQ], start=True, stop=False)
                    ins = pe.matmul(to[:, P:SEQ], sbv[:, 1, cols], sb_b[:, 1024 + i * P:1024 + (i + 1) * P],
                                    start=False, stop=True)
                ins.then_inc(ov_full, 1)
                u = MIX.index("ukv")
                w = weights(u, 512, 512)
                use(first + u)
                latkv = (lat_hi, lat_lo)
                for i in range(2):
                    b = bank(f"ukv{i}")
                    for h in range(2):
                        col = (2 * i + h) * 2 * HEAD
                        ins = product(b[:, h * SEQ:(h + 1) * SEQ], at(w, 0, slice(col, col + P)),
                                      at(latkv, 2), True, True)
                    ins.then_inc(pj_full, 1)
                b = bank("ukvv")
                for t in range(TILES):
                    for h in range(HEADS):
                        col = h * 2 * HEAD + NOPE
                        ins = product(b[:, t * WIDTH + h * HEAD:t * WIDTH + (h + 1) * HEAD],
                                      at(latkv, 2, slice(t * P, (t + 1) * P)), at(w, 0, slice(col, col + HEAD)),
                                      True, True)
                ins.then_inc(pj_full, 1)
                for i in range(2):
                    swap(f"uq{i}", mq[0:MLA_QK, 2 * i:2 * i + 2, :], MLA_QK, "swap96")
                features("d1q")
                features("d1k")
                tokens("d1v")
                swap("d1q", dq[1][:, :, :], P, "swap64")
                features("d2q")
                swap("d1k", dk[1][:, :, :], P, "swap64")
                features("d2k")
                tokens("d2v")
                swap("d2q", dq[2][:, :, :], P, "swap64")

                def scores(j):
                    kind, h, b = JOBS[j]
                    if j >= 1:
                        pe.wait_ge(max_ready, layer * len(JOBS) + j)
                    if kind == "mla":
                        pe.wait_ge(roped, layer * len(ROTATIONS) + 5)
                        act_has("ukvv")
                    else:
                        pe.wait_ge(roped, layer * len(ROTATIONS) + 9)
                    for b_, lo, n, g in spans(h, b, kind):
                        qs = slice(b_ * P, (b_ + 1) * P)
                        if kind == "mla":
                            q_, k_ = mq[0:MLA_QK, h, qs], mk[0:MLA_QK, h, 0:n]
                        else:
                            q_, k_ = dq[g][half(h), h // 2, qs], dk[g][half(h), h // 2, 0:n]
                        ins = pe.matmul(SC[:, lo:lo + n], q_, k_, start=True, stop=True)
                    ins.then_inc(sc_full, 1)

                def transposed(j):
                    pe.wait_ge(probs_ready, layer * len(JOBS) + j + 1)
                    if j >= 1:
                        pe.wait_ge(pT_ready, layer * len(JOBS) + j)
                    for i in range(6 if JOBS[j][2] == 1 else 3):
                        ins = pe.transpose(TR[:, i * P:(i + 1) * P], probs[:, j % 2, i * P:(i + 1) * P], const("ident"))
                    ins.then_inc(tr_full, 1)

                def values(j):
                    kind, h, b = JOBS[j]
                    pe.wait_ge(pT_ready, layer * len(JOBS) + j + 1)
                    if j in (0, HEADS):
                        pe.wait_ge(o_ready, layer * BRANCHES + (1 if j == 0 else 2))
                    to = OV[half(h), (h // 2) * SEQ:(h // 2 + 1) * SEQ]
                    cols = slice(h * HEAD, (h + 1) * HEAD)
                    if kind == "mla":
                        pe.matmul(to, mv[:, 0, cols], pT[:, 0:2, :].rearrange("p a b -> p (a b)"), start=True, stop=False)
                        ins = pe.matmul(to[:, P:SEQ], mv[:, 1, cols], pT[:, 2, :], start=False, stop=True)
                    else:
                        n = 3 * (b + 1)
                        for i in range(n):
                            ins = pe.matmul(to[:, b * P:(b + 1) * P], dv[i // (b + 1)][:, i % (b + 1), cols],
                                            pT[:, i, :], start=i == 0, stop=i == n - 1)
                    if j in (HEADS - 1, len(JOBS) - 1):
                        ins.then_inc(ov_full, 1)
                    else:
                        ins.then_inc(av_done, 1)

                for i in range(12):
                    features(f"gate{i}")
                    if i == 0:
                        swap("d2k", dk[2][:, :, :], P, "swap64")
                    if i >= 1:
                        transposed(i - 1)
                    scores(i)
                    if i >= 2:
                        values(i - 2)

                def branch(n):
                    u = MIX.index(f"branch{n}")
                    pe.wait_ge(o_ready, layer * BRANCHES + n + 1)
                    project(u, [(f"branch{n}_{j}", [((2 * j + f) * P, P, f * SEQ) for f in range(2)])
                                for j in range(4)], D_MODEL, act_in=o[n], chunks=2)

                branch(0)
                transposed(11)
                values(10)
                branch(1)
                values(11)
                branch(2)
                for i in range(4):
                    u = MIX.index(f"out{i}")
                    w = weights(u, UNIT, D_MODEL)
                    use(first + u)
                    pe.wait_ge(m_ready, layer * 4 + i + 1)
                    for t, acc in enumerate((SC, TR)):
                        for n in range(2):
                            for k in range(2):
                                ins = product(acc[:, n * 512:(n + 1) * 512], at(m, 2 * i + k, slice(t * P, (t + 1) * P)),
                                              at(w, k, slice(n * 512, (n + 1) * 512)), (i, k) == (0, 0), (i, k) == (3, 1))
                    ins.then_inc(out_used if i < 3 else mix_full, 1)

                pe.wait_ge(hn_ready, layer * 2 + 2)
                transposes("moe_norm")
                pe.wait_ge(pj_dve, layer * PJ_TOTAL["dve"] + pj_emptied("moe_norm3")[1])
                b = bank("logits")
                router = param("router").rearrange("p (k n) -> p k n", n=20)
                for t in range(TILES):
                    for k in range(CHUNKS):
                        ins = pe.matmul(b[:, t * 20:(t + 1) * 20], hTf[:, k, t * P:(t + 1) * P], router[:, k, :],
                                        start=k == 0, stop=k == CHUNKS - 1)
                ins.then_inc(pj_full, 1)
                pe.wait_ge(ghot_ready, layer + 1)
                b = bank("rank")
                pe.matmul(b[:, 0:4], const("before"), ghot[:, 0, :], start=True, stop=True)
                pe.matmul(b[:, 4:8], const("ones"), ghot[:, 0, :], start=True, stop=False)
                pe.matmul(b[:, 4:8], const("before"), ghot[:, 1, :], start=False, stop=True)
                pe.matmul(b[:, 8:12], const("ones"), ghot[:, 0, :], start=True, stop=False)
                pe.matmul(b[:, 8:12], const("ones"), ghot[:, 1, :], start=False, stop=True).then_inc(pj_full, 1)
                alone(pe, routed, layer + 2)
                end = pe.value_load(rounds[0:1, 0:1], min_val=0, max_val=2 * DEPTH)
                with pe.Fori(before, end) as r:
                    with pe.Fori(0, GROUPS) as g:
                        q = pe.snap(r * GROUPS + g)
                        first = pe.snap((layer + 1) * MIX_UNITS + q * GROUP_UNITS)
                        pe.wait_ge(sel_ready, q + 1)
                        pe.wait_ge(x_moe, q + 1)
                        for t in range(TILES):
                            pe.transpose(SC[:, t * P:(t + 1) * P], sel[:, t, :], const("ident"))
                        for t in range(TILES):
                            pe.matmul(SC[:, 512:512 + PER_GROUP], sel[:, t, :], gcomb[:, t, :], start=t == 0, stop=t == 1)
                        for c in range(CHUNKS):
                            for t in range(TILES):
                                ins = pe.matmul(TR[:, c * P:(c + 1) * P], hn[:, t, c * P:(c + 1) * P], sel[:, t, :],
                                                start=t == 0, stop=t == 1)
                        ins.then_inc(gather_full, 1)
                        xg = (xg_hi, xg_lo)

                        def gate_up(e):
                            if e == 0:
                                pe.wait_ge(xg_ready, q + 1)
                            for i, part in enumerate("AB"):
                                u = MOE.index(f"{part}{e}")
                                w = weights(u, UNIT, 2 * WIDTH)
                                use(first + u)
                                for k in range(4):
                                    ins = product(GU[e % 2], at(xg, 4 * i + k), at(w, k),
                                                  (i, k) == (0, 0), (i, k) == (1, 3))
                                ins.then_inc(a_used if i == 0 else gu_full, 1)

                        def down(e):
                            pe.wait_ge(hid_ready, q * PER_GROUP + e + 1)
                            for f in range(2):
                                ins = pe.transpose(HT[e % 2][:, f * P:(f + 1) * P], hid[:, e % 2, f * P:(f + 1) * P],
                                                   const("ident"))
                            ins.then_inc(ht_full, 1)
                            pe.wait_ge(hidT_ready, q * PER_GROUP + e + 1)
                            if e == 0:
                                pe.wait_ge(selT_ready, q + 1)
                            u = MOE.index(f"D{e}")
                            w = weights(u, UNIT, D_MODEL)
                            use(first + u)
                            for f in range(2):
                                for n in range(2):
                                    ins = product(SC[:, n * 512:(n + 1) * 512], at((hidT_hi, hidT_lo), e % 2, f),
                                                  at(w, f, slice(n * 512, (n + 1) * 512)), (e, f) == (0, 0), (e, f) == (3, 1))
                            ins.then_inc(d_used if e < 3 else y_full, 1)

                        gate_up(0)
                        gate_up(1)
                        down(0)
                        gate_up(2)
                        down(1)
                        gate_up(3)
                        down(2)
                        down(3)
                        pe.wait_ge(y_ready, q + 1)
                        for t, acc in enumerate((TR, GU2)):
                            for n in range(2):
                                half_ = slice(n * 512, (n + 1) * 512)
                                pe.matmul(acc[:, half_], selT[:, t, :], y_lo[:, half_], start=True, stop=False)
                                ins = pe.matmul(acc[:, half_], selT[:, t, :], y_hi[:, half_], start=False, stop=True)
                        ins.then_inc(scatter_full, 1)


def shape_constants():
    c = {}
    i = np.arange(P)
    c["ident"] = np.eye(P)
    c["before"] = i[:, None] < i[None, :]
    c["later"] = i[:, None] > i[None, :]
    c["ones"] = np.ones((P, P))
    swap = np.zeros((P, P))
    for f in range(P):
        swap[(f + 32 if f % 64 < 32 else f - 32), f] = -1 if f % 64 < 32 else 1
    c["swap64"] = swap
    swap = np.zeros((P, P))
    for f in range(NOPE, MLA_QK):
        swap[(f + 16 if f < NOPE + 16 else f - 16), f] = -1 if f < NOPE + 16 else 1
    c["swap96"] = swap
    c["iota"] = np.broadcast_to(i, (P, P))
    query, key = np.arange(SEQ), np.arange(SEQ)
    c["sb_mask"] = key[:P, None] < query[None, :]
    causal = np.where(key[None, :] <= query[:, None], 0.0, NEG)
    c["mla_mask"] = np.concatenate([causal[:P, :P], causal[P:, :]], 1)
    span = query[:, None] - key[None, :]
    dil = [np.where((span >= 0) & (span <= w) & (span % d == 0), 0.0, NEG) for w, d in DIL]
    c["dil_mask0"] = np.concatenate([m[:P, :P] for m in dil], 1)
    c["dil_mask1"] = np.concatenate([m[P:, :] for m in dil], 1)
    f32 = np.float32
    for dim, rows, lo in ((HEAD, P, 0), (ROPE, MLA_QK, NOPE)):
        inv = f32(THETA) ** (-np.arange(0, dim, 2, dtype=f32) / f32(dim))
        col = np.zeros((P, 1), f32)
        for f in range(lo, rows):
            col[f, 0] = inv[(f - lo) % (dim // 2)]
        c["freq64" if dim == HEAD else "freq96"] = col
    c["first4"] = np.broadcast_to(np.arange(4, 0, -1), (P, 4))
    c["first16"] = np.broadcast_to(np.arange(16, 0, -1), (P, 16))
    c["minus_half"] = np.full((P, 2), -0.5)
    out = np.zeros((P, CONST_COLS), f32)
    for name, (lo, hi) in CONST.items():
        out[:, lo:hi] = c[name]
    return out


def rows_of_chunks(w):
    n = w.shape[-1]
    return w.reshape(-1, P, n).transpose(1, 0, 2).reshape(P, -1)


def unit_of(parts):
    out = np.zeros((P, UNIT), np.float32)
    out[:, :parts.shape[1]] = parts
    return out


def lay_out(inputs):
    mix = np.zeros((DEPTH, MIX_UNITS, P, UNIT), np.float32)
    moe = np.zeros((DEPTH, GROUPS, GROUP_UNITS, P, UNIT), np.float32)
    params = np.zeros((DEPTH, P, PARAM_COLS), np.float32)
    col = {}
    at = 0
    for name, n in (("sbq", 256), ("sbk", 256), ("sbv", 256), ("cq", 256), ("ckv", 128), ("kr", 32)):
        col[name] = (at, n)
        at += n
    for g in range(3):
        for c in "qkv":
            col[f"d{g}{c}"] = (at, 256)
            at += 256
    for i in range(12):
        col[f"gate{i}"] = (at, 256)
        at += 256
    for layer in range(DEPTH):
        w_in = inputs["w_in"][layer]
        for u, name in enumerate(MIX):
            if name == "kr":
                lo, n = col[name]
                padded = np.zeros((D_MODEL, MLA_QK), np.float32)
                padded[:, NOPE:] = w_in[:, lo:lo + n]
                part = rows_of_chunks(padded)
            elif name in col:
                lo, n = col[name]
                part = rows_of_chunks(w_in[:, lo:lo + n])
            elif name == "uq":
                part = rows_of_chunks(inputs["w_uq"][layer])
            elif name == "ukv":
                part = rows_of_chunks(inputs["w_ukv"][layer])
            elif name[:6] == "branch":
                part = rows_of_chunks(inputs["w_branch"][layer, int(name[6:])])
            else:
                i = int(name[3:])
                part = rows_of_chunks(inputs["w_out"][layer, 2 * i * P:(2 * i + 2) * P])
            mix[layer, u] = unit_of(part)
        for g in range(GROUPS):
            for u, name in enumerate(MOE):
                e = g * PER_GROUP + int(name[1])
                if name[0] == "D":
                    part = rows_of_chunks(inputs["w_down"][layer, e])
                else:
                    rows = slice(0, 512) if name[0] == "A" else slice(512, 1024)
                    part = rows_of_chunks(np.concatenate([inputs["w_gate"][layer, e, rows],
                                                          inputs["w_up"][layer, e, rows]], 1))
                moe[layer, g, u] = unit_of(part)
        by_name = {
            "g_mix": inputs["g_mix"][layer].reshape(CHUNKS, P).T, "g_ffn": inputs["g_ffn"][layer].reshape(CHUNKS, P).T,
            "g_q": inputs["g_q_lat"][layer].reshape(2, P).T, "g_kv": inputs["g_kv_lat"][layer].reshape(1, P).T,
            "router": rows_of_chunks(np.concatenate([inputs["w_group_router"][layer],
                                                     inputs["w_expert_router"][layer]], 1)),
            "bias": np.broadcast_to(np.concatenate([inputs["b_group_router"][layer],
                                                    inputs["b_expert_router"][layer]]), (P, 20)),
        }
        for name, (lo, hi) in PARAM.items():
            params[layer, :, lo:hi] = by_name[name]
    return mix, moe, params


def kernel(**inputs):
    import concourse.bacc as bacc
    from concourse import mybir
    from concourse.bass_utils import run_bass_kernel_spmd

    inputs = {name: np.ascontiguousarray(a) for name, a in inputs.items()}
    mix, moe, params = lay_out(inputs)
    arrays = {
        "x": inputs["x"][0], "positions": inputs["positions"], "mix_weights": mix, "moe_weights": moe,
        "params": params, "g_final": inputs["g_final"].reshape(1, D_MODEL), "constants": shape_constants(),
    }
    nc = bacc.Bacc("TRN2", target_bir_lowering=False, num_devices=1)
    args = [nc.dram_tensor(name, a.shape, mybir.dt.from_np(a.dtype), kind="ExternalInput").ap()
            for name, a in arrays.items()]
    out = nc.dram_tensor("out", (SEQ, D_MODEL), mybir.dt.float32, kind="ExternalOutput").ap()
    build(nc, *args, out)
    r = run_bass_kernel_spmd(nc, [arrays], core_ids=[0])
    return r.results[0]["out"].reshape(1, SEQ, D_MODEL)
```

```python
import numpy as np

D_MODEL = 1024
SEQ = 256
DEPTH = 2
HEAD = 64
THETA = 10000.0
EPS = 1e-6
NEG = -1e30
P = 128
TILES = SEQ // P
CHUNKS = D_MODEL // P
BRANCHES = 3
WIDTH = D_MODEL // 4
HEADS = WIDTH // HEAD
NOPE, ROPE = 64, 32
MLA_QK = NOPE + ROPE
GROUPS, PER_GROUP = 4, 4
EXPERTS = GROUPS * PER_GROUP
DIL = ((128, 1), (512, 4), (2048, 16))

UNIT = CHUNKS * WIDTH
RAW_SLOTS = 4
SPLIT_SLOTS = 3

MIX = ["sbq", "sbk", "sbv", "cq", "ckv", "kr", "d0q", "d0k", "d0v", "uq", "ukv",
       "d1q", "d1k", "d1v", "d2q", "d2k", "d2v"]
MIX += [f"gate{i}" for i in range(12)] + [f"branch{n}" for n in range(3)] + [f"out{i}" for i in range(4)]
FILL = {"ckv": CHUNKS * 128, "kr": CHUNKS * MLA_QK, "uq": 2 * HEADS * MLA_QK, "ukv": 512}
MIX_UNITS = len(MIX)
MOE = ["A0", "B0", "A1", "B1", "D0", "A2", "B2", "D1", "A3", "B3", "D2", "D3"]
MOE_SPLIT = [name for name in MOE if name[0] != "D"]
GROUP_UNITS = len(MOE_SPLIT)
MOE_UNITS = GROUPS * GROUP_UNITS
MOE_SLOTS = SPLIT_SLOTS + 1
DOWN_SLOTS = PER_GROUP
assert MIX_UNITS % RAW_SLOTS == MIX_UNITS % SPLIT_SLOTS == 0
assert GROUP_UNITS % RAW_SLOTS == GROUP_UNITS % MOE_SLOTS == 0

PJ = [(f"norm{c}", "dve") for c in range(4)]
PJ += [(n, "act") for n in ("sbq", "sbk", "sbv", "cq", "ckv", "kr", "d0q")]
PJ += [("sw_kr", "dve"), ("d0k", "act"), ("d0v", "act"), ("sw_d0q", "dve"), ("sw_d0k", "dve"),
       ("uq0", "act"), ("uq1", "act"), ("ukv0", "act"), ("ukv1", "act"), ("ukvv", "act"),
       ("sw_mq0", "dve"), ("sw_mq1", "dve"), ("d1q", "act"), ("d1k", "act"), ("d1v", "act"),
       ("sw_d1q", "dve"), ("d2q", "act"), ("sw_d1k", "dve"), ("d2k", "act"), ("d2v", "act"),
       ("sw_d2q", "dve"), ("gate0", "act"), ("sw_d2k", "dve")]
PJ += [(f"gate{i}", "act") for i in range(1, 12)]
PJ += [(f"branch{n}_{j}", "dve") for n in range(3) for j in range(4)]
PJ += [(f"moe_norm{c}", "dve") for c in range(4)] + [("logits", "dve"), ("rank", "dve")]
PJ_INDEX = {name: i for i, (name, _) in enumerate(PJ)}
PJ_BANKS = 3
PJ_TOTAL = {who: sum(w == who for _, w in PJ) for who in ("act", "dve")}

LAST_FILL = [{"uq": "uq1", "ukv": "ukvv"}.get(name, f"{name}_3" if name[:6] == "branch" else name)
             for name in MIX[:-4]]

ROTATIONS = ["sw_kr", "sw_d0q", "sw_d0k", "sw_mq0", "sw_mq1", "sw_d1q", "sw_d1k", "sw_d2q", "sw_d2k"]

JOBS = [("mla", h, None) for h in range(HEADS)] + [("dil", h, b) for h in range(HEADS) for b in range(2)]

CONST = {}
_at = 0
for _name, _n in (("ident", 128), ("before", 128), ("later", 128), ("ones", 128), ("swap64", 128),
                  ("swap96", 128), ("iota", 128), ("sb_mask", 256), ("mla_mask", 384),
                  ("dil_mask0", 384), ("dil_mask1", 768), ("freq64", 1), ("freq96", 1),
                  ("first4", 4), ("first16", 16), ("minus_half", 4)):
    CONST[_name] = (_at, _at + _n)
    _at += _n
CONST_COLS = _at
PARAM = {"g_mix": (0, 8), "g_ffn": (8, 16), "g_q": (16, 18), "g_kv": (18, 19), "router": (19, 179),
         "bias": (179, 199)}
PARAM_COLS = 199

DVE_LAYER_STEPS = 74
ACT_LAYER_STEPS = 2


def build(nc, x, positions, mix_weights, moe_weights, params, g_final, constants, out):
    import concourse.bass as bass
    from concourse import mybir
    from contextlib import ExitStack

    F32, F32R, I32 = mybir.dt.float32, mybir.dt.float32r, mybir.dt.int32
    ALU, ACT, AX = mybir.AluOpType, mybir.ActivationFunctionType, mybir.AxisListType

    cursor = [(nc.sbuf_base + 63) // 64 * 64]

    def place(name, shape, dtype=F32, at=None):
        size = 4 * int(np.prod(shape[1:]))
        if at is None:
            at = cursor[0]
            cursor[0] += (size + 31) // 32 * 32
        return nc.alloc_sbuf_tensor_at(name, shape, dtype, offset=at), at

    raw, _ = place("raw", [P, RAW_SLOTS, UNIT])
    w_hi, _ = place("w_hi", [P, SPLIT_SLOTS, UNIT], F32R)
    w_lo, _ = place("w_lo", [P, SPLIT_SLOTS, UNIT], F32R)
    xt, _ = place("xt", [P, TILES, D_MODEL])
    hn, hn_at = place("hn", [P, TILES, D_MODEL])
    o_hi, o_lo = [None] * 3, [None] * 3
    for n in (1, 2):
        o_hi[n], _ = place(f"o_hi{n}", [P, 2, SEQ], F32R, hn_at + (n - 1) * 4096)
        o_lo[n], _ = place(f"o_lo{n}", [P, 2, SEQ], F32R, hn_at + (n - 1) * 4096 + 2048)
    hTf, hTf_at = place("hTf", [P, CHUNKS, SEQ])
    lat, _ = place("lat", [P, 3, SEQ], F32, hTf_at)
    lat_sq, _ = place("lat_sq", [P, 3, SEQ], F32, hTf_at + 3072)
    lat_diag, _ = place("lat_diag", [P, 4, P], F32, hTf_at + 6144)
    xgf, _ = place("xgf", [P, CHUNKS, P], F32, hTf_at)
    merged, _ = place("merged", [P, CHUNKS, SEQ], F32, hTf_at)
    hT_hi, hh_at = place("hT_hi", [P, CHUNKS, SEQ], F32R)
    hT_lo, hl_at = place("hT_lo", [P, CHUNKS, SEQ], F32R)
    m_hi, _ = place("m_hi", [P, CHUNKS, SEQ], F32R, hh_at)
    m_lo, _ = place("m_lo", [P, CHUNKS, SEQ], F32R, hl_at)
    xg_hi, _ = place("xg_hi", [P, CHUNKS, P], F32R, hh_at)
    xg_lo, _ = place("xg_lo", [P, CHUNKS, P], F32R, hh_at + 4096)
    y_hi, _ = place("y_hi", [P, D_MODEL], F32R, hl_at)
    y_lo, _ = place("y_lo", [P, D_MODEL], F32R, hl_at + 4096)
    cst, _ = place("cst", [P, CONST_COLS])
    all_params, _ = place("all_params", [P, DEPTH, PARAM_COLS])
    par, _ = place("par", [P, PARAM_COLS])
    gfin, _ = place("gfin", [P, D_MODEL])
    tables, _ = place("tables", [P, 4, SEQ])
    rope = {k: tables[:, i, :] for i, k in enumerate(("sin64", "sin96", "cos64", "cos96"))}
    stat, _ = place("stat", [P, 64])
    rounds_f, _ = place("rounds_f", [1, 1])
    rounds, _ = place("rounds", [1, 1], I32)
    region = cursor[0]
    gates, gates_at = place("gates", [P, BRANCHES, CHUNKS, SEQ])
    sb_a, _ = place("sb_a", [P, 1536], F32, gates_at)
    sb_b, _ = place("sb_b", [P, 1536], F32, gates_at + 6144)
    sb_c, _ = place("sb_c", [P, 1536], F32, gates_at + 12288)
    lat_hi, _ = place("lat_hi", [P, 3, SEQ], F32R, gates_at + 18432)
    lat_lo, _ = place("lat_lo", [P, 3, SEQ], F32R, gates_at + 21504)
    dil_at = cursor[0]
    dq, dk, dv = ([place(f"d{g}{c}", [P, 2, SEQ])[0] for g in range(3)] for c in "qkv")
    mq, _ = place("mq", [P, HEADS, SEQ])
    mk, _ = place("mk", [P, HEADS, SEQ])
    mv, _ = place("mv", [P, TILES, WIDTH])
    o_hi[0], _ = place("o_hi0", [P, 2, SEQ], F32R)
    o_lo[0], _ = place("o_lo0", [P, 2, SEQ], F32R)
    sbq, sbq_at = place("sbq", [P, 2, SEQ])
    sbk, _ = place("sbk", [P, 2, SEQ])
    sbv, _ = place("sbv", [P, TILES, WIDTH])
    probs, _ = place("probs", [P, 2, 768], F32, sbq_at)
    pT, pT_at = place("pT", [P, 6, P])
    kr, _ = place("kr", [P, SEQ], F32, pT_at)
    rope_tmp, _ = place("rope_tmp", [P, 2, SEQ], F32, pT_at + 1024)
    pos_i, _ = place("pos_i", [P, SEQ], I32, dil_at)
    pos_f, _ = place("pos_f", [P, SEQ], F32, dil_at + 1024)
    turns, _ = place("turns", [P, 4, SEQ], F32, dil_at + 2048)
    full_turns, _ = place("full_turns", [P, 4, SEQ], F32, dil_at + 6144)
    end_mix = cursor[0]
    w_down, _ = place("w_down", [P, DOWN_SLOTS, UNIT], F32, dil_at)
    cursor[0] = region
    extra_hi, _ = place("extra_hi", [P, UNIT], F32R)
    extra_lo, _ = place("extra_lo", [P, UNIT], F32R)
    scomb, _ = place("scomb", [P, PER_GROUP])
    next_scomb, _ = place("next_scomb", [P, PER_GROUP])
    gcomb, _ = place("gcomb", [P, TILES, PER_GROUP])
    sel, _ = place("sel", [P, TILES, P])
    selT, _ = place("selT", [P, TILES, P], F32R)
    comb, _ = place("comb", [P, TILES, EXPERTS])
    slot_of, _ = place("slot_of", [P, TILES * GROUPS])
    gl, _ = place("gl", [P, TILES, GROUPS])
    el, _ = place("el", [P, TILES, EXPERTS])
    r1, _ = place("r1", [P, TILES, EXPERTS])
    r2, _ = place("r2", [P, TILES, EXPERTS])
    hot1, _ = place("hot1", [P, TILES, EXPERTS])
    hot2, _ = place("hot2", [P, TILES, EXPERTS])
    ghot, _ = place("ghot", [P, TILES, GROUPS])
    g1, _ = place("g1", [P, TILES, GROUPS])
    th, _ = place("th", [P, 2, WIDTH])
    assert cursor[0] <= dil_at, (cursor[0], dil_at)
    cursor[0] = dil_at + 4 * DOWN_SLOTS * UNIT
    hid, _ = place("hid", [P, 2, WIDTH])
    hidT, _ = place("hidT", [P, 2, 2, P])
    assert max(end_mix, cursor[0]) <= nc.sbuf_usable_end, (end_mix, cursor[0], nc.sbuf_usable_end)

    def const(name, rows=P):
        a, b = CONST[name]
        return cst[0:rows, a:b]

    def param(name):
        a, b = PARAM[name]
        return par[:, a:b]

    ctx = ExitStack()
    with ctx:
        ps = ctx.enter_context(nc.psum_tensor("ps", [P, 8, 512], F32))

        def sem(name):
            return ctx.enter_context(nc.semaphore(name))

        OV = ps[:, 3, :]
        SC = ps[:, 4:6, :].rearrange("p b n -> p (b n)")
        TR = ps[:, 6:8, :].rearrange("p b n -> p (b n)")
        GU = [ps[:, 0, :], ps[:, 1, :]]
        HT = [ps[:, 2, 0:256], ps[:, 3, 0:256]]
        SELT, SCOMB = ps[:, 2, 256:512], ps[:, 3, 256:256 + PER_GROUP]

        TR2 = ps[:, 6:8, 0:256]

        def alone(eng, sem_, value):
            eng.wait_ge(sem_, value)
            eng.sem_inc(waits_carried, 1)

        def two(ap):
            return ap.rearrange("p (b n) -> p b n", b=2)

        def pj(name):
            return ps[:, PJ_INDEX[name] % PJ_BANKS, :]

        weights_landed = [sem(f"weights_landed{s}") for s in range(RAW_SLOTS)]
        x_landed, const_landed, params_landed = sem("x_landed"), sem("const_landed"), sem("params_landed")
        down_landed = [sem(f"down_landed{s}") for s in range(DOWN_SLOTS)]
        pos_landed, gfin_landed, out_stored = sem("pos_landed"), sem("gfin_landed"), sem("out_stored")
        split_hi, split_lo = sem("split_hi"), sem("split_lo")
        out_used, a_used, d_used = sem("out_used"), sem("a_used"), sem("d_used")
        pj_full, pj_act, pj_dve = sem("pj_full"), sem("pj_act"), sem("pj_dve")
        dve_chain, dve_gchain, dve_pchain = sem("dve_chain"), sem("dve_gchain"), sem("dve_pchain")
        act_chain = sem("act_chain")
        setup_chain, angles_chain = sem("setup_chain"), sem("angles_chain")
        angles_ready, tables_ready = sem("angles_ready"), sem("tables_ready")
        squares_ready, rstd_ready, hn_ready, pool_chain = (sem("squares_ready"), sem("rstd_ready"),
                                                           sem("hn_ready"), sem("pool_chain"))
        hT_hi_ready, hT_ready = sem("hT_hi_ready"), sem("hT_ready")
        z_full, softplus_ready, strict_ready, after_full = (sem("z_full"), sem("softplus_ready"),
                                                            sem("strict_ready"), sem("after_full"))
        logw_ready, wexp_ready, w_ready = sem("logw_ready"), sem("wexp_ready"), sem("w_ready")
        lat_sq_ready, lat_full, lat_var, lat_rstd = (sem("lat_sq_ready"), sem("lat_full"),
                                                     sem("lat_var"), sem("lat_rstd"))
        diag_ready, lat_spread = sem("diag_ready"), sem("lat_spread")
        lat_normed, lat_hi_ready, lat_ready = sem("lat_normed"), sem("lat_hi_ready"), sem("lat_ready")
        roped = sem("roped")
        sc_full, max_ready, exp_ready, probs_ready = (sem("sc_full"), sem("max_ready"),
                                                      sem("exp_ready"), sem("probs_ready"))
        tr_full, pT_ready = sem("tr_full"), sem("pT_ready")
        av_done = sem("av_done")
        ov_full, o_hi_ready, o_ready = sem("ov_full"), sem("o_hi_ready"), sem("o_ready")
        merged_done, m_hi_ready, m_ready = sem("merged_done"), sem("m_hi_ready"), sem("m_ready")
        mix_full, x_mixed = sem("mix_full"), sem("x_mixed")
        route_max, route_exp, ghot_ready, routed = (sem("route_max"), sem("route_exp"),
                                                    sem("ghot_ready"), sem("routed"))
        sel_ready, gather_full, selT_ready, xgf_ready = (sem("sel_ready"), sem("gather_full"),
                                                         sem("selT_ready"), sem("xgf_ready"))
        xg_hi_ready, xg_ready = sem("xg_hi_ready"), sem("xg_ready")
        gu_full, th_ready, hid_ready, ht_full = sem("gu_full"), sem("th_ready"), sem("hid_ready"), sem("ht_full")
        hidT_ready = sem("hidT_ready")
        y_full, y_hi_ready, y_ready, scatter_full, x_moe = (sem("y_full"), sem("y_hi_ready"), sem("y_ready"),
                                                            sem("scatter_full"), sem("x_moe"))
        out_ready, waits_carried = sem("out_ready"), sem("waits_carried")

        block = ctx.enter_context(nc.Block())

        def slot_width(n):
            return FILL.get(MIX[n], UNIT) if n < MIX_UNITS else UNIT

        def pj_emptied(name):
            i = PJ_INDEX[name]
            who = PJ[i][1]
            return who, sum(w == who for _, w in PJ[:i + 1])

        def moe_slot(v):
            slot = v % MOE_SLOTS
            return (extra_hi[:, :], extra_lo[:, :]) if slot == SPLIT_SLOTS else (w_hi[:, slot, :], w_lo[:, slot, :])

        def spans(h, b, kind):
            if kind == "mla":
                return [(0, 0, 128, None), (1, 128, 256, None)]
            w = 128 * (b + 1)
            return [(b, g * w, w, g) for g in range(3)]

        @block.sync
        def _(sp):
            def load(n, slot, src, width):
                sp.wait_ge(split_lo, n + 1)
                sp.dma_start(raw[:, slot, 0:width], src).then_inc(weights_landed[slot], 16)

            def load_down(e, src, q=None):
                if q is None:
                    sp.wait_ge(ov_full, (layer + 1) * BRANCHES)
                elif e == 3:
                    sp.wait_ge(y_full, q)
                else:
                    sp.wait_ge(d_used, q * 3 + e - 2)
                sp.dma_start(w_down[:, e, :], src).then_inc(down_landed[e], 16)

            def load_group(base, src, q=None):
                for u, name in enumerate(MOE):
                    if name[0] == "D":
                        load_down(int(name[1]), src(u), q)
                    else:
                        v = MOE_SPLIT.index(name)
                        load(base + v, v % RAW_SLOTS, src(u), UNIT)

            sp.dma_start(xt[:, :, :], x.rearrange("(t p) d -> p t d", p=P)).then_inc(x_landed, 16)
            sp.sem_inc(split_lo, RAW_SLOTS)
            with sp.Fori(0, DEPTH) as layer:
                alone(sp, routed, layer + 1)
                before = sp.value_load(rounds[0:1, 0:1], min_val=0, max_val=2 * DEPTH)
                first = sp.snap(layer * MIX_UNITS + before * MOE_UNITS)
                for u in range(MIX_UNITS):
                    load(first + u, u % RAW_SLOTS, mix_weights[layer, u, :, 0:slot_width(u)], slot_width(u))
                first = sp.snap((layer + 1) * MIX_UNITS + before * MOE_UNITS)
                load_group(first, lambda u: moe_weights[layer, 0, u])
                with sp.Fori(1, GROUPS) as g:
                    load_group(sp.snap(first + g * GROUP_UNITS), lambda u: moe_weights[layer, g, u],
                               sp.snap(before * GROUPS + g))
                alone(sp, routed, layer + 2)
                end = sp.value_load(rounds[0:1, 0:1], min_val=0, max_val=2 * DEPTH)
                with sp.If(end - before - 1):
                    with sp.Fori(0, GROUPS) as g:
                        load_group(sp.snap(first + MOE_UNITS + g * GROUP_UNITS), lambda u: moe_weights[layer, g, u],
                                   sp.snap((before + 1) * GROUPS + g))
            end = sp.value_load(rounds[0:1, 0:1], min_val=0, max_val=2 * DEPTH)
            last = sp.snap(DEPTH * MIX_UNITS + end * MOE_UNITS)
            for u in range(SPLIT_SLOTS):
                load(last + u, u, mix_weights[0, u, :, 0:16], 16)
            sp.wait_ge(out_ready, 1)
            sp.dma_start(out.rearrange("(t p) d -> p t d", p=P), hn[:, :, :]).then_inc(out_stored, 16)
            sp.wait_ge(out_stored, 16)
            for s in range(RAW_SLOTS):
                sp.wait_ge(weights_landed[s], 16)

        @block.scalar
        def _(act):
            def split(u, width=UNIT, hi=None):
                slot = u % RAW_SLOTS
                hi = w_hi[:, u % SPLIT_SLOTS, :] if hi is None else hi
                act.wait_ge(weights_landed[slot], 16 * (landed + u // RAW_SLOTS + 1))
                act.activation(hi[:, 0:width], raw[:, slot, 0:width], ACT.Copy).then_inc(split_hi, 1)

            act.dma_start(cst[:, :], constants).then_inc(const_landed, 16)
            act.dma_start(pos_i[:, :], positions.broadcast_to([P, SEQ])).then_inc(pos_landed, 16)
            act.dma_start(all_params[:, :, :], params.rearrange("l p n -> p l n")).then_inc(params_landed, 16)
            act.dma_start(gfin[:, :], g_final.broadcast_to([P, D_MODEL])).then_inc(gfin_landed, 16)

            def squares():
                for t in range(TILES):
                    act.activation(hn[:, t, :], xt[:, t, :], ACT.Square,
                                   accum_out=stat[:, t:t + 1]).then_inc(squares_ready, 1)

            act.wait_ge(x_landed, 16)
            act.sem_inc(x_moe, 1)
            squares()
            landed = 0
            for u in range(SPLIT_SLOTS):
                split(u)
            with act.Fori(0, DEPTH) as layer:
                alone(act, routed, layer + 1)
                before = act.value_load(rounds[0:1, 0:1], min_val=0, max_val=2 * DEPTH)
                landed = act.snap(layer * (MIX_UNITS // RAW_SLOTS) + before * (MOE_UNITS // RAW_SLOTS))

                def full(name):
                    act.wait_ge(pj_full, layer * len(PJ) + PJ_INDEX[name] + 1)

                def after(u):
                    if u < MIX_UNITS - 4:
                        full(LAST_FILL[u])
                    elif u < MIX_UNITS - 1:
                        act.wait_ge(out_used, layer * 3 + u - (MIX_UNITS - 4) + 1)
                    else:
                        act.wait_ge(mix_full, layer + 1)
                    split(u + SPLIT_SLOTS, slot_width(u + SPLIT_SLOTS))

                def copy(name, dst, src=None):
                    full(name)
                    act.activation(dst, pj(name) if src is None else src, ACT.Copy).then_inc(pj_act, 1)

                for c in range(4):
                    act.wait_ge(pj_dve, layer * PJ_TOTAL["dve"] + c + 1)
                    act.activation(hT_hi[:, 2 * c:2 * c + 2, :], hTf[:, 2 * c:2 * c + 2, :],
                                   ACT.Copy).then_inc(hT_hi_ready, 1)
                after(0)
                copy("sbq", sbq[:, :, :])
                after(1)
                copy("sbk", sbk[:, :, :])
                after(2)
                copy("sbv", sbv[:, :, :])
                act.wait_ge(z_full, layer + 1)
                act.activation(sb_a[:, 0:1024], SC[:, :], ACT.Abs, scale=HEAD ** -0.5)
                act.activation(two(sb_a[:, 1024:1536]), TR2, ACT.Abs, scale=HEAD ** -0.5).then_inc(act_chain, 1)
                act.wait_ge(act_chain, layer * ACT_LAYER_STEPS + 1)
                act.activation(sb_a[:, :], sb_a[:, :], ACT.Exp, scale=-1.0).then_inc(act_chain, 1)
                act.wait_ge(act_chain, layer * ACT_LAYER_STEPS + 2)
                act.activation(sb_a[:, :], sb_a[:, :], ACT.Ln, bias=1.0).then_inc(softplus_ready, 1)
                after(3)
                full("cq")
                act.activation(lat_sq[:, 0:2, :], pj("cq"), ACT.Square)
                copy("cq", lat[:, 0:2, :])
                after(4)
                full("ckv")
                act.activation(lat_sq[:, 2, :], pj("ckv")[:, 0:SEQ], ACT.Square).then_inc(lat_sq_ready, 1)
                copy("ckv", lat[:, 2, :], pj("ckv")[:, 0:SEQ])
                after(5)
                with act.If(1 - layer):
                    act.wait_ge(angles_ready, 1)
                    act.activation(tables[:, :, :], tables[:, :, :], ACT.Sin).then_inc(tables_ready, 1)
                copy("kr", kr[0:MLA_QK, :], pj("kr")[0:MLA_QK, 0:SEQ])
                after(6)
                copy("d0q", dq[0][:, :, :])
                act.wait_ge(lat_normed, layer + 1)
                act.activation(lat_hi[:, :, :], lat[:, :, :], ACT.Copy).then_inc(lat_hi_ready, 1)
                after(7)
                copy("d0k", dk[0][:, :, :])
                act.wait_ge(logw_ready, layer + 1)
                act.activation(sb_b[:, :], sb_b[:, :], ACT.Exp).then_inc(wexp_ready, 1)
                after(8)
                copy("d0v", dv[0][:, :, :])
                after(9)
                for i in range(2):
                    copy(f"uq{i}", mq[0:MLA_QK, 2 * i:2 * i + 2, :], pj(f"uq{i}")[0:MLA_QK, :])
                act.wait_ge(ov_full, layer * BRANCHES + 1)
                act.activation(o_hi[0][:, :, :], OV, ACT.Copy).then_inc(o_hi_ready, 1)
                after(10)
                for i in range(2):
                    copy(f"ukv{i}", mk[0:NOPE, 2 * i:2 * i + 2, :], pj(f"ukv{i}")[0:NOPE, :])
                copy("ukvv", mv[:, :, :])
                for u, name, dst in ((11, "d1q", dq[1]), (12, "d1k", dk[1]), (13, "d1v", dv[1]),
                                     (14, "d2q", dq[2]), (15, "d2k", dk[2]), (16, "d2v", dv[2])):
                    after(u)
                    copy(name, dst[:, :, :])

                def exps(j):
                    kind, h, b = JOBS[j]
                    act.wait_ge(max_ready, layer * len(JOBS) + j + 1)
                    rows = ((0, 128), (128, 384)) if kind == "mla" else ((0, 384 * (b + 1)),)
                    for i, (lo, hi) in enumerate(rows):
                        ins = act.activation(probs[:, j % 2, lo:hi], probs[:, j % 2, lo:hi], ACT.Exp,
                                             bias=stat[:, 8 + 4 * (j % 2) + i:9 + 4 * (j % 2) + i],
                                             accum_out=stat[:, 16 + 4 * (j % 2) + i:17 + 4 * (j % 2) + i])
                    ins.then_inc(exp_ready, 1)

                def out_of_transposes(j):
                    kind, h, b = JOBS[j]
                    n = 6 if b == 1 else 3
                    act.wait_ge(tr_full, layer * len(JOBS) + j + 1)
                    if j == HEADS:
                        act.wait_ge(ov_full, layer * BRANCHES + 2)
                    elif j >= 1:
                        act.wait_ge(av_done, layer * (len(JOBS) - 2) + j - (j > HEADS))
                    act.activation(pT[:, 0:n, :], TR[:, 0:128 * n], ACT.Copy).then_inc(pT_ready, 1)

                for i in range(12):
                    if i == 6:
                        act.wait_ge(ov_full, layer * BRANCHES + 2)
                        act.activation(o_hi[1][:, :, :], OV, ACT.Copy).then_inc(o_hi_ready, 1)
                    if i >= 1:
                        exps(i - 1)
                    after(17 + i)
                    full(f"gate{i}")
                    act.activation(gates[:, i // 4, 2 * (i % 4):2 * (i % 4) + 2, :], pj(f"gate{i}"), ACT.Tanh,
                                   scale=0.5).then_inc(pj_act, 1)
                    if i >= 1:
                        out_of_transposes(i - 1)
                exps(11)
                after(29)
                out_of_transposes(11)
                after(30)
                act.wait_ge(ov_full, layer * BRANCHES + 3)
                act.activation(o_hi[2][:, :, :], OV, ACT.Copy).then_inc(o_hi_ready, 1)
                after(31)
                for j in range(4):
                    act.wait_ge(merged_done, layer * 4 + j + 1)
                    act.activation(m_hi[:, 2 * j:2 * j + 2, :], merged[:, 2 * j:2 * j + 2, :], ACT.Copy,
                                   scale=0.5).then_inc(m_hi_ready, 1)
                for u in range(32, 36):
                    after(u)

                act.wait_ge(x_mixed, layer + 1)
                squares()
                act.wait_ge(route_max, layer + 1)
                ins = act.activation(g1[:, :, :], g1[:, :, :], ACT.Exp)
                act.activation(stat[:, 36:38], stat[:, 36:38], ACT.Exp).then_inc(route_exp, 1)
                alone(act, routed, layer + 2)
                end = act.value_load(rounds[0:1, 0:1], min_val=0, max_val=2 * DEPTH)

                def group(r, g, last):
                    q = act.snap(r * GROUPS + g)
                    landed = act.snap((layer + 1) * (MIX_UNITS // RAW_SLOTS) + q * (GROUP_UNITS // RAW_SLOTS))

                    def ahead(v):
                        n = v + SPLIT_SLOTS
                        act.wait_ge(weights_landed[n % RAW_SLOTS], 16 * (landed + n // RAW_SLOTS + 1))
                        act.activation(moe_slot(n)[0], raw[:, n % RAW_SLOTS, :], ACT.Copy).then_inc(split_hi, 1)

                    def tanh(e):
                        act.wait_ge(gu_full, q * PER_GROUP + e + 1)
                        act.activation(th[:, e % 2, :], GU[e % 2][:, 0:WIDTH], ACT.Tanh,
                                       scale=0.5).then_inc(th_ready, 1)

                    def transposed_hidden(e):
                        act.wait_ge(ht_full, q * PER_GROUP + e + 1)
                        act.activation(hidT[:, e % 2, :, :], HT[e % 2], ACT.Copy).then_inc(hidT_ready, 1)

                    ahead(0)
                    for e in range(PER_GROUP):
                        act.wait_ge(a_used, q * PER_GROUP + e + 1)
                        if e >= 1:
                            transposed_hidden(e - 1)
                        ahead(2 * e + 1)
                        tanh(e)
                        if e == 0:
                            act.activation(selT[:, :, :], SELT, ACT.Copy).then_inc(selT_ready, 1)
                        if e < PER_GROUP - 1:
                            ahead(2 * e + 2)
                    if not last:
                        act.wait_ge(xgf_ready, q + 2)
                        act.activation(xg_hi[:, :, :], xgf[:, :, :], ACT.Copy).then_inc(xg_hi_ready, 1)
                    transposed_hidden(PER_GROUP - 1)
                    act.wait_ge(y_full, q + 1)
                    act.activation(y_hi[:, :], SC[:, :], ACT.Copy).then_inc(y_hi_ready, 1)

                with act.Fori(before, end) as r:
                    act.wait_ge(xgf_ready, r * GROUPS + 1)
                    act.activation(xg_hi[:, :, :], xgf[:, :, :], ACT.Copy).then_inc(xg_hi_ready, 1)
                    with act.Fori(0, GROUPS - 1) as g:
                        group(r, g, False)
                    group(r, GROUPS - 1, True)
                act.wait_ge(x_moe, end * GROUPS + 1)
                squares()

        @block.gpsimd
        def _(pool):
            def rsqrt(out_, in_, exponent):
                return pool.tensor_tensor(out_, in_, exponent, ALU.pow)

            def norm_rstd(n):
                alone(pool, squares_ready, TILES * (n + 1))
                pool.tensor_scalar(stat[:, 2:4], stat[:, 0:2], 1.0 / D_MODEL, EPS, ALU.mult,
                                   ALU.add).then_inc(pool_chain, 1)
                pool.wait_ge(pool_chain, n + 1)
                rsqrt(stat[:, 4:6], stat[:, 2:4], const("minus_half")[:, 0:2]).then_inc(rstd_ready, 1)

            angle_steps = [0]

            def step(ins):
                angle_steps[0] += 1
                ins.then_inc(angles_chain, 1)
                pool.wait_ge(angles_chain, angle_steps[0])

            pool.wait_ge(const_landed, 16)
            norm_rstd(0)
            pool.wait_ge(pos_landed, 16)
            step(pool.tensor_copy(pos_f[:, :], pos_i[:, :]))
            for i, freq in enumerate(("freq64", "freq96", "freq64", "freq96")):
                ins = pool.tensor_scalar(tables[:, i, :], pos_f[:, :], const(freq), None, ALU.mult)
            step(ins)
            two_pi = 2 * np.pi
            for half, lead in ((slice(0, 2), 0.0), (slice(2, 4), 0.25)):
                ins = pool.tensor_scalar(turns[:, half, :], tables[:, half, :], 1.0 / two_pi, lead, ALU.mult, ALU.add)
            step(ins)
            step(pool.tensor_scalar(turns[:, :, :], turns[:, :, :], 12582912.0, None, ALU.add))
            step(pool.tensor_scalar(turns[:, :, :], turns[:, :, :], 12582912.0, None, ALU.subtract))
            parts = [6.25, 0.033203125]
            parts.append(float(np.float32(two_pi - sum(parts))))
            for part in parts:
                step(pool.tensor_scalar(full_turns[:, :, :], turns[:, :, :], part, None, ALU.mult))
                step(pool.tensor_tensor(tables[:, :, :], tables[:, :, :], full_turns[:, :, :], ALU.subtract))
            step(pool.tensor_scalar(tables[:, 2:4, :], tables[:, 2:4, :], 0.25 * two_pi, None, ALU.add))
            pool.tensor_scalar(tables[:, :, :], tables[:, :, :], 3.1415925, -3.1415925, ALU.min,
                               ALU.max).then_inc(angles_ready, 1)
            with pool.Fori(0, DEPTH) as layer:
                pool.wait_ge(lat_var, layer + 1)
                rsqrt(stat[:, 60:64], stat[:, 56:60], const("minus_half")).then_inc(lat_rstd, 1)
                norm_rstd(layer * 2 + 1)
                norm_rstd(layer * 2 + 2)

        @block.vector
        def _(dve):
            steps = {"layer": 0}

            def link(ins, base):
                steps["layer"] += 1
                ins.then_inc(dve_chain, 1)
                dve.wait_ge(dve_chain, base + steps["layer"])

            setup = [0]

            def slink(ins):
                setup[0] += 1
                ins.then_inc(setup_chain, 1)
                dve.wait_ge(setup_chain, setup[0])

            def split(n, u, width=UNIT, slots=None):
                dve.wait_ge(split_hi, n + 1)
                hi, lo = slots or (w_hi[:, u % SPLIT_SLOTS, :], w_lo[:, u % SPLIT_SLOTS, :])
                dve.tensor_tensor(lo[:, 0:width], raw[:, u % RAW_SLOTS, 0:width],
                                  hi[:, 0:width].bitcast(F32), ALU.subtract).then_inc(split_lo, 1)

            slink(dve.memset(rounds_f[:, :], 0.0))
            dve.tensor_copy(rounds[:, :], rounds_f[:, :]).then_inc(routed, 1)
            for u in range(SPLIT_SLOTS):
                split(u, u)
            dve.wait_ge(params_landed, 16)
            dve.wait_ge(x_landed, 16)
            dve.wait_ge(const_landed, 16)

            def normed(n):
                dve.wait_ge(rstd_ready, n + 1)
                for t in range(TILES):
                    ins = dve.tensor_scalar(hn[:, t, :], xt[:, t, :], stat[:, 4 + t:5 + t], None, ALU.mult)
                return ins

            with dve.Fori(0, DEPTH) as layer:
                steps["layer"] = 0
                alone(dve, routed, layer + 1)
                before = dve.value_load(rounds[0:1, 0:1], min_val=0, max_val=2 * DEPTH)
                first = dve.snap(layer * MIX_UNITS + before * MOE_UNITS)
                base = dve.snap(layer * DVE_LAYER_STEPS)

                def chain(ins):
                    link(ins, base)

                def full(name):
                    dve.wait_ge(pj_full, layer * len(PJ) + PJ_INDEX[name] + 1)

                def after(u):
                    split(first + u + SPLIT_SLOTS, u + SPLIT_SLOTS, slot_width(u + SPLIT_SLOTS))

                def scaled_transposes(prefix, gain, c):
                    full(f"{prefix}{c}")
                    g = param(gain)[:, 2 * c:2 * c + 2].unsqueeze(2).broadcast_to([P, 2, SEQ])
                    dve.tensor_tensor(hTf[:, 2 * c:2 * c + 2, :],
                                      pj(f"{prefix}{c}").rearrange("p (c t) -> p c t", c=2), g,
                                      ALU.mult).then_inc(pj_dve, 1)

                def rotate(name, dst, rows, width, cos, sin):
                    full(name)
                    dve.wait_ge(tables_ready, 1)
                    if name != ROTATIONS[0]:
                        dve.wait_ge(roped, layer * len(ROTATIONS) + ROTATIONS.index(name))
                    swapped = pj(name)[rows, 0:width].rearrange("p (h t) -> p h t", t=SEQ)
                    h = width // SEQ
                    table = lambda k: rope[k][rows, :].unsqueeze(1).broadcast_to([dst.shape[0], h, SEQ])
                    dve.tensor_tensor(rope_tmp[rows, 0:h, :], swapped, table(sin), ALU.mult).then_inc(pj_dve, 1)
                    chain(dve.tensor_tensor(dst, dst, table(cos), ALU.mult))
                    return dve.tensor_tensor(dst, dst, rope_tmp[rows, 0:h, :], ALU.add)

                chain(dve.tensor_copy(par[:, :], all_params[:, layer, :]))
                normed(layer * 2).then_inc(hn_ready, 1)

                def low_hT(c):
                    dve.wait_ge(hT_hi_ready, layer * 4 + c + 1)
                    dve.tensor_tensor(hT_lo[:, 2 * c:2 * c + 2, :], hTf[:, 2 * c:2 * c + 2, :],
                                      hT_hi[:, 2 * c:2 * c + 2, :].bitcast(F32), ALU.subtract).then_inc(hT_ready, 1)

                for c in range(4):
                    scaled_transposes("norm", "g_mix", c)
                    if c >= 1:
                        low_hT(c - 1)
                low_hT(3)
                for u in range(4):
                    after(u)
                scale = HEAD ** -0.5
                blocks = ((ps[:, 4:6, :], 0, 1024, 256), (TR2, 1024, 1536, 128))
                dve.wait_ge(z_full, layer + 1)
                for z, lo, hi, _ in blocks:
                    ins = dve.tensor_scalar(two(sb_b[:, lo:hi]), z, scale, 0.0, ALU.mult, ALU.min)
                chain(ins)
                dve.wait_ge(softplus_ready, layer + 1)
                chain(dve.tensor_tensor(sb_b[:, :], sb_b[:, :], sb_a[:, :], ALU.subtract))
                for z, lo, hi, _ in blocks:
                    ins = dve.scalar_tensor_tensor(out=two(sb_c[:, lo:hi]), in0=z, scalar=-scale, in1=two(sb_b[:, lo:hi]),
                                                   op0=ALU.mult, op1=ALU.add)
                chain(ins)

                def strict(buf, lo, hi, w):
                    view = buf[:, lo:hi].rearrange("p (h t) -> p h t", t=w)
                    mask = const("sb_mask")[:, 0:w].unsqueeze(1).broadcast_to([P, HEADS, w])
                    return dve.tensor_tensor(view, view, mask, ALU.mult)

                for z, lo, hi, w in blocks:
                    ins = strict(sb_c, lo, hi, w)
                ins.then_inc(strict_ready, 1)
                after(4)
                after(5)
                dve.wait_ge(lat_full, layer + 1)
                dve.tensor_scalar(stat[:, 56:58], OV[:, 0:2], 1.0 / WIDTH, EPS, ALU.mult, ALU.add)
                dve.tensor_scalar(stat[:, 58:60], OV[:, 2:4], 1.0 / P, EPS, ALU.mult,
                                  ALU.add).then_inc(lat_var, 1)
                after(6)
                dve.wait_ge(lat_rstd, layer + 1)
                for i in range(4):
                    ins = dve.tensor_scalar(lat_diag[:, i, :], const("ident"), stat[:, 60 + i:61 + i], None, ALU.mult)
                ins.then_inc(diag_ready, 1)
                rows = slice(0, MLA_QK)
                chain(rotate("sw_kr", kr[rows, :].unsqueeze(1), rows, SEQ, "cos96", "sin96"))
                dve.tensor_copy(mk[NOPE:MLA_QK, :, :],
                                kr[NOPE:MLA_QK, :].unsqueeze(1).broadcast_to([ROPE, HEADS, SEQ])).then_inc(roped, 1)
                dve.wait_ge(lat_spread, layer + 1)
                for c in range(3):
                    gain = param("g_q")[:, c:c + 1] if c < 2 else param("g_kv")
                    ins = dve.scalar_tensor_tensor(out=lat[:, c, :], in0=lat[:, c, :], scalar=gain,
                                                   in1=OV[:, (c // 2) * SEQ:(c // 2 + 1) * SEQ], op0=ALU.mult, op1=ALU.mult)
                ins.then_inc(lat_normed, 1)
                dve.wait_ge(lat_hi_ready, layer + 1)
                dve.tensor_tensor(lat_lo[:, :, :], lat[:, :, :], lat_hi[:, :, :].bitcast(F32),
                                  ALU.subtract).then_inc(lat_ready, 1)
                after(7)
                dve.wait_ge(after_full, layer + 1)
                for z, lo, hi, _ in blocks:
                    ins = dve.tensor_tensor(two(sb_b[:, lo:hi]), z, two(sb_b[:, lo:hi]), ALU.add)
                ins.then_inc(logw_ready, 1)
                after(8)
                rows = slice(0, P)
                rotate("sw_d0q", dq[0][:, :, :], rows, 512, "cos64", "sin64").then_inc(roped, 1)
                dve.wait_ge(wexp_ready, layer + 1)
                for z, lo, hi, w in blocks:
                    ins = strict(sb_b, lo, hi, w)
                ins.then_inc(w_ready, 1)
                rotate("sw_d0k", dk[0][:, :, :], rows, 512, "cos64", "sin64").then_inc(roped, 1)
                after(9)

                def low_o(n):
                    dve.wait_ge(o_hi_ready, layer * BRANCHES + n + 1)
                    dve.tensor_tensor(o_lo[n][:, :, :], OV.rearrange("p (c t) -> p c t", c=2),
                                      o_hi[n][:, :, :].bitcast(F32), ALU.subtract).then_inc(o_ready, 1)

                low_o(0)
                after(10)
                rows = slice(0, MLA_QK)
                for i in range(2):
                    rotate(f"sw_mq{i}", mq[rows, 2 * i:2 * i + 2, :], rows, 512, "cos96", "sin96").then_inc(roped, 1)
                rows = slice(0, P)
                after(11)
                after(12)
                after(13)
                rotate("sw_d1q", dq[1][:, :, :], rows, 512, "cos64", "sin64").then_inc(roped, 1)
                after(14)
                rotate("sw_d1k", dk[1][:, :, :], rows, 512, "cos64", "sin64").then_inc(roped, 1)
                after(15)
                after(16)
                rotate("sw_d2q", dq[2][:, :, :], rows, 512, "cos64", "sin64").then_inc(roped, 1)

                def masked(j):
                    kind, h, b = JOBS[j]
                    dve.wait_ge(sc_full, layer * len(JOBS) + j + 1)
                    w = 768 if b == 1 else 384
                    mask = const("mla_mask" if kind == "mla" else f"dil_mask{b}")
                    chain(dve.scalar_tensor_tensor(out=probs[:, j % 2, 0:w], in0=SC[:, 0:w], scalar=
                                                   (MLA_QK if kind == "mla" else HEAD) ** -0.5, in1=mask,
                                                   op0=ALU.mult, op1=ALU.add))
                    rows = ((0, 128), (128, 384)) if kind == "mla" else ((0, w),)
                    for i, (lo, hi) in enumerate(rows):
                        ins = dve.tensor_reduce(stat[:, 8 + 4 * (j % 2) + i:9 + 4 * (j % 2) + i],
                                                probs[:, j % 2, lo:hi], AX.X, ALU.max, negate=True)
                    ins.then_inc(max_ready, 1)

                def normalised(j):
                    kind, h, b = JOBS[j]
                    dve.wait_ge(exp_ready, layer * len(JOBS) + j + 1)
                    w = 768 if b == 1 else 384
                    rows = ((0, 128), (128, 384)) if kind == "mla" else ((0, w),)
                    s, r = 16 + 4 * (j % 2), 24 + 4 * (j % 2)
                    chain(dve.reciprocal(stat[:, r:r + len(rows)], stat[:, s:s + len(rows)]))
                    for i, (lo, hi) in enumerate(rows):
                        ins = dve.tensor_scalar(probs[:, j % 2, lo:hi], probs[:, j % 2, lo:hi],
                                                stat[:, r + i:r + i + 1], None, ALU.mult)
                    ins.then_inc(probs_ready, 1)

                for i in range(12):
                    if i == 6:
                        low_o(1)
                    if i >= 1:
                        normalised(i - 1)
                    after(17 + i)
                    if i == 0:
                        rotate("sw_d2k", dk[2][:, :, :], rows, 512, "cos64", "sin64").then_inc(roped, 1)
                    masked(i)
                normalised(11)

                def merge(n, j):
                    full(f"branch{n}_{j}")
                    dst = (merged if n == 0 else gates[:, n])[:, 2 * j:2 * j + 2, :]
                    ins = dve.scalar_tensor_tensor(out=dst, in0=gates[:, n, 2 * j:2 * j + 2, :], scalar=1.0,
                                                   in1=pj(f"branch{n}_{j}").rearrange("p (c t) -> p c t", c=2),
                                                   op0=ALU.add, op1=ALU.mult)
                    ins.then_inc(pj_dve, 1)
                    if n > 0:
                        who, count = pj_emptied(f"branch{n}_{j}")
                        dve.wait_ge(pj_dve, layer * PJ_TOTAL["dve"] + count)
                        m = merged[:, 2 * j:2 * j + 2, :]
                        ins = dve.tensor_tensor(m, m, dst, ALU.add)
                        if n == 1:
                            chain(ins)
                        else:
                            ins.then_inc(merged_done, 1)

                for n in range(BRANCHES):
                    if n == 2:
                        low_o(2)
                    for j in range(4):
                        merge(n, j)
                    after(29 + n)
                for j in range(4):
                    dve.wait_ge(m_hi_ready, layer * 4 + j + 1)
                    dve.scalar_tensor_tensor(out=m_lo[:, 2 * j:2 * j + 2, :], in0=merged[:, 2 * j:2 * j + 2, :],
                                             scalar=0.5, in1=m_hi[:, 2 * j:2 * j + 2, :].bitcast(F32),
                                             op0=ALU.mult, op1=ALU.subtract).then_inc(m_ready, 1)
                for u in range(32, 36):
                    after(u)
                dve.wait_ge(mix_full, layer + 1)
                dve.tensor_tensor(xt[:, 0, :], xt[:, 0, :], SC, ALU.add)
                dve.tensor_tensor(xt[:, 1, :], xt[:, 1, :], TR, ALU.add).then_inc(x_mixed, 1)

                normed(layer * 2 + 1).then_inc(hn_ready, 1)
                for c in range(4):
                    scaled_transposes("moe_norm", "g_ffn", c)
                full("logits")
                logits = pj("logits")[:, 0:2 * 20].rearrange("p (t n) -> p t n", n=20)
                bias = param("bias").unsqueeze(1).broadcast_to([P, TILES, 20])
                chain(dve.tensor_tensor(gl[:, :, :], logits[:, :, 0:GROUPS], bias[:, :, 0:GROUPS], ALU.add))
                ins = dve.tensor_tensor(el[:, :, :], logits[:, :, GROUPS:20], bias[:, :, GROUPS:20], ALU.add)
                ins.then_inc(pj_dve, 1)

                def over(col, n):
                    return stat[:, col:col + 2].unsqueeze(2).broadcast_to([P, TILES, n])

                def first_largest(hot, values, top, tmp, n):
                    chain(dve.tensor_reduce(stat[:, top:top + 2], values, AX.X, ALU.max))
                    chain(dve.tensor_tensor(tmp, values, over(top, n), ALU.is_equal))
                    order = const(f"first{n}").unsqueeze(1).broadcast_to([P, TILES, n])
                    chain(dve.tensor_tensor(tmp, tmp, order, ALU.mult))
                    chain(dve.tensor_reduce(stat[:, 34:36], tmp, AX.X, ALU.max))
                    return dve.tensor_tensor(hot, tmp, over(34, n), ALU.is_equal)

                first_largest(ghot[:, :, :], gl[:, :, :], 32, g1[:, :, :], GROUPS).then_inc(ghot_ready, 1)
                dve.wait_ge(ghot_ready, layer + 1)
                chain(dve.tensor_tensor(g1[:, :, :], gl[:, :, :], over(32, GROUPS), ALU.subtract))
                el8 = el[:, :, :].rearrange("p t (g e) -> p (t g) e", e=PER_GROUP)
                gh8 = ghot[:, :, :].rearrange("p t g -> p (t g)")
                r8 = r1[:, :, :].rearrange("p t (g e) -> p (t g) e", e=PER_GROUP)
                wide = lambda a: a.unsqueeze(2).broadcast_to([P, TILES * GROUPS, PER_GROUP])
                chain(dve.tensor_tensor(r8, el8, wide(gh8), ALU.mult))
                chain(dve.tensor_scalar(slot_of[:, :], gh8, -NEG, NEG, ALU.mult, ALU.add))
                chain(dve.tensor_tensor(el8, r8, wide(slot_of[:, :]), ALU.add))
                chain(first_largest(hot1[:, :, :], el[:, :, :], 40, r1[:, :, :], EXPERTS))
                chain(dve.scalar_tensor_tensor(out=el[:, :, :], in0=hot1[:, :, :], scalar=2 * NEG, in1=el[:, :, :],
                                               op0=ALU.mult, op1=ALU.add))
                chain(first_largest(hot2[:, :, :], el[:, :, :], 42, r1[:, :, :], EXPERTS))
                dve.tensor_tensor(stat[:, 36:38], stat[:, 42:44], stat[:, 40:42], ALU.subtract).then_inc(route_max, 1)
                full("rank")
                rank = pj("rank")[:, 0:TILES * GROUPS]
                chain(dve.scalar_tensor_tensor(out=slot_of[:, :], in0=rank, scalar=1.0, in1=gh8,
                                               op0=ALU.add, op1=ALU.mult))
                chain(dve.tensor_scalar(slot_of[:, :], slot_of[:, :], -1.0, None, ALU.add))
                chain(dve.tensor_reduce(stat[:, 44:45], pj("rank")[:, 8:12], AX.X, ALU.max))
                ins = dve.tensor_scalar(stat[:, 45:46], stat[:, 44:45], float(P), 1.0, ALU.is_gt, ALU.add)
                ins.then_inc(pj_dve, 1)
                who, count = pj_emptied("rank")
                dve.wait_ge(pj_dve, layer * PJ_TOTAL["dve"] + count)
                chain(dve.tensor_tensor(rounds_f[:, :], rounds_f[:, :], stat[0:1, 45:46], ALU.add))
                dve.tensor_copy(rounds[:, :], rounds_f[:, :]).then_inc(routed, 1)
                dve.wait_ge(route_exp, layer + 1)
                chain(dve.tensor_reduce(stat[:, 46:48], g1[:, :, :], AX.X, ALU.add))
                chain(dve.tensor_scalar(stat[:, 48:50], stat[:, 36:38], 1.0, 2.0, ALU.add, ALU.mult))
                chain(dve.tensor_tensor(stat[:, 50:52], stat[:, 48:50], stat[:, 46:48], ALU.mult))
                chain(dve.reciprocal(stat[:, 52:54], stat[:, 50:52]))
                chain(dve.tensor_tensor(stat[:, 54:56], stat[:, 52:54], stat[:, 36:38], ALU.mult))
                chain(dve.tensor_tensor(hot1[:, :, :], hot1[:, :, :], over(52, EXPERTS), ALU.mult))
                chain(dve.tensor_tensor(hot2[:, :, :], hot2[:, :, :], over(54, EXPERTS), ALU.mult))
                chain(dve.tensor_tensor(comb[:, :, :], hot1[:, :, :], hot2[:, :, :], ALU.add))
                assert steps["layer"] == DVE_LAYER_STEPS, steps
                alone(dve, routed, layer + 2)
                end = dve.value_load(rounds[0:1, 0:1], min_val=0, max_val=2 * DEPTH)

                def select(g):
                    for t in range(TILES):
                        dve.tensor_scalar(sel[:, t, :], const("iota"), slot_of[:, bass.ds(g + t * GROUPS, 1)],
                                          None, ALU.is_equal)
                    dve.tensor_copy(gcomb[:, :, :],
                                    comb[:, :, bass.ds(g * PER_GROUP, PER_GROUP)]).then_inc(sel_ready, 1)

                def gathered(q):
                    dve.wait_ge(gather_full, q + 1)
                    dve.tensor_copy(next_scomb[:, :], SCOMB)
                    gain = param("g_ffn").unsqueeze(2).broadcast_to([P, CHUNKS, P])
                    dve.tensor_tensor(xgf[:, :, :], TR.rearrange("p (c s) -> p c s", s=P), gain,
                                      ALU.mult).then_inc(xgf_ready, 1)

                def low_gathered(q):
                    dve.wait_ge(xgf_ready, q + 1)
                    dve.tensor_copy(scomb[:, :], next_scomb[:, :])
                    dve.wait_ge(xg_hi_ready, q + 1)
                    dve.tensor_tensor(xg_lo[:, :, :], xgf[:, :, :], xg_hi[:, :, :].bitcast(F32),
                                      ALU.subtract).then_inc(xg_ready, 1)

                def group(r, g, last):
                    q = dve.snap(r * GROUPS + g)
                    first = dve.snap((layer + 1) * MIX_UNITS + q * GROUP_UNITS)

                    def hidden(e):
                        dve.wait_ge(th_ready, q * PER_GROUP + e + 1)
                        dve.scalar_tensor_tensor(out=hid[:, e % 2, :], in0=th[:, e % 2, :], scalar=1.0,
                                                 in1=GU[e % 2][:, 0:WIDTH], op0=ALU.add,
                                                 op1=ALU.mult).then_inc(dve_gchain, 1)
                        dve.wait_ge(dve_gchain, q * PER_GROUP + e + 1)
                        dve.scalar_tensor_tensor(out=hid[:, e % 2, :], in0=hid[:, e % 2, :],
                                                 scalar=scomb[:, e:e + 1], in1=GU[e % 2][:, WIDTH:2 * WIDTH],
                                                 op0=ALU.mult, op1=ALU.mult).then_inc(hid_ready, 1)

                    def ahead(v):
                        n = v + SPLIT_SLOTS
                        split(first + n, n, slots=moe_slot(n))

                    ahead(0)
                    for e in range(PER_GROUP):
                        ahead(2 * e + 1)
                        if e == PER_GROUP - 1:
                            break
                        hidden(e)
                        ahead(2 * e + 2)
                        if e == 1 and not last:
                            select(g + 1)
                        if e == 2 and not last:
                            gathered(q + 1)
                    hidden(PER_GROUP - 1)
                    if not last:
                        dve.wait_ge(hid_ready, q * PER_GROUP + PER_GROUP)
                        low_gathered(q + 1)
                    dve.wait_ge(y_hi_ready, q + 1)
                    dve.tensor_tensor(y_lo[:, :], SC, y_hi[:, :].bitcast(F32), ALU.subtract).then_inc(y_ready, 1)
                    dve.wait_ge(scatter_full, q + 1)
                    dve.tensor_tensor(xt[:, 0, :], xt[:, 0, :], TR, ALU.add)
                    dve.tensor_tensor(xt[:, 1, :], xt[:, 1, :], SC, ALU.add).then_inc(x_moe, 1)

                with dve.Fori(before, end) as r:
                    select(0)
                    gathered(r * GROUPS)
                    low_gathered(r * GROUPS)
                    with dve.Fori(0, GROUPS - 1) as g:
                        group(r, g, False)
                    group(r, GROUPS - 1, True)
                    dve.tensor_scalar(slot_of[:, :], slot_of[:, :], -float(P), None, ALU.add).then_inc(dve_pchain, 1)
                    dve.wait_ge(dve_pchain, r + 1)

            dve.wait_ge(rstd_ready, 2 * DEPTH + 1)
            dve.wait_ge(gfin_landed, 16)
            for t in range(TILES):
                ins = dve.scalar_tensor_tensor(out=hn[:, t, :], in0=xt[:, t, :], scalar=stat[:, 4 + t:5 + t],
                                               in1=gfin[:, :], op0=ALU.mult, op1=ALU.mult)
            ins.then_inc(out_ready, 1)

        @block.tensor
        def _(pe):
            def product(out_, lhs, rhs, start, stop, **kw):
                pe.matmul(out_, lhs[1], rhs[0], start=start, stop=False, **kw)
                pe.matmul(out_, lhs[0], rhs[1], start=False, stop=False, **kw)
                return pe.matmul(out_, lhs[0], rhs[0], start=False, stop=stop, **kw)

            def weights(u, width, cols):
                slot = u % SPLIT_SLOTS
                return tuple(w[:, slot, 0:width].rearrange("p (k n) -> p k n", n=cols) for w in (w_hi, w_lo))

            def at(pair, *index):
                return tuple(w[(slice(None), *index)] for w in pair)

            def use(n):
                pe.wait_ge(split_lo, RAW_SLOTS + n + 1)

            pe.wait_ge(const_landed, 16)
            hT, o, m = (hT_hi, hT_lo), list(zip(o_hi, o_lo)), (m_hi, m_lo)
            with pe.Fori(0, DEPTH) as layer:
                alone(pe, routed, layer + 1)
                before = pe.value_load(rounds[0:1, 0:1], min_val=0, max_val=2 * DEPTH)
                first = pe.snap(layer * MIX_UNITS + before * MOE_UNITS)

                def bank(name):
                    i = PJ_INDEX[name]
                    if i >= PJ_BANKS:
                        who, count = pj_emptied(PJ[i - PJ_BANKS][0])
                        pe.wait_ge({"act": pj_act, "dve": pj_dve}[who], layer * PJ_TOTAL[who] + count)
                    return pj(name)

                def transposes(prefix):
                    for c2 in range(4):
                        b = bank(f"{prefix}{c2}")
                        for c in range(2):
                            for t in range(TILES):
                                ins = pe.transpose(b[:, c * SEQ + t * P:c * SEQ + (t + 1) * P],
                                                   hn[:, t, (2 * c2 + c) * P:(2 * c2 + c + 1) * P], const("ident"))
                        ins.then_inc(pj_full, 1)


                def project(u, fills, cols, act_in=hT, chunks=CHUNKS, wait=None):
                    w = weights(u, chunks * cols, cols)
                    use(first + u)
                    for name, parts in fills:
                        b = bank(name)
                        for col, n, to in parts:
                            for k in range(chunks):
                                if wait is not None and (col, k % 2) == (0, 0):
                                    wait(k)
                                ins = product(b[0:n, to:to + SEQ], at(w, k, slice(col, col + n)),
                                              at(act_in, k), k == 0, k == chunks - 1)
                        ins.then_inc(pj_full, 1)

                def features(name, wait=None):
                    project(MIX.index(name), [(name, [(0, P, 0), (P, P, SEQ)])], WIDTH, wait=wait)

                def tokens(name):
                    u = MIX.index(name)
                    w = weights(u, UNIT, WIDTH)
                    use(first + u)
                    b = bank(name)
                    for t in range(TILES):
                        for k in range(CHUNKS):
                            ins = product(b[:, t * WIDTH:(t + 1) * WIDTH], at(hT, k, slice(t * P, (t + 1) * P)),
                                          at(w, k), k == 0, k == CHUNKS - 1)
                    ins.then_inc(pj_full, 1)

                def act_has(name):
                    pe.wait_ge(pj_act, layer * PJ_TOTAL["act"] + pj_emptied(name)[1])

                def swap(name, src, rows, perm):
                    act_has(name)
                    b = bank(f"sw_{SWAPS[name]}")
                    pe.matmul(b[0:rows, 0:int(np.prod(src.shape[1:]))], const(perm, rows)[:, 0:rows], src,
                              start=True, stop=True).then_inc(pj_full, 1)

                SWAPS = {"kr": "kr", "d0q": "d0q", "d0k": "d0k", "uq0": "mq0", "uq1": "mq1",
                         "d1q": "d1q", "d1k": "d1k", "d2q": "d2q", "d2k": "d2k"}

                def place_of(h):
                    return 2 * (h % 2) + h // 2

                def half(h):
                    return slice(HEAD * (h % 2), HEAD * (h % 2) + HEAD)

                pe.wait_ge(hn_ready, layer * 2 + 1)
                transposes("norm")
                features("sbq", wait=lambda k: pe.wait_ge(hT_ready, layer * 4 + k // 2 + 1))
                features("sbk")
                tokens("sbv")
                features("cq")
                act_has("sbk")
                for h in range(HEADS):
                    pe.matmul(SC[:, place_of(h) * SEQ:(place_of(h) + 1) * SEQ], sbk[half(h), h // 2, 0:P],
                              sbq[half(h), h // 2, :], start=True, stop=True)
                for h in range(HEADS):
                    ins = pe.matmul(TR[:, 512 * (h % 2) + (h // 2) * P:512 * (h % 2) + (h // 2 + 1) * P],
                                    sbk[half(h), h // 2, P:SEQ], sbq[half(h), h // 2, P:SEQ], start=True, stop=True)
                ins.then_inc(z_full, 1)
                project(MIX.index("ckv"), [("ckv", [(0, P, 0)])], P)
                project(MIX.index("kr"), [("kr", [(0, MLA_QK, 0)])], MLA_QK)
                pe.wait_ge(lat_sq_ready, layer + 1)
                for t in range(TILES):
                    for c in range(3):
                        col = TILES * (c // 2) + t
                        ins = pe.matmul(OV[:, col:col + 1], lat_sq[:, c, t * P:(t + 1) * P], const("ones")[:, 0:1],
                                        start=c != 1, stop=c != 0)
                ins.then_inc(lat_full, 1)
                features("d0q")
                swap("kr", kr[0:MLA_QK, :], MLA_QK, "swap96")
                pe.wait_ge(diag_ready, layer + 1)
                pe.matmul(OV, const("ones"), lat_diag[:, :, :].rearrange("p a b -> p (a b)"), start=True,
                          stop=True).then_inc(lat_spread, 1)
                features("d0k")
                pe.wait_ge(strict_ready, layer + 1)
                near, far = sb_c[:, 0:1024], sb_c[:, 1024:1536]
                for i in range(2):
                    pe.matmul(SC[:, i * 512:(i + 1) * 512], const("later"), near[:, i * 512:(i + 1) * 512],
                              start=True, stop=False)
                    pe.matmul(SC[:, i * 512:(i + 1) * 512].rearrange("p (h t) -> p h t", t=SEQ)[:, :, P:SEQ],
                              const("ones"), far[:, i * 256:(i + 1) * 256].rearrange("p (h t) -> p h t", t=P),
                              start=False, stop=True)
                for i in range(2):
                    ins = pe.matmul(TR[:, 512 * i:512 * i + 256], const("later"), far[:, i * 256:(i + 1) * 256],
                                    start=True, stop=True)
                ins.then_inc(after_full, 1)
                tokens("d0v")
                swap("d0q", dq[0][:, :, :], P, "swap64")
                swap("d0k", dk[0][:, :, :], P, "swap64")
                pe.wait_ge(lat_ready, layer + 1)
                latq = (lat_hi[:, 0:2, :], lat_lo[:, 0:2, :])
                project(MIX.index("uq"), [(f"uq{i}", [((2 * i + h) * MLA_QK, MLA_QK, h * SEQ) for h in range(2)])
                                          for i in range(2)], HEADS * MLA_QK, act_in=latq, chunks=2)
                pe.wait_ge(w_ready, layer + 1)
                for h in range(HEADS):
                    to = OV[half(h), (h // 2) * SEQ:(h // 2 + 1) * SEQ]
                    cols = slice(h * HEAD, (h + 1) * HEAD)
                    i = place_of(h)
                    pe.matmul(to, sbv[:, 0, cols], sb_b[:, i * SEQ:(i + 1) * SEQ], start=True, stop=False)
                    ins = pe.matmul(to[:, P:SEQ], sbv[:, 1, cols], sb_b[:, 1024 + i * P:1024 + (i + 1) * P],
                                    start=False, stop=True)
                ins.then_inc(ov_full, 1)
                u = MIX.index("ukv")
                w = weights(u, 512, 512)
                use(first + u)
                latkv = (lat_hi, lat_lo)
                for i in range(2):
                    b = bank(f"ukv{i}")
                    for h in range(2):
                        col = (2 * i + h) * 2 * HEAD
                        ins = product(b[:, h * SEQ:(h + 1) * SEQ], at(w, 0, slice(col, col + P)),
                                      at(latkv, 2), True, True)
                    ins.then_inc(pj_full, 1)
                b = bank("ukvv")
                for t in range(TILES):
                    for h in range(HEADS):
                        col = h * 2 * HEAD + NOPE
                        ins = product(b[:, t * WIDTH + h * HEAD:t * WIDTH + (h + 1) * HEAD],
                                      at(latkv, 2, slice(t * P, (t + 1) * P)), at(w, 0, slice(col, col + HEAD)),
                                      True, True)
                ins.then_inc(pj_full, 1)
                for i in range(2):
                    swap(f"uq{i}", mq[0:MLA_QK, 2 * i:2 * i + 2, :], MLA_QK, "swap96")
                features("d1q")
                features("d1k")
                tokens("d1v")
                swap("d1q", dq[1][:, :, :], P, "swap64")
                features("d2q")
                swap("d1k", dk[1][:, :, :], P, "swap64")
                features("d2k")
                tokens("d2v")
                swap("d2q", dq[2][:, :, :], P, "swap64")

                def scores(j):
                    kind, h, b = JOBS[j]
                    if j >= 1:
                        pe.wait_ge(max_ready, layer * len(JOBS) + j)
                    if kind == "mla":
                        pe.wait_ge(roped, layer * len(ROTATIONS) + 5)
                        act_has("ukvv")
                    else:
                        pe.wait_ge(roped, layer * len(ROTATIONS) + 9)
                    for b_, lo, n, g in spans(h, b, kind):
                        qs = slice(b_ * P, (b_ + 1) * P)
                        if kind == "mla":
                            q_, k_ = mq[0:MLA_QK, h, qs], mk[0:MLA_QK, h, 0:n]
                        else:
                            q_, k_ = dq[g][half(h), h // 2, qs], dk[g][half(h), h // 2, 0:n]
                        ins = pe.matmul(SC[:, lo:lo + n], q_, k_, start=True, stop=True)
                    ins.then_inc(sc_full, 1)

                def transposed(j):
                    pe.wait_ge(probs_ready, layer * len(JOBS) + j + 1)
                    if j >= 1:
                        pe.wait_ge(pT_ready, layer * len(JOBS) + j)
                    for i in range(6 if JOBS[j][2] == 1 else 3):
                        ins = pe.transpose(TR[:, i * P:(i + 1) * P], probs[:, j % 2, i * P:(i + 1) * P], const("ident"))
                    ins.then_inc(tr_full, 1)

                def values(j):
                    kind, h, b = JOBS[j]
                    pe.wait_ge(pT_ready, layer * len(JOBS) + j + 1)
                    if j in (0, HEADS):
                        pe.wait_ge(o_ready, layer * BRANCHES + (1 if j == 0 else 2))
                    to = OV[half(h), (h // 2) * SEQ:(h // 2 + 1) * SEQ]
                    cols = slice(h * HEAD, (h + 1) * HEAD)
                    if kind == "mla":
                        pe.matmul(to, mv[:, 0, cols], pT[:, 0:2, :].rearrange("p a b -> p (a b)"), start=True, stop=False)
                        ins = pe.matmul(to[:, P:SEQ], mv[:, 1, cols], pT[:, 2, :], start=False, stop=True)
                    else:
                        n = 3 * (b + 1)
                        for i in range(n):
                            ins = pe.matmul(to[:, b * P:(b + 1) * P], dv[i // (b + 1)][:, i % (b + 1), cols],
                                            pT[:, i, :], start=i == 0, stop=i == n - 1)
                    if j in (HEADS - 1, len(JOBS) - 1):
                        ins.then_inc(ov_full, 1)
                    else:
                        ins.then_inc(av_done, 1)

                for i in range(12):
                    features(f"gate{i}")
                    if i == 0:
                        swap("d2k", dk[2][:, :, :], P, "swap64")
                    if i >= 1:
                        transposed(i - 1)
                    scores(i)
                    if i >= 2:
                        values(i - 2)

                def branch(n):
                    u = MIX.index(f"branch{n}")
                    pe.wait_ge(o_ready, layer * BRANCHES + n + 1)
                    project(u, [(f"branch{n}_{j}", [((2 * j + f) * P, P, f * SEQ) for f in range(2)])
                                for j in range(4)], D_MODEL, act_in=o[n], chunks=2)

                branch(0)
                transposed(11)
                values(10)
                branch(1)
                values(11)
                branch(2)
                for i in range(4):
                    u = MIX.index(f"out{i}")
                    w = weights(u, UNIT, D_MODEL)
                    use(first + u)
                    pe.wait_ge(m_ready, layer * 4 + i + 1)
                    for t, acc in enumerate((SC, TR)):
                        for n in range(2):
                            for k in range(2):
                                ins = product(acc[:, n * 512:(n + 1) * 512], at(m, 2 * i + k, slice(t * P, (t + 1) * P)),
                                              at(w, k, slice(n * 512, (n + 1) * 512)), (i, k) == (0, 0), (i, k) == (3, 1))
                    ins.then_inc(out_used if i < 3 else mix_full, 1)

                pe.wait_ge(hn_ready, layer * 2 + 2)
                transposes("moe_norm")
                pe.wait_ge(pj_dve, layer * PJ_TOTAL["dve"] + pj_emptied("moe_norm3")[1])
                b = bank("logits")
                router = param("router").rearrange("p (k n) -> p k n", n=20)
                for t in range(TILES):
                    for k in range(CHUNKS):
                        ins = pe.matmul(b[:, t * 20:(t + 1) * 20], hTf[:, k, t * P:(t + 1) * P], router[:, k, :],
                                        start=k == 0, stop=k == CHUNKS - 1)
                ins.then_inc(pj_full, 1)
                pe.wait_ge(ghot_ready, layer + 1)
                b = bank("rank")
                pe.matmul(b[:, 0:4], const("before"), ghot[:, 0, :], start=True, stop=True)
                pe.matmul(b[:, 4:8], const("ones"), ghot[:, 0, :], start=True, stop=False)
                pe.matmul(b[:, 4:8], const("before"), ghot[:, 1, :], start=False, stop=True)
                pe.matmul(b[:, 8:12], const("ones"), ghot[:, 0, :], start=True, stop=False)
                pe.matmul(b[:, 8:12], const("ones"), ghot[:, 1, :], start=False, stop=True).then_inc(pj_full, 1)
                alone(pe, routed, layer + 2)
                end = pe.value_load(rounds[0:1, 0:1], min_val=0, max_val=2 * DEPTH)

                def gather(r, g):
                    q = pe.snap(r * GROUPS + g)
                    pe.wait_ge(sel_ready, q + 1)
                    if not isinstance(g, int):
                        pe.wait_ge(x_moe, q)
                    for t in range(TILES):
                        pe.transpose(SELT[:, t * P:(t + 1) * P], sel[:, t, :], const("ident"))
                    for t in range(TILES):
                        pe.matmul(SCOMB, sel[:, t, :], gcomb[:, t, :], start=t == 0, stop=t == 1)
                    for c in range(CHUNKS):
                        for t in range(TILES):
                            ins = pe.matmul(TR[:, c * P:(c + 1) * P], hn[:, t, c * P:(c + 1) * P], sel[:, t, :],
                                            start=t == 0, stop=t == 1)
                    ins.then_inc(gather_full, 1)

                def gate_up(q, part, e):
                    v = MOE_SPLIT.index(f"{part}{e}")
                    w = tuple(w[:, 0:UNIT].rearrange("p (k n) -> p k n", n=2 * WIDTH) for w in moe_slot(v))
                    use((layer + 1) * MIX_UNITS + q * GROUP_UNITS + v)
                    i = "AB".index(part)
                    for k in range(4):
                        ins = product(GU[e % 2], at((xg_hi, xg_lo), 4 * i + k), at(w, k), (i, k) == (0, 0), (i, k) == (1, 3))
                    ins.then_inc(a_used if i == 0 else gu_full, 1)

                def first_gate_up(q):
                    pe.wait_ge(xg_ready, q + 1)
                    gate_up(q, "A", 0)

                def group(r, g, last):
                    q = pe.snap(r * GROUPS + g)

                    def transposed_hidden(e):
                        pe.wait_ge(hid_ready, q * PER_GROUP + e + 1)
                        if e == 0:
                            pe.wait_ge(selT_ready, q + 1)
                        for f in range(2):
                            ins = pe.transpose(HT[e % 2][:, f * P:(f + 1) * P], hid[:, e % 2, f * P:(f + 1) * P],
                                               const("ident"))
                        ins.then_inc(ht_full, 1)

                    def down(e):
                        pe.wait_ge(hidT_ready, q * PER_GROUP + e + 1)
                        if e == 0:
                            pe.wait_ge(x_moe, q + 1)
                        pe.wait_ge(down_landed[e], 16 * (q + 1))
                        w = w_down[:, e, :].rearrange("p (k n) -> p k n", n=D_MODEL)
                        for f in range(2):
                            for n in range(2):
                                cols = slice(n * 512, (n + 1) * 512)
                                ins = pe.matmul(SC[:, cols], hidT[:, e % 2, f, :], w[:, f, cols],
                                                start=(e, f) == (0, 0), stop=(e, f) == (3, 1))
                        ins.then_inc(d_used if e < 3 else y_full, 1)

                    for e in range(PER_GROUP):
                        if e >= 1:
                            gate_up(q, "A", e)
                            transposed_hidden(e - 1)
                        gate_up(q, "B", e)
                        if e >= 1:
                            down(e - 1)
                        if e == 2 and not last:
                            gather(r, g + 1)
                    transposed_hidden(PER_GROUP - 1)
                    down(PER_GROUP - 1)
                    if not last:
                        first_gate_up(q + 1)
                    pe.wait_ge(y_ready, q + 1)
                    for t, acc in enumerate((TR, SC)):
                        for n in range(2):
                            half_ = slice(n * 512, (n + 1) * 512)
                            pe.matmul(acc[:, half_], selT[:, t, :], y_lo[:, half_], start=True, stop=False)
                            ins = pe.matmul(acc[:, half_], selT[:, t, :], y_hi[:, half_], start=False, stop=True)
                    ins.then_inc(scatter_full, 1)

                with pe.Fori(before, end) as r:
                    gather(r, 0)
                    first_gate_up(r * GROUPS)
                    with pe.Fori(0, GROUPS - 1) as g:
                        group(r, g, False)
                    group(r, GROUPS - 1, True)


def shape_constants():
    c = {}
    i = np.arange(P)
    c["ident"] = np.eye(P)
    c["before"] = i[:, None] < i[None, :]
    c["later"] = i[:, None] > i[None, :]
    c["ones"] = np.ones((P, P))
    swap = np.zeros((P, P))
    for f in range(P):
        swap[(f + 32 if f % 64 < 32 else f - 32), f] = -1 if f % 64 < 32 else 1
    c["swap64"] = swap
    swap = np.zeros((P, P))
    for f in range(NOPE, MLA_QK):
        swap[(f + 16 if f < NOPE + 16 else f - 16), f] = -1 if f < NOPE + 16 else 1
    c["swap96"] = swap
    c["iota"] = np.broadcast_to(i, (P, P))
    query, key = np.arange(SEQ), np.arange(SEQ)
    c["sb_mask"] = key[:P, None] < query[None, :]
    causal = np.where(key[None, :] <= query[:, None], 0.0, NEG)
    c["mla_mask"] = np.concatenate([causal[:P, :P], causal[P:, :]], 1)
    span = query[:, None] - key[None, :]
    dil = [np.where((span >= 0) & (span <= w) & (span % d == 0), 0.0, NEG) for w, d in DIL]
    c["dil_mask0"] = np.concatenate([m[:P, :P] for m in dil], 1)
    c["dil_mask1"] = np.concatenate([m[P:, :] for m in dil], 1)
    f32 = np.float32
    for dim, rows, lo in ((HEAD, P, 0), (ROPE, MLA_QK, NOPE)):
        inv = f32(THETA) ** (-np.arange(0, dim, 2, dtype=f32) / f32(dim))
        col = np.zeros((P, 1), f32)
        for f in range(lo, rows):
            col[f, 0] = inv[(f - lo) % (dim // 2)]
        c["freq64" if dim == HEAD else "freq96"] = col
    c["first4"] = np.broadcast_to(np.arange(4, 0, -1), (P, 4))
    c["first16"] = np.broadcast_to(np.arange(16, 0, -1), (P, 16))
    c["minus_half"] = np.full((P, 4), -0.5)
    out = np.zeros((P, CONST_COLS), f32)
    for name, (lo, hi) in CONST.items():
        out[:, lo:hi] = c[name]
    return out


def rows_of_chunks(w):
    n = w.shape[-1]
    return w.reshape(-1, P, n).transpose(1, 0, 2).reshape(P, -1)


def unit_of(parts):
    out = np.zeros((P, UNIT), np.float32)
    out[:, :parts.shape[1]] = parts
    return out


def lay_out(inputs):
    mix = np.zeros((DEPTH, MIX_UNITS, P, UNIT), np.float32)
    moe = np.zeros((DEPTH, GROUPS, len(MOE), P, UNIT), np.float32)
    params = np.zeros((DEPTH, P, PARAM_COLS), np.float32)
    col = {}
    at = 0
    for name, n in (("sbq", 256), ("sbk", 256), ("sbv", 256), ("cq", 256), ("ckv", 128), ("kr", 32)):
        col[name] = (at, n)
        at += n
    for g in range(3):
        for c in "qkv":
            col[f"d{g}{c}"] = (at, 256)
            at += 256
    for i in range(12):
        col[f"gate{i}"] = (at, 256)
        at += 256
    for layer in range(DEPTH):
        w_in = inputs["w_in"][layer]
        for u, name in enumerate(MIX):
            if name == "kr":
                lo, n = col[name]
                padded = np.zeros((D_MODEL, MLA_QK), np.float32)
                padded[:, NOPE:] = w_in[:, lo:lo + n]
                part = rows_of_chunks(padded)
            elif name in col:
                lo, n = col[name]
                part = rows_of_chunks(w_in[:, lo:lo + n])
            elif name == "uq":
                part = rows_of_chunks(inputs["w_uq"][layer])
            elif name == "ukv":
                part = rows_of_chunks(inputs["w_ukv"][layer])
            elif name[:6] == "branch":
                part = rows_of_chunks(inputs["w_branch"][layer, int(name[6:])])
            else:
                i = int(name[3:])
                part = rows_of_chunks(inputs["w_out"][layer, 2 * i * P:(2 * i + 2) * P])
            mix[layer, u] = unit_of(part)
        for g in range(GROUPS):
            for u, name in enumerate(MOE):
                e = g * PER_GROUP + int(name[1])
                if name[0] == "D":
                    part = rows_of_chunks(inputs["w_down"][layer, e])
                else:
                    rows = slice(0, 512) if name[0] == "A" else slice(512, 1024)
                    part = rows_of_chunks(np.concatenate([inputs["w_gate"][layer, e, rows],
                                                          inputs["w_up"][layer, e, rows]], 1))
                moe[layer, g, u] = unit_of(part)
        by_name = {
            "g_mix": inputs["g_mix"][layer].reshape(CHUNKS, P).T, "g_ffn": inputs["g_ffn"][layer].reshape(CHUNKS, P).T,
            "g_q": inputs["g_q_lat"][layer].reshape(2, P).T, "g_kv": inputs["g_kv_lat"][layer].reshape(1, P).T,
            "router": rows_of_chunks(np.concatenate([inputs["w_group_router"][layer],
                                                     inputs["w_expert_router"][layer]], 1)),
            "bias": np.broadcast_to(np.concatenate([inputs["b_group_router"][layer],
                                                    inputs["b_expert_router"][layer]]), (P, 20)),
        }
        for name, (lo, hi) in PARAM.items():
            params[layer, :, lo:hi] = by_name[name]
    return mix, moe, params


def kernel(**inputs):
    import concourse.bacc as bacc
    from concourse import mybir
    from concourse.bass_utils import run_bass_kernel_spmd

    inputs = {name: np.ascontiguousarray(a) for name, a in inputs.items()}
    mix, moe, params = lay_out(inputs)
    arrays = {
        "x": inputs["x"][0], "positions": inputs["positions"], "mix_weights": mix, "moe_weights": moe,
        "params": params, "g_final": inputs["g_final"].reshape(1, D_MODEL), "constants": shape_constants(),
    }
    nc = bacc.Bacc("TRN2", target_bir_lowering=False, num_devices=1)
    args = [nc.dram_tensor(name, a.shape, mybir.dt.from_np(a.dtype), kind="ExternalInput").ap()
            for name, a in arrays.items()]
    out = nc.dram_tensor("out", (SEQ, D_MODEL), mybir.dt.float32, kind="ExternalOutput").ap()
    build(nc, *args, out)
    r = run_bass_kernel_spmd(nc, [arrays], core_ids=[0])
    return r.results[0]["out"].reshape(1, SEQ, D_MODEL)
```

```python
import numpy as np

D_MODEL = 1024
SEQ = 256
DEPTH = 2
HEAD = 64
THETA = 10000.0
EPS = 1e-6
NEG = -1e30
P = 128
TILES = SEQ // P
CHUNKS = D_MODEL // P
BRANCHES = 3
WIDTH = D_MODEL // 4
HEADS = WIDTH // HEAD
NOPE, ROPE = 64, 32
MLA_QK = NOPE + ROPE
GROUPS, PER_GROUP = 4, 4
EXPERTS = GROUPS * PER_GROUP
DIL = ((128, 1), (512, 4), (2048, 16))

UNIT = CHUNKS * WIDTH
RAW_SLOTS = 4
SPLIT_SLOTS = 3

MIX = ["sbq", "sbk", "cq", "ckv", "sbv", "kr", "d0q", "d0k", "d0v", "uq", "d1q", "ukv",
       "d1k", "d1v", "d2q", "d2k", "d2v"]
MIX += [f"gate{i}" for i in range(6)] + ["branch0"] + [f"gate{i}" for i in range(6, 12)]
MIX += ["branch1", "branch2"] + [f"out{i}" for i in range(4)]
FILL = {"ckv": CHUNKS * 128, "kr": CHUNKS * MLA_QK, "uq": 2 * HEADS * MLA_QK, "ukv": 512}
MIX_UNITS = len(MIX)
MOE = ["A0", "B0", "A1", "B1", "D0", "A2", "B2", "D1", "A3", "B3", "D2", "D3"]
DOWN_LOW = {"pool": [(0, 0), (0, 1), (2, 0)], "dve": [(1, 0), (1, 1), (2, 1)]}
MOE_SPLIT = [name for name in MOE if name[0] != "D"]
GROUP_UNITS = len(MOE_SPLIT)
MOE_UNITS = GROUPS * GROUP_UNITS
MOE_SLOTS = SPLIT_SLOTS + 1
DOWN_SLOTS = PER_GROUP
assert MIX_UNITS % RAW_SLOTS == MIX_UNITS % SPLIT_SLOTS == 0
assert GROUP_UNITS % RAW_SLOTS == GROUP_UNITS % MOE_SLOTS == 0

PJ = [(f"norm{c}", "dve") for c in range(4)]
PJ += [(n, "act") for n in ("sbq", "sbk", "cq", "ckv", "sbv", "kr", "d0q")]
PJ += [("sw_kr", "dve"), ("d0k", "act"), ("d0v", "act"), ("sw_d0q", "dve"), ("sw_d0k", "dve"),
       ("uq0", "act"), ("uq1", "act"), ("d1q", "act"), ("sw_mq0", "dve"), ("sw_mq1", "dve"),
       ("ukv0", "act"), ("ukv1", "act"), ("ukvv", "act"), ("d1k", "act"), ("sw_d1q", "dve"),
       ("d1v", "act"), ("d2q", "act"), ("sw_d1k", "dve"), ("d2k", "act"), ("sw_d2q", "dve"),
       ("d2v", "act"), ("sw_d2k", "dve")]
PJ += [(f"gate{i}", "act") for i in range(6)] + [(f"branch0_{j}", "dve") for j in range(4)]
PJ += [(f"gate{i}", "act") for i in range(6, 12)]
PJ += [(f"branch{n}_{j}", "dve") for n in (1, 2) for j in range(4)]
PJ += [(f"moe_norm{c}", "dve") for c in range(4)] + [("logits", "dve"), ("rank", "dve")]
PJ_INDEX = {name: i for i, (name, _) in enumerate(PJ)}
PJ_BANKS = 3
PJ_TOTAL = {who: sum(w == who for _, w in PJ) for who in ("act", "dve")}

LAST_FILL = [{"uq": "uq1", "ukv": "ukvv"}.get(name, f"{name}_3" if name[:6] == "branch" else name)
             for name in MIX[:-4]]

ROTATIONS = ["sw_kr", "sw_d0q", "sw_d0k", "sw_mq0", "sw_mq1", "sw_d1q", "sw_d1k", "sw_d2q", "sw_d2k"]

JOBS = [("mla", h, None) for h in range(HEADS)] + [("dil", h, b) for h in range(HEADS) for b in range(2)]

CONST = {}
_at = 0
for _name, _n in (("ident", 128), ("minus_half", 4), ("freq64", 1), ("freq96", 1), ("before", 128),
                  ("later", 128), ("ones", 128), ("swap64", 128), ("swap96", 128), ("iota", 128),
                  ("sb_mask", 256), ("mla_mask", 384), ("dil_mask0", 384), ("dil_mask1", 768),
                  ("first4", 4), ("first16", 16)):
    CONST[_name] = (_at, _at + _n)
    _at += _n
CONST_COLS = _at
FRONT_COLS = CONST["before"][0]
PARAM = {"g_mix": (0, 8), "g_ffn": (8, 16), "g_q": (16, 18), "g_kv": (18, 19), "router": (19, 179),
         "bias": (179, 199)}
PARAM_COLS = 199

DVE_LAYER_STEPS = 55
ACT_LAYER_STEPS = 2


def build(nc, x, positions, mix_weights, moe_weights, params, g_final, constants, out):
    import concourse.bass as bass
    from concourse import mybir
    from contextlib import ExitStack

    F32, F32R, I32 = mybir.dt.float32, mybir.dt.float32r, mybir.dt.int32
    ALU, ACT, AX = mybir.AluOpType, mybir.ActivationFunctionType, mybir.AxisListType

    cursor = [(nc.sbuf_base + 63) // 64 * 64]

    def place(name, shape, dtype=F32, at=None):
        size = 4 * int(np.prod(shape[1:]))
        if at is None:
            at = cursor[0]
            cursor[0] += (size + 31) // 32 * 32
        return nc.alloc_sbuf_tensor_at(name, shape, dtype, offset=at), at

    raw, _ = place("raw", [P, RAW_SLOTS, UNIT])
    w_hi, _ = place("w_hi", [P, SPLIT_SLOTS, UNIT], F32R)
    w_lo, _ = place("w_lo", [P, SPLIT_SLOTS, UNIT], F32R)
    xt, _ = place("xt", [P, TILES, D_MODEL])
    hn, hn_at = place("hn", [P, TILES, D_MODEL])
    o_hi, o_lo = [None] * 3, [None] * 3
    for n in (1, 2):
        o_hi[n], _ = place(f"o_hi{n}", [P, 2, SEQ], F32R, hn_at + (n - 1) * 4096)
        o_lo[n], _ = place(f"o_lo{n}", [P, 2, SEQ], F32R, hn_at + (n - 1) * 4096 + 2048)
    hTf, hTf_at = place("hTf", [P, CHUNKS, SEQ])
    lat, _ = place("lat", [P, 3, SEQ], F32, hTf_at)
    lat_sq, _ = place("lat_sq", [P, 3, SEQ], F32, hTf_at + 3072)
    lat_diag, _ = place("lat_diag", [P, 4, P], F32, hTf_at + 6144)
    xgf, _ = place("xgf", [P, CHUNKS, P], F32, hTf_at)
    norm_diag, _ = place("norm_diag", [P, TILES, P], F32, hTf_at + 6144)
    merged, _ = place("merged", [P, CHUNKS, SEQ], F32, hTf_at)
    hT_hi, hh_at = place("hT_hi", [P, CHUNKS, SEQ], F32R)
    hT_lo, hl_at = place("hT_lo", [P, CHUNKS, SEQ], F32R)
    m_hi, _ = place("m_hi", [P, CHUNKS, SEQ], F32R, hh_at)
    m_lo, _ = place("m_lo", [P, CHUNKS, SEQ], F32R, hl_at)
    xg_hi, _ = place("xg_hi", [P, CHUNKS, P], F32R, hh_at)
    xg_lo, _ = place("xg_lo", [P, CHUNKS, P], F32R, hh_at + 4096)
    y_hi, _ = place("y_hi", [P, D_MODEL], F32R, hl_at)
    y_lo, _ = place("y_lo", [P, D_MODEL], F32R, hl_at + 4096)
    cst, _ = place("cst", [P, CONST_COLS])
    all_params, _ = place("all_params", [P, DEPTH, PARAM_COLS])
    par, _ = place("par", [P, PARAM_COLS])
    gfin, _ = place("gfin", [P, D_MODEL])
    tables, _ = place("tables", [P, 4, SEQ])
    rope = {k: tables[:, i, :] for i, k in enumerate(("sin64", "sin96", "cos64", "cos96"))}
    exact_cst, _ = place("exact_cst", [P, 3, P], F32R)
    stat, _ = place("stat", [P, 64])
    rounds_f, _ = place("rounds_f", [1, 1])
    rounds, _ = place("rounds", [1, 1], I32)
    region = cursor[0]
    gates, gates_at = place("gates", [P, BRANCHES, CHUNKS, SEQ])
    sb_a, _ = place("sb_a", [P, 1536], F32, gates_at)
    sb_b, _ = place("sb_b", [P, 1536], F32, gates_at + 6144)
    sb_c, _ = place("sb_c", [P, 1536], F32, gates_at + 12288)
    lat_hi, _ = place("lat_hi", [P, 3, SEQ], F32R, gates_at + 18432)
    lat_lo, _ = place("lat_lo", [P, 3, SEQ], F32R, gates_at + 21504)
    dil_at = cursor[0]
    dq, dk, dv = ([place(f"d{g}{c}", [P, 2, SEQ])[0] for g in range(3)] for c in "qkv")
    mq, _ = place("mq", [P, HEADS, SEQ])
    mk, _ = place("mk", [P, HEADS, SEQ])
    mv, _ = place("mv", [P, TILES, WIDTH])
    o_hi[0], _ = place("o_hi0", [P, 2, SEQ], F32R)
    o_lo[0], _ = place("o_lo0", [P, 2, SEQ], F32R)
    sbq, sbq_at = place("sbq", [P, 2, SEQ])
    sbk, _ = place("sbk", [P, 2, SEQ])
    sbv, _ = place("sbv", [P, TILES, WIDTH])
    probs, _ = place("probs", [P, 2, 768], F32, sbq_at)
    pT, pT_at = place("pT", [P, 6, P])
    kr, _ = place("kr", [P, SEQ], F32, pT_at)
    rope_tmp = [place("rope_tmp0", [P, 2, SEQ], F32, pT_at + 1024)[0],
                place("rope_tmp1", [P, 2, SEQ], F32, hTf_at + 3072)[0]]
    pos_i, _ = place("pos_i", [P, SEQ], I32, dil_at)
    pos_f, _ = place("pos_f", [P, SEQ], F32, dil_at + 1024)
    turns, _ = place("turns", [P, 4, SEQ], F32, dil_at + 2048)
    full_turns, _ = place("full_turns", [P, 4, SEQ], F32, dil_at + 6144)
    end_mix = cursor[0]
    w_down, _ = place("w_down", [P, DOWN_SLOTS, UNIT], F32, dil_at)
    cursor[0] = region
    extra_hi, _ = place("extra_hi", [P, UNIT], F32R)
    extra_lo, _ = place("extra_lo", [P, UNIT], F32R)
    scomb, _ = place("scomb", [P, PER_GROUP])
    next_scomb, _ = place("next_scomb", [P, PER_GROUP])
    gcomb, _ = place("gcomb", [P, TILES, PER_GROUP])
    sel, _ = place("sel", [P, TILES, P])
    selT, _ = place("selT", [P, TILES, P], F32R)
    comb, _ = place("comb", [P, TILES, EXPERTS])
    slot_of, _ = place("slot_of", [P, TILES * GROUPS])
    logits, _ = place("logits", [P, TILES, GROUPS + EXPERTS])
    el, _ = place("el", [P, TILES, EXPERTS])
    r1, _ = place("r1", [P, TILES, EXPERTS])
    r2, _ = place("r2", [P, TILES, EXPERTS])
    hot1, _ = place("hot1", [P, TILES, EXPERTS])
    hot2, _ = place("hot2", [P, TILES, EXPERTS])
    ghot, _ = place("ghot", [P, TILES, GROUPS])
    g1, _ = place("g1", [P, TILES, GROUPS])
    th, _ = place("th", [P, 2, WIDTH])
    assert cursor[0] <= dil_at, (cursor[0], dil_at)
    cursor[0] = dil_at + 4 * DOWN_SLOTS * UNIT
    hid, _ = place("hid", [P, 2, WIDTH])
    hidT, _ = place("hidT", [P, 2, P])
    hidT_hi, _ = place("hidT_hi", [P, 2, P], F32R)
    hidT_lo, _ = place("hidT_lo", [P, 2, P], F32R)
    down_hi = [place("down_hi0", [P, D_MODEL], F32R)[0], place("down_hi1", [P, D_MODEL], F32R, hTf_at + 4096)[0]]
    down_lo, _ = place("down_lo", [P, DOWN_SLOTS, UNIT], F32R, dil_at)
    assert max(end_mix, cursor[0]) <= nc.sbuf_usable_end, (end_mix, cursor[0], nc.sbuf_usable_end)

    def const(name, rows=P):
        a, b = CONST[name]
        return cst[0:rows, a:b]

    def exact(name):
        return exact_cst[:, ("ident", "before", "ones").index(name), :]

    def param(name):
        a, b = PARAM[name]
        return par[:, a:b]

    ctx = ExitStack()
    with ctx:
        ps = ctx.enter_context(nc.psum_tensor("ps", [P, 8, 512], F32))

        def sem(name):
            return ctx.enter_context(nc.semaphore(name))

        OV = ps[:, 3, :]
        SC = ps[:, 4:6, :].rearrange("p b n -> p (b n)")
        TR = ps[:, 6:8, :].rearrange("p b n -> p (b n)")
        GU = [ps[:, 0, :], ps[:, 1, :]]
        HT = [ps[:, 2, 0:256], ps[:, 3, 0:256]]
        SELT, SCOMB = ps[:, 2, 256:512], ps[:, 3, 256:256 + PER_GROUP]

        TR2 = ps[:, 6:8, 0:256]

        def alone(eng, sem_, value):
            eng.wait_ge(sem_, value)
            eng.sem_inc(waits_carried, 1)

        def two(ap):
            return ap.rearrange("p (b n) -> p b n", b=2)

        def pj(name):
            return ps[:, PJ_INDEX[name] % PJ_BANKS, :]

        weights_landed = [sem(f"weights_landed{s}") for s in range(RAW_SLOTS)]
        x_landed = [sem(f"x_landed{t}") for t in range(TILES)]
        const_landed, params_landed = sem("const_landed"), sem("params_landed")
        front_landed = sem("front_landed")
        down_landed = [sem(f"down_landed{s}") for s in range(DOWN_SLOTS)]
        pos_landed, gfin_landed, out_stored = sem("pos_landed"), sem("gfin_landed"), sem("out_stored")
        split_hi, split_lo = sem("split_hi"), sem("split_lo")
        out_used, a_used, d_used = sem("out_used"), sem("a_used"), sem("d_used")
        pj_full, pj_act, pj_dve = sem("pj_full"), sem("pj_act"), sem("pj_dve")
        dve_chain, dve_gchain, dve_pchain = sem("dve_chain"), sem("dve_gchain"), sem("dve_pchain")
        act_chain = sem("act_chain")
        setup_chain, angles_chain = sem("setup_chain"), sem("angles_chain")
        angles_ready, tables_ready = sem("angles_ready"), sem("tables_ready")
        squares_ready, rstd_ready, hn_ready, pool_chain = (sem("squares_ready"), sem("rstd_ready"),
                                                           sem("hn_ready"), sem("pool_chain"))
        hT_hi_ready, hT_ready = sem("hT_hi_ready"), sem("hT_ready")
        z_full, softplus_ready, strict_ready, after_full = (sem("z_full"), sem("softplus_ready"),
                                                            sem("strict_ready"), sem("after_full"))
        logw_ready, wexp_ready, w_ready = sem("logw_ready"), sem("wexp_ready"), sem("w_ready")
        lat_sq_ready, lat_full, lat_var, lat_rstd = (sem("lat_sq_ready"), sem("lat_full"),
                                                     sem("lat_var"), sem("lat_rstd"))
        norm_diag_ready, stat_cleared = sem("norm_diag_ready"), sem("stat_cleared")
        diag_ready, lat_spread = sem("diag_ready"), sem("lat_spread")
        lat_normed, lat_hi_ready, lat_ready = sem("lat_normed"), sem("lat_hi_ready"), sem("lat_ready")
        kr_roped = sem("kr_roped")
        roped, rope_chain = sem("roped"), sem("rope_chain")
        sc_full, max_ready, exp_ready, probs_ready = (sem("sc_full"), sem("max_ready"),
                                                      sem("exp_ready"), sem("probs_ready"))
        tr_full, pT_ready = sem("tr_full"), sem("pT_ready")
        av_done = sem("av_done")
        ov_full, o_hi_ready, o_ready = sem("ov_full"), sem("o_hi_ready"), sem("o_ready")
        merged_done, m_hi_ready, m_ready = sem("merged_done"), sem("m_hi_ready"), sem("m_ready")
        pair_merged = sem("pair_merged")
        mix_half_full, mix_full, x_mixed = sem("mix_half_full"), sem("mix_full"), sem("x_mixed")
        route_max, route_exp, ghot_ready, routed = (sem("route_max"), sem("route_exp"),
                                                    sem("ghot_ready"), sem("routed"))
        gcomb_ready, scomb_full, scomb_ready = sem("gcomb_ready"), sem("scomb_full"), sem("scomb_ready")
        next_scomb_ready = sem("next_scomb_ready")
        sel_ready, gather_full, selT_ready, xgf_ready = (sem("sel_ready"), sem("gather_full"),
                                                         sem("selT_ready"), sem("xgf_ready"))
        xg_hi_ready, xg_ready = sem("xg_hi_ready"), sem("xg_ready")
        gu_full, th_ready, hid_ready, ht_full = sem("gu_full"), sem("th_ready"), sem("hid_ready"), sem("ht_full")
        hidT_hi_ready, hidT_lo_ready, hidT_ready = sem("hidT_hi_ready"), sem("hidT_lo_ready"), sem("hidT_ready")
        down_hi_ready, pool_down_ready, dve_down_ready = (sem("down_hi_ready"), sem("pool_down_ready"),
                                                          sem("dve_down_ready"))
        y_half_full, x_moe_first = sem("y_half_full"), sem("x_moe_first")
        y_full, y_hi_ready, y_ready, scatter_full, x_moe = (sem("y_full"), sem("y_hi_ready"), sem("y_ready"),
                                                            sem("scatter_full"), sem("x_moe"))
        out_ready, waits_carried = sem("out_ready"), sem("waits_carried")

        block = ctx.enter_context(nc.Block())

        def slot_width(n):
            return FILL.get(MIX[n], UNIT) if n < MIX_UNITS else UNIT

        def pj_emptied(name):
            i = PJ_INDEX[name]
            who = PJ[i][1]
            return who, sum(w == who for _, w in PJ[:i + 1])

        def moe_slot(v):
            slot = v % MOE_SLOTS
            return (extra_hi[:, :], extra_lo[:, :]) if slot == SPLIT_SLOTS else (w_hi[:, slot, :], w_lo[:, slot, :])

        def spans(h, b, kind):
            if kind == "mla":
                return [(0, 0, 128, None), (1, 128, 256, None)]
            w = 128 * (b + 1)
            return [(b, g * w, w, g) for g in range(3)]

        @block.sync
        def _(sp):
            def load(n, slot, src, width):
                sp.wait_ge(split_lo, n + 1)
                sp.dma_start(raw[:, slot, 0:width], src).then_inc(weights_landed[slot], 16)

            def load_down(e, src, q=None):
                if q is None:
                    sp.wait_ge(ov_full, (layer + 1) * BRANCHES)
                elif e == 3:
                    sp.wait_ge(y_full, q)
                else:
                    sp.wait_ge(d_used, q * 3 + e - 2)
                sp.dma_start(w_down[:, e, :], src).then_inc(down_landed[e], 16)

            def load_group(base, src, q=None):
                for u, name in enumerate(MOE):
                    if name[0] == "D":
                        load_down(int(name[1]), src(u), q)
                    else:
                        v = MOE_SPLIT.index(name)
                        load(base + v, v % RAW_SLOTS, src(u), UNIT)

            for t in range(TILES):
                sp.dma_start(xt[:, t, :], x[t * P:(t + 1) * P, :]).then_inc(x_landed[t], 16)
            sp.sem_inc(split_lo, RAW_SLOTS)
            with sp.Fori(0, DEPTH) as layer:
                alone(sp, routed, layer + 1)
                before = sp.value_load(rounds[0:1, 0:1], min_val=0, max_val=2 * DEPTH)
                first = sp.snap(layer * MIX_UNITS + before * MOE_UNITS)
                for u in range(MIX_UNITS):
                    load(first + u, u % RAW_SLOTS, mix_weights[layer, u, :, 0:slot_width(u)], slot_width(u))
                first = sp.snap((layer + 1) * MIX_UNITS + before * MOE_UNITS)
                load_group(first, lambda u: moe_weights[layer, 0, u])
                with sp.Fori(1, GROUPS) as g:
                    load_group(sp.snap(first + g * GROUP_UNITS), lambda u: moe_weights[layer, g, u],
                               sp.snap(before * GROUPS + g))
                alone(sp, routed, layer + 2)
                end = sp.value_load(rounds[0:1, 0:1], min_val=0, max_val=2 * DEPTH)
                with sp.If(end - before - 1):
                    with sp.Fori(0, GROUPS) as g:
                        load_group(sp.snap(first + MOE_UNITS + g * GROUP_UNITS), lambda u: moe_weights[layer, g, u],
                                   sp.snap((before + 1) * GROUPS + g))
            end = sp.value_load(rounds[0:1, 0:1], min_val=0, max_val=2 * DEPTH)
            last = sp.snap(DEPTH * MIX_UNITS + end * MOE_UNITS)
            for u in range(SPLIT_SLOTS):
                load(last + u, u, mix_weights[0, u, :, 0:16], 16)
            for t in range(TILES):
                sp.wait_ge(out_ready, t + 1)
                sp.dma_start(out[t * P:(t + 1) * P, :], hn[:, t, :]).then_inc(out_stored, 16)
            sp.wait_ge(out_stored, 16 * TILES)
            for s in range(RAW_SLOTS):
                sp.wait_ge(weights_landed[s], 16)

        @block.scalar
        def _(act):
            def split(u, width=UNIT, hi=None):
                slot = u % RAW_SLOTS
                hi = w_hi[:, u % SPLIT_SLOTS, :] if hi is None else hi
                act.wait_ge(weights_landed[slot], 16 * (landed + u // RAW_SLOTS + 1))
                act.activation(hi[:, 0:width], raw[:, slot, 0:width], ACT.Copy).then_inc(split_hi, 1)

            act.dma_start(cst[:, 0:FRONT_COLS], constants[:, 0:FRONT_COLS]).then_inc(front_landed, 16)
            act.dma_start(pos_i[:, :], positions.broadcast_to([P, SEQ])).then_inc(pos_landed, 16)
            act.dma_start(all_params[:, :, :], params.rearrange("l p n -> p l n")).then_inc(params_landed, 16)
            act.dma_start(cst[:, FRONT_COLS:], constants[:, FRONT_COLS:]).then_inc(const_landed, 16)
            act.dma_start(gfin[:, :], g_final.broadcast_to([P, D_MODEL])).then_inc(gfin_landed, 16)

            def squares(mixed=None, final=None, start=False):
                for t in range(TILES):
                    if start:
                        act.wait_ge(x_landed[t], 16)
                    if mixed is not None:
                        act.wait_ge(x_mixed, mixed + t)
                    if final is not None:
                        act.wait_ge((x_moe_first, x_moe)[t], final + t)
                    act.activation(hn[:, t, :], xt[:, t, :], ACT.Square,
                                   accum_out=stat[:, t:t + 1]).then_inc(squares_ready, 1)

            act.wait_ge(stat_cleared, 1)
            act.activation(stat[:, 6:7], stat[:, 6:7], ACT.Square)
            act.sem_inc(x_moe, 1)
            squares(start=True)
            with act.Fori(0, DEPTH) as layer:
                alone(act, routed, layer + 1)
                before = act.value_load(rounds[0:1, 0:1], min_val=0, max_val=2 * DEPTH)
                landed = act.snap(layer * (MIX_UNITS // RAW_SLOTS) + before * (MOE_UNITS // RAW_SLOTS))

                def full(name):
                    act.wait_ge(pj_full, layer * len(PJ) + PJ_INDEX[name] + 1)

                def after(u):
                    if u < MIX_UNITS - 4:
                        full(LAST_FILL[u])
                    elif u < MIX_UNITS - 1:
                        act.wait_ge(out_used, layer * 3 + u - (MIX_UNITS - 4) + 1)
                    else:
                        act.wait_ge(mix_full, layer + 1)
                    split(u + SPLIT_SLOTS, slot_width(u + SPLIT_SLOTS))

                def copy(name, dst, src=None):
                    full(name)
                    act.activation(dst, pj(name) if src is None else src, ACT.Copy).then_inc(pj_act, 1)

                with act.If(1 - layer):
                    split(0)
                for c in range(4):
                    act.wait_ge(pj_dve, layer * PJ_TOTAL["dve"] + c + 1)
                    act.activation(hT_hi[:, 2 * c:2 * c + 2, :], hTf[:, 2 * c:2 * c + 2, :],
                                   ACT.Copy).then_inc(hT_hi_ready, 1)
                with act.If(1 - layer):
                    for u in range(1, SPLIT_SLOTS):
                        split(u)
                after(0)
                copy("sbq", sbq[:, :, :])
                after(1)
                copy("sbk", sbk[:, :, :])
                after(2)
                full("cq")
                act.activation(lat_sq[:, 0:2, :], pj("cq"), ACT.Square)
                copy("cq", lat[:, 0:2, :])
                act.wait_ge(z_full, layer + 1)
                act.activation(sb_a[:, 0:1024], SC[:, :], ACT.Abs, scale=HEAD ** -0.5)
                act.activation(two(sb_a[:, 1024:1536]), TR2, ACT.Abs, scale=HEAD ** -0.5).then_inc(act_chain, 1)
                after(3)
                act.activation(lat_sq[:, 2, :], pj("ckv")[:, 0:SEQ], ACT.Square).then_inc(lat_sq_ready, 1)
                copy("ckv", lat[:, 2, :], pj("ckv")[:, 0:SEQ])
                act.wait_ge(act_chain, layer * ACT_LAYER_STEPS + 1)
                act.activation(sb_a[:, :], sb_a[:, :], ACT.Exp, scale=-1.0).then_inc(act_chain, 1)
                act.wait_ge(act_chain, layer * ACT_LAYER_STEPS + 2)
                act.activation(sb_a[:, :], sb_a[:, :], ACT.Ln, bias=1.0).then_inc(softplus_ready, 1)
                after(4)
                copy("sbv", sbv[:, :, :])
                after(5)
                with act.If(1 - layer):
                    act.wait_ge(front_landed, 16)
                    act.wait_ge(const_landed, 16)
                    for name in ("ident", "before", "ones"):
                        act.activation(exact(name), const(name), ACT.Copy)
                    act.wait_ge(angles_ready, 1)
                    act.activation(tables[:, :, :], tables[:, :, :], ACT.Sin).then_inc(tables_ready, 1)
                copy("kr", kr[0:MLA_QK, :], pj("kr")[0:MLA_QK, 0:SEQ])
                after(6)
                copy("d0q", dq[0][:, :, :])
                after(7)
                copy("d0k", dk[0][:, :, :])
                act.wait_ge(lat_normed, layer + 1)
                act.activation(lat_hi[:, :, :], lat[:, :, :], ACT.Copy).then_inc(lat_hi_ready, 1)
                act.wait_ge(logw_ready, layer + 1)
                act.activation(sb_b[:, :], sb_b[:, :], ACT.Exp).then_inc(wexp_ready, 1)
                after(8)
                copy("d0v", dv[0][:, :, :])
                after(9)
                for i in range(2):
                    copy(f"uq{i}", mq[0:MLA_QK, 2 * i:2 * i + 2, :], pj(f"uq{i}")[0:MLA_QK, :])
                after(10)
                copy("d1q", dq[1][:, :, :])
                act.wait_ge(ov_full, layer * BRANCHES + 1)
                act.activation(o_hi[0][:, :, :], OV, ACT.Copy).then_inc(o_hi_ready, 1)
                for i in range(2):
                    copy(f"ukv{i}", mk[0:NOPE, 2 * i:2 * i + 2, :], pj(f"ukv{i}")[0:NOPE, :])
                copy("ukvv", mv[:, :, :])
                after(11)
                for u, name, dst in ((12, "d1k", dk[1]), (13, "d1v", dv[1]),
                                     (14, "d2q", dq[2]), (15, "d2k", dk[2]), (16, "d2v", dv[2])):
                    after(u)
                    copy(name, dst[:, :, :])

                def exps(j):
                    kind, h, b = JOBS[j]
                    act.wait_ge(max_ready, layer * len(JOBS) + j + 1)
                    rows = ((0, 128), (128, 384)) if kind == "mla" else ((0, 384 * (b + 1)),)
                    for i, (lo, hi) in enumerate(rows):
                        ins = act.activation(probs[:, j % 2, lo:hi], probs[:, j % 2, lo:hi], ACT.Exp,
                                             bias=stat[:, 8 + 4 * (j % 2) + i:9 + 4 * (j % 2) + i],
                                             accum_out=stat[:, 16 + 4 * (j % 2) + i:17 + 4 * (j % 2) + i])
                    ins.then_inc(exp_ready, 1)

                def out_of_transposes(j):
                    kind, h, b = JOBS[j]
                    n = 6 if b == 1 else 3
                    act.wait_ge(tr_full, layer * len(JOBS) + j + 1)
                    if j == 0:
                        act.wait_ge(roped, (layer + 1) * len(ROTATIONS))
                    elif j == HEADS:
                        act.wait_ge(ov_full, layer * BRANCHES + 2)
                    elif j >= 1:
                        act.wait_ge(av_done, layer * (len(JOBS) - 2) + j - (j > HEADS))
                    act.activation(pT[:, 0:n, :], TR[:, 0:128 * n], ACT.Copy).then_inc(pT_ready, 1)

                exps(0)
                for i in range(12):
                    if i == 5:
                        act.wait_ge(ov_full, layer * BRANCHES + 2)
                        act.activation(o_hi[1][:, :, :], OV, ACT.Copy).then_inc(o_hi_ready, 1)
                    after(MIX.index(f"gate{i}"))
                    act.activation(gates[:, i // 4, 2 * (i % 4):2 * (i % 4) + 2, :], pj(f"gate{i}"), ACT.Tanh,
                                   scale=0.5).then_inc(pj_act, 1)
                    if i < 11:
                        exps(i + 1)
                    out_of_transposes(i)
                    if i == 5:
                        after(MIX.index("branch0"))
                act.wait_ge(ov_full, layer * BRANCHES + 3)
                act.activation(o_hi[2][:, :, :], OV, ACT.Copy).then_inc(o_hi_ready, 1)
                after(MIX.index("branch1"))
                for j in range(4):
                    act.wait_ge(merged_done, layer * 4 + j + 1)
                    act.activation(m_hi[:, 2 * j:2 * j + 2, :], merged[:, 2 * j:2 * j + 2, :], ACT.Copy,
                                   scale=0.5).then_inc(m_hi_ready, 1)
                for u in range(31, 35):
                    after(u)

                squares(mixed=layer * TILES + 1)
                after(MIX_UNITS - 1)

                def route_exponentials():
                    act.wait_ge(route_max, layer + 1)
                    act.activation(g1[:, :, :], g1[:, :, :], ACT.Exp)
                    act.activation(stat[:, 36:38], stat[:, 36:38], ACT.Exp).then_inc(route_exp, 1)

                def gathered_high(q):
                    for i in range(2):
                        act.wait_ge(xgf_ready, 2 * q + i + 1)
                        act.activation(xg_hi[:, 4 * i:4 * i + 4, :], xgf[:, 4 * i:4 * i + 4, :],
                                       ACT.Copy).then_inc(xg_hi_ready, 1)

                def ahead(q, v):
                    n = v + SPLIT_SLOTS
                    landed = act.snap((layer + 1) * (MIX_UNITS // RAW_SLOTS) + q * (GROUP_UNITS // RAW_SLOTS))
                    act.wait_ge(weights_landed[n % RAW_SLOTS], 16 * (landed + n // RAW_SLOTS + 1))
                    act.activation(moe_slot(n)[0], raw[:, n % RAW_SLOTS, :], ACT.Copy).then_inc(split_hi, 1)

                def group(r, g, last):
                    q = act.snap(r * GROUPS + g)

                    def tanh(e):
                        act.wait_ge(gu_full, q * PER_GROUP + e + 1)
                        act.activation(th[:, e % 2, :], GU[e % 2][:, 0:WIDTH], ACT.Tanh,
                                       scale=0.5).then_inc(th_ready, 1)

                    def transposed_hidden(e):
                        act.wait_ge(ht_full, q * PER_GROUP + e + 1)
                        if e < 3:
                            act.activation(hidT_hi[:, :, :], HT[e % 2], ACT.Copy).then_inc(hidT_hi_ready, 1)
                        else:
                            act.activation(hidT[:, :, :], HT[1], ACT.Copy).then_inc(hidT_ready, 1)

                    def high_down(e):
                        act.wait_ge(down_landed[e], 16 * (q + 1))
                        for f in range(2):
                            act.activation(down_hi[f][:, :], w_down[:, e, f * D_MODEL:(f + 1) * D_MODEL],
                                           ACT.Copy).then_inc(down_hi_ready, 1)

                    high_down(0)
                    tanh(0)
                    act.activation(selT[:, :, :], SELT, ACT.Copy).then_inc(selT_ready, 1)
                    ahead(q, 1)
                    transposed_hidden(0)
                    ahead(q, 2)
                    act.wait_ge(a_used, q * PER_GROUP + 2)
                    ahead(q, 3)
                    tanh(1)
                    act.wait_ge(d_used, 3 * q + 1)
                    high_down(1)
                    act.wait_ge(a_used, q * PER_GROUP + 3)
                    transposed_hidden(1)
                    ahead(q, 4)
                    ahead(q, 5)
                    tanh(2)
                    ahead(q, 6)
                    act.wait_ge(d_used, 3 * q + 2)
                    high_down(2)
                    act.wait_ge(a_used, q * PER_GROUP + 4)
                    transposed_hidden(2)
                    ahead(q, 7)
                    tanh(3)
                    if not last:
                        gathered_high(q + 1)
                    transposed_hidden(PER_GROUP - 1)
                    if not last:
                        ahead(q, GROUP_UNITS)
                    for n, full_ in enumerate((y_half_full, y_full)):
                        act.wait_ge(full_, q + 1)
                        cols = slice(n * 512, (n + 1) * 512)
                        act.activation(y_hi[:, cols], SC[:, cols], ACT.Copy).then_inc(y_hi_ready, 1)

                def one_pass(r, first_of_layer=False):
                    gathered_high(r * GROUPS)
                    if first_of_layer:
                        route_exponentials()
                    ahead(act.snap(r * GROUPS), 0)
                    with act.Fori(0, GROUPS - 1) as g:
                        group(r, g, False)
                    group(r, GROUPS - 1, True)

                one_pass(before, True)
                alone(act, routed, layer + 2)
                end = act.value_load(rounds[0:1, 0:1], min_val=0, max_val=2 * DEPTH)
                with act.If(end - before - 1):
                    one_pass(act.snap(before + 1))
                squares(final=end * GROUPS)

        @block.gpsimd
        def _(pool):
            def rsqrt(out_, in_, exponent):
                return pool.tensor_tensor(out_, in_, exponent, ALU.pow)

            def norm_rstd(n):
                alone(pool, squares_ready, TILES * (n + 1))
                pool.tensor_scalar(stat[:, 2:4], stat[:, 0:2], 1.0 / D_MODEL, EPS, ALU.mult,
                                   ALU.add).then_inc(pool_chain, 1)
                pool.wait_ge(pool_chain, n + 1)
                rsqrt(stat[:, 4:6], stat[:, 2:4], const("minus_half")[:, 0:2]).then_inc(rstd_ready, 1)

            angle_steps = [0]

            def step(ins):
                angle_steps[0] += 1
                ins.then_inc(angles_chain, 1)
                pool.wait_ge(angles_chain, angle_steps[0])

            pool.wait_ge(front_landed, 16)
            norm_rstd(0)
            pool.wait_ge(pos_landed, 16)
            step(pool.tensor_copy(pos_f[:, :], pos_i[:, :]))
            for i, freq in enumerate(("freq64", "freq96", "freq64", "freq96")):
                ins = pool.tensor_scalar(tables[:, i, :], pos_f[:, :], const(freq), None, ALU.mult)
            step(ins)
            two_pi = 2 * np.pi
            for half, lead in ((slice(0, 2), 0.0), (slice(2, 4), 0.25)):
                ins = pool.tensor_scalar(turns[:, half, :], tables[:, half, :], 1.0 / two_pi, lead, ALU.mult, ALU.add)
            step(ins)
            step(pool.tensor_scalar(turns[:, :, :], turns[:, :, :], 12582912.0, None, ALU.add))
            step(pool.tensor_scalar(turns[:, :, :], turns[:, :, :], 12582912.0, None, ALU.subtract))
            parts = [6.25, 0.033203125]
            parts.append(float(np.float32(two_pi - sum(parts))))
            for part in parts:
                step(pool.tensor_scalar(full_turns[:, :, :], turns[:, :, :], part, None, ALU.mult))
                step(pool.tensor_tensor(tables[:, :, :], tables[:, :, :], full_turns[:, :, :], ALU.subtract))
            step(pool.tensor_scalar(tables[:, 2:4, :], tables[:, 2:4, :], 0.25 * two_pi, None, ALU.add))
            pool.tensor_scalar(tables[:, :, :], tables[:, :, :], 3.1415925, -3.1415925, ALU.min,
                               ALU.max).then_inc(angles_ready, 1)
            with pool.Fori(0, DEPTH) as layer:
                alone(pool, routed, layer + 1)
                before = pool.value_load(rounds[0:1, 0:1], min_val=0, max_val=2 * DEPTH)

                def rotate(name, dst, use, rows, cos):
                    i = ROTATIONS.index(name)
                    if i == 1:
                        alone(pool, roped, layer * len(ROTATIONS) + 1)
                    alone(pool, pj_act, layer * PJ_TOTAL["act"] + pj_emptied(use)[1])
                    alone(pool, tables_ready, 1)
                    h = dst.shape[1]
                    table = rope[cos][rows, :].unsqueeze(1).broadcast_to([dst.shape[0], h, SEQ])
                    alone(pool, pj_dve, layer * PJ_TOTAL["dve"] + pj_emptied(name)[1])
                    pool.tensor_tensor(dst, dst, table, ALU.mult).then_inc(rope_chain, 1)
                    alone(pool, rope_chain, layer * len(ROTATIONS) + i + 1)
                    return pool.tensor_tensor(dst, dst, rope_tmp[i % 2][rows, 0:h, :], ALU.add)

                pool.wait_ge(lat_var, layer + 1)
                rsqrt(stat[:, 60:64], stat[:, 56:60], const("minus_half")).then_inc(lat_rstd, 1)
                rows = slice(0, MLA_QK)
                rotate("sw_kr", kr[rows, :].unsqueeze(1), "kr", rows, "cos96").then_inc(kr_roped, 1)
                alone(pool, kr_roped, layer + 1)
                pool.tensor_copy(mk[NOPE:MLA_QK, :, :],
                                 kr[NOPE:MLA_QK, :].unsqueeze(1).broadcast_to([ROPE, HEADS, SEQ])).then_inc(roped, 1)
                for name, dst in (("d0q", dq[0]), ("d0k", dk[0])):
                    rotate(f"sw_{name}", dst[:, :, :], name, slice(0, P), "cos64").then_inc(roped, 1)
                for i in range(2):
                    rotate(f"sw_mq{i}", mq[rows, 2 * i:2 * i + 2, :], f"uq{i}", rows, "cos96").then_inc(roped, 1)
                for name, dst in (("d1q", dq[1]), ("d1k", dk[1]), ("d2q", dq[2]), ("d2k", dk[2])):
                    rotate(f"sw_{name}", dst[:, :, :], name, slice(0, P), "cos64").then_inc(roped, 1)
                for j in range(4):
                    alone(pool, pj_dve, layer * PJ_TOTAL["dve"] + pj_emptied(f"branch1_{j}")[1])
                    m = merged[:, 2 * j:2 * j + 2, :]
                    pool.tensor_tensor(m, m, gates[:, 1, 2 * j:2 * j + 2, :], ALU.add).then_inc(pair_merged, 1)
                norm_rstd(layer * 2 + 1)

                def low_downs(r):
                    with pool.Fori(0, GROUPS) as g:
                        q = pool.snap(r * GROUPS + g)
                        for e, f in DOWN_LOW["pool"]:
                            alone(pool, down_hi_ready, 6 * q + 2 * e + f + 1)
                            cols = slice(f * D_MODEL, (f + 1) * D_MODEL)
                            pool.tensor_tensor(down_lo[:, e, cols], w_down[:, e, cols], down_hi[f][:, :].bitcast(F32),
                                               ALU.subtract).then_inc(pool_down_ready, 1)

                low_downs(before)
                alone(pool, routed, layer + 2)
                end = pool.value_load(rounds[0:1, 0:1], min_val=0, max_val=2 * DEPTH)
                with pool.If(end - before - 1):
                    low_downs(pool.snap(before + 1))
                norm_rstd(layer * 2 + 2)

        @block.vector
        def _(dve):
            steps = {"layer": 0}

            def link(ins, base):
                steps["layer"] += 1
                ins.then_inc(dve_chain, 1)
                dve.wait_ge(dve_chain, base + steps["layer"])

            setup = [0]

            def slink(ins):
                setup[0] += 1
                ins.then_inc(setup_chain, 1)
                dve.wait_ge(setup_chain, setup[0])

            def split(n, u, width=UNIT, slots=None):
                dve.wait_ge(split_hi, n + 1)
                hi, lo = slots or (w_hi[:, u % SPLIT_SLOTS, :], w_lo[:, u % SPLIT_SLOTS, :])
                dve.tensor_tensor(lo[:, 0:width], raw[:, u % RAW_SLOTS, 0:width],
                                  hi[:, 0:width].bitcast(F32), ALU.subtract).then_inc(split_lo, 1)

            dve.memset(stat[:, :], 1.0).then_inc(stat_cleared, 1)
            slink(dve.memset(rounds_f[:, :], 0.0))
            dve.tensor_copy(rounds[:, :], rounds_f[:, :]).then_inc(routed, 1)
            dve.wait_ge(params_landed, 16)
            for t in range(TILES):
                dve.wait_ge(x_landed[t], 16)

            def normed(n):
                dve.wait_ge(rstd_ready, n + 1)
                for t in range(TILES):
                    ins = dve.tensor_scalar(hn[:, t, :], xt[:, t, :], stat[:, 4 + t:5 + t], None, ALU.mult)
                return ins

            with dve.Fori(0, DEPTH) as layer:
                steps["layer"] = 0
                alone(dve, routed, layer + 1)
                before = dve.value_load(rounds[0:1, 0:1], min_val=0, max_val=2 * DEPTH)
                first = dve.snap(layer * MIX_UNITS + before * MOE_UNITS)
                base = dve.snap(layer * DVE_LAYER_STEPS)

                def chain(ins):
                    link(ins, base)

                def full(name):
                    dve.wait_ge(pj_full, layer * len(PJ) + PJ_INDEX[name] + 1)

                def after(u):
                    split(first + u + SPLIT_SLOTS, u + SPLIT_SLOTS, slot_width(u + SPLIT_SLOTS))

                def scaled_transposes(prefix, gain, c):
                    full(f"{prefix}{c}")
                    g = param(gain)[:, 2 * c:2 * c + 2].unsqueeze(2).broadcast_to([P, 2, SEQ])
                    dve.tensor_tensor(hTf[:, 2 * c:2 * c + 2, :],
                                      pj(f"{prefix}{c}").rearrange("p (c t) -> p c t", c=2), g,
                                      ALU.mult).then_inc(pj_dve, 1)

                def rotate(name, rows, width, sin):
                    full(name)
                    dve.wait_ge(tables_ready, 1)
                    i = ROTATIONS.index(name)
                    if i >= 2:
                        dve.wait_ge(roped, layer * len(ROTATIONS) + i - 1)
                    h = width // SEQ
                    swapped = pj(name)[rows, 0:width].rearrange("p (h t) -> p h t", t=SEQ)
                    table = rope[sin][rows, :].unsqueeze(1).broadcast_to([rows.stop - rows.start, h, SEQ])
                    dve.tensor_tensor(rope_tmp[i % 2][rows, 0:h, :], swapped, table, ALU.mult).then_inc(pj_dve, 1)

                dve.wait_ge(rstd_ready, layer * 2 + 1)
                for t in range(TILES):
                    ins = dve.tensor_scalar(norm_diag[:, t, :], const("ident"), stat[:, 4 + t:5 + t], None, ALU.mult)
                ins.then_inc(norm_diag_ready, 1)
                chain(dve.tensor_copy(par[:, :], all_params[:, layer, :]))

                def low_hT(c):
                    dve.wait_ge(hT_hi_ready, layer * 4 + c + 1)
                    dve.tensor_tensor(hT_lo[:, 2 * c:2 * c + 2, :], hTf[:, 2 * c:2 * c + 2, :],
                                      hT_hi[:, 2 * c:2 * c + 2, :].bitcast(F32), ALU.subtract).then_inc(hT_ready, 1)

                for c in range(4):
                    scaled_transposes("norm", "g_mix", c)
                    if c == 1:
                        with dve.If(1 - layer):
                            split(0, 0)
                            dve.wait_ge(const_landed, 16)
                    if c >= 1:
                        low_hT(c - 1)
                low_hT(3)
                with dve.If(1 - layer):
                    for u in range(1, SPLIT_SLOTS):
                        split(u, u)
                for u in range(3):
                    after(u)
                scale = HEAD ** -0.5
                blocks = ((ps[:, 4:6, :], 0, 1024, 256), (TR2, 1024, 1536, 128))
                dve.wait_ge(z_full, layer + 1)
                dve.wait_ge(act_chain, layer * ACT_LAYER_STEPS + 1)
                for z, lo, hi, _ in blocks:
                    ins = dve.tensor_scalar(two(sb_b[:, lo:hi]), z, scale, 0.0, ALU.mult, ALU.min)
                chain(ins)
                after(3)
                dve.wait_ge(softplus_ready, layer + 1)
                chain(dve.tensor_tensor(sb_b[:, :], sb_b[:, :], sb_a[:, :], ALU.subtract))
                after(4)
                for z, lo, hi, _ in blocks:
                    ins = dve.scalar_tensor_tensor(out=two(sb_c[:, lo:hi]), in0=z, scalar=-scale, in1=two(sb_b[:, lo:hi]),
                                                   op0=ALU.mult, op1=ALU.add)
                chain(ins)

                def strict(buf, lo, hi, w):
                    view = buf[:, lo:hi].rearrange("p (h t) -> p h t", t=w)
                    mask = const("sb_mask")[:, 0:w].unsqueeze(1).broadcast_to([P, HEADS, w])
                    return dve.tensor_tensor(view, view, mask, ALU.mult)

                for z, lo, hi, w in blocks:
                    ins = strict(sb_c, lo, hi, w)
                ins.then_inc(strict_ready, 1)
                after(5)
                dve.wait_ge(lat_full, layer + 1)
                dve.tensor_scalar(stat[:, 56:58], OV[:, 0:2], 1.0 / WIDTH, EPS, ALU.mult, ALU.add)
                dve.tensor_scalar(stat[:, 58:60], OV[:, 2:4], 1.0 / P, EPS, ALU.mult,
                                  ALU.add).then_inc(lat_var, 1)
                after(6)
                dve.wait_ge(lat_rstd, layer + 1)
                for i in range(4):
                    ins = dve.tensor_scalar(lat_diag[:, i, :], const("ident"), stat[:, 60 + i:61 + i], None, ALU.mult)
                ins.then_inc(diag_ready, 1)
                rotate("sw_kr", slice(0, MLA_QK), SEQ, "sin96")
                dve.wait_ge(lat_spread, layer + 1)
                for c in range(3):
                    gain = param("g_q")[:, c:c + 1] if c < 2 else param("g_kv")
                    ins = dve.scalar_tensor_tensor(out=lat[:, c, :], in0=lat[:, c, :], scalar=gain,
                                                   in1=OV[:, (c // 2) * SEQ:(c // 2 + 1) * SEQ], op0=ALU.mult, op1=ALU.mult)
                ins.then_inc(lat_normed, 1)
                dve.wait_ge(lat_hi_ready, layer + 1)
                dve.tensor_tensor(lat_lo[:, :, :], lat[:, :, :], lat_hi[:, :, :].bitcast(F32),
                                  ALU.subtract).then_inc(lat_ready, 1)
                after(7)
                dve.wait_ge(after_full, layer + 1)
                for z, lo, hi, _ in blocks:
                    ins = dve.tensor_tensor(two(sb_b[:, lo:hi]), z, two(sb_b[:, lo:hi]), ALU.add)
                ins.then_inc(logw_ready, 1)
                after(8)
                rows = slice(0, P)
                rotate("sw_d0q", rows, 512, "sin64")
                dve.wait_ge(wexp_ready, layer + 1)
                for z, lo, hi, w in blocks:
                    ins = strict(sb_b, lo, hi, w)
                ins.then_inc(w_ready, 1)
                rotate("sw_d0k", rows, 512, "sin64")
                after(9)

                def low_o(n):
                    dve.wait_ge(o_hi_ready, layer * BRANCHES + n + 1)
                    dve.tensor_tensor(o_lo[n][:, :, :], OV.rearrange("p (c t) -> p c t", c=2),
                                      o_hi[n][:, :, :].bitcast(F32), ALU.subtract).then_inc(o_ready, 1)

                rows = slice(0, MLA_QK)
                low_o(0)
                for i in range(2):
                    rotate(f"sw_mq{i}", rows, 512, "sin96")
                after(10)
                after(11)
                rows = slice(0, P)
                after(12)
                rotate("sw_d1q", rows, 512, "sin64")
                after(13)
                after(14)
                rotate("sw_d1k", rows, 512, "sin64")
                after(15)
                rotate("sw_d2q", rows, 512, "sin64")
                after(16)
                rotate("sw_d2k", rows, 512, "sin64")

                def masked(j):
                    kind, h, b = JOBS[j]
                    dve.wait_ge(sc_full, layer * len(JOBS) + j + 1)
                    w = 768 if b == 1 else 384
                    mask = const("mla_mask" if kind == "mla" else f"dil_mask{b}")
                    chain(dve.scalar_tensor_tensor(out=probs[:, j % 2, 0:w], in0=SC[:, 0:w], scalar=
                                                   (MLA_QK if kind == "mla" else HEAD) ** -0.5, in1=mask,
                                                   op0=ALU.mult, op1=ALU.add))
                    rows = ((0, 128), (128, 384)) if kind == "mla" else ((0, w),)
                    for i, (lo, hi) in enumerate(rows):
                        ins = dve.tensor_reduce(stat[:, 8 + 4 * (j % 2) + i:9 + 4 * (j % 2) + i],
                                                probs[:, j % 2, lo:hi], AX.X, ALU.max, negate=True)
                    ins.then_inc(max_ready, 1)

                def normalised(j):
                    kind, h, b = JOBS[j]
                    dve.wait_ge(exp_ready, layer * len(JOBS) + j + 1)
                    w = 768 if b == 1 else 384
                    rows = ((0, 128), (128, 384)) if kind == "mla" else ((0, w),)
                    s, r = 16 + 4 * (j % 2), 24 + 4 * (j % 2)
                    chain(dve.reciprocal(stat[:, r:r + len(rows)], stat[:, s:s + len(rows)]))
                    for i, (lo, hi) in enumerate(rows):
                        ins = dve.tensor_scalar(probs[:, j % 2, lo:hi], probs[:, j % 2, lo:hi],
                                                stat[:, r + i:r + i + 1], None, ALU.mult)
                    ins.then_inc(probs_ready, 1)

                def merge(n, j):
                    full(f"branch{n}_{j}")
                    dst = (merged if n == 0 else gates[:, n])[:, 2 * j:2 * j + 2, :]
                    ins = dve.scalar_tensor_tensor(out=dst, in0=gates[:, n, 2 * j:2 * j + 2, :], scalar=1.0,
                                                   in1=pj(f"branch{n}_{j}").rearrange("p (c t) -> p c t", c=2),
                                                   op0=ALU.add, op1=ALU.mult)
                    ins.then_inc(pj_dve, 1)
                    if n == 2:
                        dve.wait_ge(pair_merged, layer * 4 + j + 1)
                        dve.wait_ge(pj_dve, layer * PJ_TOTAL["dve"] + pj_emptied(f"branch2_{j}")[1])
                        m = merged[:, 2 * j:2 * j + 2, :]
                        dve.tensor_tensor(m, m, dst, ALU.add).then_inc(merged_done, 1)

                def low_merged(j):
                    dve.wait_ge(m_hi_ready, layer * 4 + j + 1)
                    dve.scalar_tensor_tensor(out=m_lo[:, 2 * j:2 * j + 2, :], in0=merged[:, 2 * j:2 * j + 2, :],
                                             scalar=0.5, in1=m_hi[:, 2 * j:2 * j + 2, :].bitcast(F32),
                                             op0=ALU.mult, op1=ALU.subtract).then_inc(m_ready, 1)

                masked(0)
                normalised(0)
                for i in range(12):
                    if i == 5:
                        low_o(1)
                    if i < 11:
                        masked(i + 1)
                    after(MIX.index(f"gate{i}"))
                    if i < 11:
                        normalised(i + 1)
                    if i == 5:
                        for j in range(4):
                            merge(0, j)
                        after(MIX.index("branch0"))
                for j in range(4):
                    merge(1, j)
                low_o(2)
                after(MIX.index("branch1"))
                for j in range(4):
                    merge(2, j)
                    if j >= 1:
                        low_merged(j - 1)
                low_merged(3)
                for u in range(31, 35):
                    after(u)
                dve.wait_ge(mix_half_full, layer + 1)
                dve.tensor_tensor(xt[:, 0, :], xt[:, 0, :], SC, ALU.add).then_inc(x_mixed, 1)
                dve.wait_ge(mix_full, layer + 1)
                dve.tensor_tensor(xt[:, 1, :], xt[:, 1, :], TR, ALU.add).then_inc(x_mixed, 1)

                for c in range(4):
                    t, h = divmod(c, 2)
                    full(f"moe_norm{c}")
                    gain = param("g_ffn")[:, 4 * h:4 * h + 4].unsqueeze(2).broadcast_to([P, 4, P])
                    dve.tensor_tensor(hTf[:, 4 * h:4 * h + 4, t * P:(t + 1) * P],
                                      pj(f"moe_norm{c}").rearrange("p (c t) -> p c t", c=4), gain,
                                      ALU.mult).then_inc(pj_dve, 1)
                normed(layer * 2 + 1).then_inc(hn_ready, 1)
                full("logits")
                for t, acc in enumerate((pj("logits"), OV)):
                    ins = dve.scalar_tensor_tensor(out=logits[:, t, :], in0=acc[:, 0:GROUPS + EXPERTS],
                                                   scalar=stat[:, 4 + t:5 + t], in1=param("bias"),
                                                   op0=ALU.mult, op1=ALU.add)
                ins.then_inc(pj_dve, 1)
                dve.wait_ge(pj_dve, layer * PJ_TOTAL["dve"] + pj_emptied("logits")[1])
                group_logits = logits[:, :, 0:GROUPS]

                def over(col, n):
                    return stat[:, col:col + 2].unsqueeze(2).broadcast_to([P, TILES, n])

                def first_largest(hot, values, top, tmp, n):
                    chain(dve.tensor_reduce(stat[:, top:top + 2], values, AX.X, ALU.max))
                    chain(dve.tensor_tensor(tmp, values, over(top, n), ALU.is_equal))
                    order = const(f"first{n}").unsqueeze(1).broadcast_to([P, TILES, n])
                    chain(dve.tensor_tensor(tmp, tmp, order, ALU.mult))
                    chain(dve.tensor_reduce(stat[:, 34:36], tmp, AX.X, ALU.max))
                    return dve.tensor_tensor(hot, tmp, over(34, n), ALU.is_equal)

                first_largest(ghot[:, :, :].bitcast(F32R), group_logits, 32, g1[:, :, :], GROUPS).then_inc(ghot_ready, 1)
                dve.wait_ge(ghot_ready, layer + 1)
                dve.tensor_tensor(g1[:, :, :], group_logits, over(32, GROUPS), ALU.subtract)
                by_group = lambda a: a.rearrange("p t (g e) -> p t g e", e=PER_GROUP)
                wide = lambda a: a.unsqueeze(3).broadcast_to([P, TILES, GROUPS, PER_GROUP])
                dve.tensor_scalar(by_group(r2[:, :, :]), wide(ghot[:, :, :]), -NEG, NEG, ALU.mult, ALU.add)
                chain(dve.tensor_tensor(by_group(r1[:, :, :]), by_group(logits[:, :, GROUPS:]), wide(ghot[:, :, :]),
                                        ALU.mult))
                dve.tensor_tensor(el[:, :, :], r1[:, :, :], r2[:, :, :], ALU.add)
                full("rank")
                rank = pj("rank")[:, 0:TILES * GROUPS]
                gh8 = ghot[:, :, :].rearrange("p t g -> p (t g)")
                chain(dve.scalar_tensor_tensor(out=slot_of[:, :], in0=rank, scalar=1.0, in1=gh8,
                                               op0=ALU.add, op1=ALU.mult))
                dve.tensor_reduce(stat[:, 44:45], pj("rank")[:, 8:12], AX.X, ALU.max).then_inc(pj_dve, 1)
                chain(dve.tensor_scalar(slot_of[:, :], slot_of[:, :], -1.0, None, ALU.add))

                def top_two():
                    chain(first_largest(hot1[:, :, :], el[:, :, :], 40, r1[:, :, :], EXPERTS))
                    chain(dve.scalar_tensor_tensor(out=el[:, :, :], in0=hot1[:, :, :], scalar=2 * NEG,
                                                   in1=el[:, :, :], op0=ALU.mult, op1=ALU.add))
                    chain(first_largest(hot2[:, :, :], el[:, :, :], 42, r1[:, :, :], EXPERTS))
                    dve.tensor_tensor(stat[:, 36:38], stat[:, 42:44], stat[:, 40:42], ALU.subtract).then_inc(route_max, 1)

                def token_weights():
                    dve.wait_ge(route_exp, layer + 1)
                    chain(dve.tensor_reduce(stat[:, 46:48], g1[:, :, :], AX.X, ALU.add))
                    chain(dve.tensor_scalar(stat[:, 48:50], stat[:, 36:38], 1.0, 2.0, ALU.add, ALU.mult))
                    chain(dve.tensor_tensor(stat[:, 50:52], stat[:, 48:50], stat[:, 46:48], ALU.mult))
                    chain(dve.reciprocal(stat[:, 52:54], stat[:, 50:52]))
                    chain(dve.tensor_tensor(stat[:, 54:56], stat[:, 52:54], stat[:, 36:38], ALU.mult))
                    dve.tensor_tensor(hot1[:, :, :], hot1[:, :, :], over(52, EXPERTS), ALU.mult)
                    chain(dve.tensor_tensor(hot2[:, :, :], hot2[:, :, :], over(54, EXPERTS), ALU.mult))
                    chain(dve.tensor_tensor(comb[:, :, :], hot1[:, :, :], hot2[:, :, :], ALU.add))

                def count_passes():
                    chain(dve.tensor_scalar(stat[:, 45:46], stat[:, 44:45], float(P), 1.0, ALU.is_gt, ALU.add))
                    chain(dve.tensor_tensor(rounds_f[:, :], rounds_f[:, :], stat[0:1, 45:46], ALU.add))
                    dve.tensor_copy(rounds[:, :], rounds_f[:, :]).then_inc(routed, 1)
                    assert steps["layer"] == DVE_LAYER_STEPS, steps

                def select(g):
                    for t in range(TILES):
                        ins = dve.tensor_scalar(sel[:, t, :].bitcast(F32R), const("iota"),
                                                slot_of[:, bass.ds(g + t * GROUPS, 1)], None, ALU.is_equal)
                    ins.then_inc(sel_ready, 1)

                def group_weights(g):
                    dve.tensor_copy(gcomb[:, :, :],
                                    comb[:, :, bass.ds(g * PER_GROUP, PER_GROUP)]).then_inc(gcomb_ready, 1)

                def gathered(q, i):
                    dve.wait_ge(gather_full, 2 * q + i + 1)
                    gain = param("g_ffn")[:, 4 * i:4 * i + 4].unsqueeze(2).broadcast_to([P, 4, P])
                    dve.tensor_tensor(xgf[:, 4 * i:4 * i + 4, :],
                                      TR[:, 512 * i:512 * (i + 1)].rearrange("p (c s) -> p c s", s=P), gain,
                                      ALU.mult).then_inc(xgf_ready, 1)

                def low_gathered(q, i):
                    dve.wait_ge(xg_hi_ready, 2 * q + i + 1)
                    half_ = slice(4 * i, 4 * i + 4)
                    dve.tensor_tensor(xg_lo[:, half_, :], xgf[:, half_, :], xg_hi[:, half_, :].bitcast(F32),
                                      ALU.subtract).then_inc(xg_ready, 1)

                def ahead(q, v):
                    n = v + SPLIT_SLOTS
                    split((layer + 1) * MIX_UNITS + q * GROUP_UNITS + n, n, slots=moe_slot(n))

                def group(r, g, last):
                    q = dve.snap(r * GROUPS + g)
                    next_scombs = dve.snap(r * (GROUPS - 1) + g)

                    def hidden(e):
                        if e == 0:
                            dve.wait_ge(scomb_ready, q + 1)
                        dve.wait_ge(th_ready, q * PER_GROUP + e + 1)
                        dve.scalar_tensor_tensor(out=hid[:, e % 2, :], in0=th[:, e % 2, :], scalar=1.0,
                                                 in1=GU[e % 2][:, 0:WIDTH], op0=ALU.add,
                                                 op1=ALU.mult).then_inc(dve_gchain, 1)
                        dve.wait_ge(dve_gchain, q * PER_GROUP + e + 1)
                        dve.scalar_tensor_tensor(out=hid[:, e % 2, :], in0=hid[:, e % 2, :],
                                                 scalar=scomb[:, e:e + 1], in1=GU[e % 2][:, WIDTH:2 * WIDTH],
                                                 op0=ALU.mult, op1=ALU.mult).then_inc(hid_ready, 1)

                    def low_hidden(e):
                        dve.wait_ge(hidT_hi_ready, 3 * q + e + 1)
                        dve.tensor_tensor(hidT_lo[:, :, :], HT[e % 2].rearrange("p (c s) -> p c s", s=P),
                                          hidT_hi[:, :, :].bitcast(F32), ALU.subtract).then_inc(hidT_lo_ready, 1)

                    def low_down(expert):
                        for e, f in DOWN_LOW["dve"]:
                            if e == expert:
                                dve.wait_ge(down_hi_ready, 6 * q + 2 * e + f + 1)
                                cols = slice(f * D_MODEL, (f + 1) * D_MODEL)
                                dve.tensor_tensor(down_lo[:, e, cols], w_down[:, e, cols],
                                                  down_hi[f][:, :].bitcast(F32), ALU.subtract).then_inc(dve_down_ready, 1)

                    hidden(0)
                    ahead(q, 1)
                    low_hidden(0)
                    ahead(q, 2)
                    ahead(q, 3)
                    hidden(1)
                    if not last:
                        select(g + 1)
                        group_weights(g + 1)
                    low_down(1)
                    low_hidden(1)
                    ahead(q, 4)
                    ahead(q, 5)
                    hidden(2)
                    ahead(q, 6)
                    if not last:
                        gathered(q + 1, 0)
                        gathered(q + 1, 1)
                        dve.wait_ge(scomb_full, q + 2)
                        dve.tensor_copy(next_scomb[:, :], SCOMB).then_inc(next_scomb_ready, 1)
                    low_down(2)
                    low_hidden(2)
                    hidden(3)
                    ahead(q, 7)
                    if not last:
                        low_gathered(q + 1, 0)
                        low_gathered(q + 1, 1)
                        dve.wait_ge(hid_ready, q * PER_GROUP + PER_GROUP)
                        dve.wait_ge(next_scomb_ready, next_scombs + 1)
                        dve.tensor_copy(scomb[:, :], next_scomb[:, :]).then_inc(scomb_ready, 1)
                    for n in range(2):
                        dve.wait_ge(y_hi_ready, 2 * q + n + 1)
                        cols = slice(n * 512, (n + 1) * 512)
                        dve.tensor_tensor(y_lo[:, cols], SC[:, cols], y_hi[:, cols].bitcast(F32),
                                          ALU.subtract).then_inc(y_ready, 1)
                    if not last:
                        ahead(q, GROUP_UNITS)
                    for n in range(2):
                        dve.wait_ge(scatter_full, 2 * q + n + 1)
                        cols = slice(n * 512, (n + 1) * 512)
                        for t, (acc, done) in enumerate(((TR, x_moe_first), (SC, x_moe))):
                            ins = dve.tensor_tensor(xt[:, t, cols], xt[:, t, cols], acc[:, cols], ALU.add)
                            if n == 1:
                                ins.then_inc(done, 1)

                def one_pass(r, first_of_layer=False):
                    q = dve.snap(r * GROUPS)
                    select(0)
                    if first_of_layer:
                        top_two()
                        after(MIX_UNITS - 1)
                    for i in range(2):
                        gathered(q, i)
                        low_gathered(q, i)
                    if first_of_layer:
                        token_weights()
                    group_weights(0)
                    if first_of_layer:
                        count_passes()
                    ahead(q, 0)
                    dve.wait_ge(scomb_full, q + 1)
                    dve.tensor_copy(scomb[:, :], SCOMB).then_inc(scomb_ready, 1)
                    with dve.Fori(0, GROUPS - 1) as g:
                        group(r, g, False)
                    group(r, GROUPS - 1, True)
                    dve.tensor_scalar(slot_of[:, :], slot_of[:, :], -float(P), None, ALU.add).then_inc(dve_pchain, 1)
                    alone(dve, dve_pchain, r + 1)

                one_pass(before, True)
                alone(dve, routed, layer + 2)
                end = dve.value_load(rounds[0:1, 0:1], min_val=0, max_val=2 * DEPTH)
                with dve.If(end - before - 1):
                    one_pass(dve.snap(before + 1))

            dve.wait_ge(rstd_ready, 2 * DEPTH + 1)
            dve.wait_ge(gfin_landed, 16)
            for t in range(TILES):
                ins = dve.scalar_tensor_tensor(out=hn[:, t, :], in0=xt[:, t, :], scalar=stat[:, 4 + t:5 + t],
                                               in1=gfin[:, :], op0=ALU.mult, op1=ALU.mult)
                ins.then_inc(out_ready, 1)

        @block.tensor
        def _(pe):
            def product(out_, lhs, rhs, start, stop, **kw):
                pe.matmul(out_, lhs[1], rhs[0], start=start, stop=False, **kw)
                pe.matmul(out_, lhs[0], rhs[1], start=False, stop=False, **kw)
                return pe.matmul(out_, lhs[0], rhs[0], start=False, stop=stop, **kw)

            def weights(u, width, cols):
                slot = u % SPLIT_SLOTS
                return tuple(w[:, slot, 0:width].rearrange("p (k n) -> p k n", n=cols) for w in (w_hi, w_lo))

            def at(pair, *index):
                return tuple(w[(slice(None), *index)] for w in pair)

            def use(n):
                pe.wait_ge(split_lo, RAW_SLOTS + n + 1)

            pe.wait_ge(front_landed, 16)
            hT, o, m = (hT_hi, hT_lo), list(zip(o_hi, o_lo)), (m_hi, m_lo)
            with pe.Fori(0, DEPTH) as layer:
                alone(pe, routed, layer + 1)
                before = pe.value_load(rounds[0:1, 0:1], min_val=0, max_val=2 * DEPTH)
                first = pe.snap(layer * MIX_UNITS + before * MOE_UNITS)

                def bank(name):
                    i = PJ_INDEX[name]
                    if i >= PJ_BANKS:
                        who, count = pj_emptied(PJ[i - PJ_BANKS][0])
                        pe.wait_ge({"act": pj_act, "dve": pj_dve}[who], layer * PJ_TOTAL[who] + count)
                    return pj(name)

                def normed_transposes():
                    for c2 in range(4):
                        b = bank(f"norm{c2}")
                        for c in range(2):
                            for t in range(TILES):
                                ins = pe.matmul(b[:, c * SEQ + t * P:c * SEQ + (t + 1) * P],
                                                xt[:, t, (2 * c2 + c) * P:(2 * c2 + c + 1) * P],
                                                norm_diag[:, t, :], start=True, stop=True)
                        ins.then_inc(pj_full, 1)


                def project(u, fills, cols, act_in=hT, chunks=CHUNKS, wait=None, between=None):
                    w = weights(u, chunks * cols, cols)
                    use(first + u)
                    for i, (name, parts) in enumerate(fills):
                        if i == 2 and between is not None:
                            between()
                        b = bank(name)
                        for col, n, to in parts:
                            for k in range(chunks):
                                if wait is not None and (col, k % 2) == (0, 0):
                                    wait(k)
                                ins = product(b[0:n, to:to + SEQ], at(w, k, slice(col, col + n)),
                                              at(act_in, k), k == 0, k == chunks - 1)
                        ins.then_inc(pj_full, 1)

                def features(name, wait=None):
                    project(MIX.index(name), [(name, [(0, P, 0), (P, P, SEQ)])], WIDTH, wait=wait)

                def tokens(name):
                    u = MIX.index(name)
                    w = weights(u, UNIT, WIDTH)
                    use(first + u)
                    b = bank(name)
                    for t in range(TILES):
                        for k in range(CHUNKS):
                            ins = product(b[:, t * WIDTH:(t + 1) * WIDTH], at(hT, k, slice(t * P, (t + 1) * P)),
                                          at(w, k), k == 0, k == CHUNKS - 1)
                    ins.then_inc(pj_full, 1)

                def act_has(name):
                    pe.wait_ge(pj_act, layer * PJ_TOTAL["act"] + pj_emptied(name)[1])

                def swap(name, src, rows, perm):
                    act_has(name)
                    b = bank(f"sw_{SWAPS[name]}")
                    pe.matmul(b[0:rows, 0:int(np.prod(src.shape[1:]))], const(perm, rows)[:, 0:rows], src,
                              start=True, stop=True).then_inc(pj_full, 1)

                SWAPS = {"kr": "kr", "d0q": "d0q", "d0k": "d0k", "uq0": "mq0", "uq1": "mq1",
                         "d1q": "d1q", "d1k": "d1k", "d2q": "d2q", "d2k": "d2k"}

                def place_of(h):
                    return 2 * (h % 2) + h // 2

                def half(h):
                    return slice(HEAD * (h % 2), HEAD * (h % 2) + HEAD)

                pe.wait_ge(norm_diag_ready, layer + 1)
                normed_transposes()
                features("sbq", wait=lambda k: pe.wait_ge(hT_ready, layer * 4 + k // 2 + 1))
                features("sbk")
                features("cq")
                act_has("sbk")
                for h in range(HEADS):
                    pe.matmul(SC[:, place_of(h) * SEQ:(place_of(h) + 1) * SEQ], sbk[half(h), h // 2, 0:P],
                              sbq[half(h), h // 2, :], start=True, stop=True)
                for h in range(HEADS):
                    ins = pe.matmul(TR[:, 512 * (h % 2) + (h // 2) * P:512 * (h % 2) + (h // 2 + 1) * P],
                                    sbk[half(h), h // 2, P:SEQ], sbq[half(h), h // 2, P:SEQ], start=True, stop=True)
                ins.then_inc(z_full, 1)
                project(MIX.index("ckv"), [("ckv", [(0, P, 0)])], P)
                tokens("sbv")
                project(MIX.index("kr"), [("kr", [(0, MLA_QK, 0)])], MLA_QK)
                pe.wait_ge(lat_sq_ready, layer + 1)
                for t in range(TILES):
                    for c in range(3):
                        col = TILES * (c // 2) + t
                        ins = pe.matmul(OV[:, col:col + 1], lat_sq[:, c, t * P:(t + 1) * P], const("ones")[:, 0:1],
                                        start=c != 1, stop=c != 0)
                ins.then_inc(lat_full, 1)
                features("d0q")
                swap("kr", kr[0:MLA_QK, :], MLA_QK, "swap96")
                features("d0k")
                pe.wait_ge(diag_ready, layer + 1)
                pe.matmul(OV, const("ones"), lat_diag[:, :, :].rearrange("p a b -> p (a b)"), start=True,
                          stop=True).then_inc(lat_spread, 1)
                pe.wait_ge(strict_ready, layer + 1)
                near, far = sb_c[:, 0:1024], sb_c[:, 1024:1536]
                for i in range(2):
                    pe.matmul(SC[:, i * 512:(i + 1) * 512], const("later"), near[:, i * 512:(i + 1) * 512],
                              start=True, stop=False)
                    pe.matmul(SC[:, i * 512:(i + 1) * 512].rearrange("p (h t) -> p h t", t=SEQ)[:, :, P:SEQ],
                              const("ones"), far[:, i * 256:(i + 1) * 256].rearrange("p (h t) -> p h t", t=P),
                              start=False, stop=True)
                for i in range(2):
                    ins = pe.matmul(TR[:, 512 * i:512 * i + 256], const("later"), far[:, i * 256:(i + 1) * 256],
                                    start=True, stop=True)
                ins.then_inc(after_full, 1)
                tokens("d0v")
                swap("d0q", dq[0][:, :, :], P, "swap64")
                swap("d0k", dk[0][:, :, :], P, "swap64")
                pe.wait_ge(lat_ready, layer + 1)
                latq = (lat_hi[:, 0:2, :], lat_lo[:, 0:2, :])
                project(MIX.index("uq"), [(f"uq{i}", [((2 * i + h) * MLA_QK, MLA_QK, h * SEQ) for h in range(2)])
                                          for i in range(2)], HEADS * MLA_QK, act_in=latq, chunks=2)
                features("d1q")
                pe.wait_ge(w_ready, layer + 1)
                for h in range(HEADS):
                    to = OV[half(h), (h // 2) * SEQ:(h // 2 + 1) * SEQ]
                    cols = slice(h * HEAD, (h + 1) * HEAD)
                    i = place_of(h)
                    pe.matmul(to, sbv[:, 0, cols], sb_b[:, i * SEQ:(i + 1) * SEQ], start=True, stop=False)
                    ins = pe.matmul(to[:, P:SEQ], sbv[:, 1, cols], sb_b[:, 1024 + i * P:1024 + (i + 1) * P],
                                    start=False, stop=True)
                ins.then_inc(ov_full, 1)
                for i in range(2):
                    swap(f"uq{i}", mq[0:MLA_QK, 2 * i:2 * i + 2, :], MLA_QK, "swap96")
                u = MIX.index("ukv")
                w = weights(u, 512, 512)
                use(first + u)
                latkv = (lat_hi, lat_lo)
                for i in range(2):
                    b = bank(f"ukv{i}")
                    for h in range(2):
                        col = (2 * i + h) * NOPE
                        ins = product(b[:, h * SEQ:(h + 1) * SEQ], at(w, 0, slice(col, col + P)),
                                      at(latkv, 2), True, True)
                    ins.then_inc(pj_full, 1)
                b = bank("ukvv")
                for t in range(TILES):
                    ins = product(b[:, t * WIDTH:(t + 1) * WIDTH], at(latkv, 2, slice(t * P, (t + 1) * P)),
                                  at(w, 0, slice(WIDTH, 2 * WIDTH)), True, True)
                ins.then_inc(pj_full, 1)
                features("d1k")
                swap("d1q", dq[1][:, :, :], P, "swap64")
                tokens("d1v")
                features("d2q")
                swap("d1k", dk[1][:, :, :], P, "swap64")
                features("d2k")
                swap("d2q", dq[2][:, :, :], P, "swap64")
                tokens("d2v")
                swap("d2k", dk[2][:, :, :], P, "swap64")

                def scores(j):
                    kind, h, b = JOBS[j]
                    if j >= 1:
                        pe.wait_ge(max_ready, layer * len(JOBS) + j)
                    if kind == "mla":
                        pe.wait_ge(roped, layer * len(ROTATIONS) + 5)
                        act_has("ukvv")
                    else:
                        pe.wait_ge(roped, layer * len(ROTATIONS) + 9)
                    for b_, lo, n, g in spans(h, b, kind):
                        qs = slice(b_ * P, (b_ + 1) * P)
                        if kind == "mla":
                            q_, k_ = mq[0:MLA_QK, h, qs], mk[0:MLA_QK, h, 0:n]
                        else:
                            q_, k_ = dq[g][half(h), h // 2, qs], dk[g][half(h), h // 2, 0:n]
                        ins = pe.matmul(SC[:, lo:lo + n], q_, k_, start=True, stop=True)
                    ins.then_inc(sc_full, 1)

                def transposed(j):
                    pe.wait_ge(probs_ready, layer * len(JOBS) + j + 1)
                    if j >= 1:
                        pe.wait_ge(pT_ready, layer * len(JOBS) + j)
                    for i in range(6 if JOBS[j][2] == 1 else 3):
                        ins = pe.transpose(TR[:, i * P:(i + 1) * P], probs[:, j % 2, i * P:(i + 1) * P], const("ident"))
                    ins.then_inc(tr_full, 1)

                def values(j):
                    kind, h, b = JOBS[j]
                    pe.wait_ge(pT_ready, layer * len(JOBS) + j + 1)
                    if j in (0, HEADS):
                        pe.wait_ge(o_ready, layer * BRANCHES + (1 if j == 0 else 2))
                    to = OV[half(h), (h // 2) * SEQ:(h // 2 + 1) * SEQ]
                    cols = slice(h * HEAD, (h + 1) * HEAD)
                    if kind == "mla":
                        pe.matmul(to, mv[:, 0, cols], pT[:, 0:2, :].rearrange("p a b -> p (a b)"), start=True, stop=False)
                        ins = pe.matmul(to[:, P:SEQ], mv[:, 1, cols], pT[:, 2, :], start=False, stop=True)
                    else:
                        n = 3 * (b + 1)
                        for i in range(n):
                            ins = pe.matmul(to[:, b * P:(b + 1) * P], dv[i // (b + 1)][:, i % (b + 1), cols],
                                            pT[:, i, :], start=i == 0, stop=i == n - 1)
                    if j in (HEADS - 1, len(JOBS) - 1):
                        ins.then_inc(ov_full, 1)
                    else:
                        ins.then_inc(av_done, 1)

                def branch(n, between=None):
                    u = MIX.index(f"branch{n}")
                    pe.wait_ge(o_ready, layer * BRANCHES + n + 1)
                    project(u, [(f"branch{n}_{j}", [((2 * j + f) * P, P, f * SEQ) for f in range(2)])
                                for j in range(4)], D_MODEL, act_in=o[n], chunks=2, between=between)

                scores(0)
                for i in range(12):
                    features(f"gate{i}")
                    transposed(i)
                    if i < 11:
                        scores(i + 1)
                    if i >= 1:
                        values(i - 1)
                    if i == 5:
                        branch(0)
                branch(1, between=lambda: values(11))
                branch(2)
                for i in range(4):
                    u = MIX.index(f"out{i}")
                    w = weights(u, UNIT, D_MODEL)
                    use(first + u)
                    pe.wait_ge(m_ready, layer * 4 + i + 1)
                    for t, acc in enumerate((SC, TR)):
                        for n in range(2):
                            for k in range(2):
                                ins = product(acc[:, n * 512:(n + 1) * 512], at(m, 2 * i + k, slice(t * P, (t + 1) * P)),
                                              at(w, k, slice(n * 512, (n + 1) * 512)), (i, k) == (0, 0), (i, k) == (3, 1))
                        if (i, t) == (3, 0):
                            ins.then_inc(mix_half_full, 1)
                    ins.then_inc(out_used if i < 3 else mix_full, 1)

                for c in range(4):
                    t, h = divmod(c, 2)
                    b = bank(f"moe_norm{c}")
                    pe.wait_ge(x_mixed, layer * TILES + t + 1)
                    for i in range(4):
                        ins = pe.transpose(b[:, i * P:(i + 1) * P], xt[:, t, (4 * h + i) * P:(4 * h + i + 1) * P],
                                           const("ident"))
                    ins.then_inc(pj_full, 1)
                b = bank("logits")
                router = param("router").rearrange("p (k n) -> p k n", n=GROUPS + EXPERTS)
                for t, acc in enumerate((b, OV)):
                    for k in range(CHUNKS):
                        if k % 4 == 0:
                            c = 2 * t + k // 4
                            pe.wait_ge(pj_dve, layer * PJ_TOTAL["dve"] + pj_emptied(f"moe_norm{c}")[1])
                        ins = pe.matmul(acc[:, 0:GROUPS + EXPERTS], hTf[:, k, t * P:(t + 1) * P], router[:, k, :],
                                        start=k == 0, stop=k == CHUNKS - 1)
                ins.then_inc(pj_full, 1)
                pe.wait_ge(ghot_ready, layer + 1)
                b = bank("rank")
                for cols, parts in (((0, 4), (("before", 0),)), ((4, 8), (("ones", 0), ("before", 1))),
                                    ((8, 12), (("ones", 0), ("ones", 1)))):
                    for i, (name, t) in enumerate(parts):
                        ins = pe.matmul(b[:, cols[0]:cols[1]], exact(name), ghot[:, t, :].bitcast(F32R), start=i == 0,
                                        stop=i == len(parts) - 1)
                ins.then_inc(pj_full, 1)
                def gather(r, g):
                    q = pe.snap(r * GROUPS + g)
                    pe.wait_ge(sel_ready, q + 1)
                    if isinstance(g, int):
                        pe.wait_ge(hn_ready, layer + 1)
                    else:
                        pe.wait_ge(x_moe, q)
                    for t in range(TILES):
                        pe.matmul(SELT[:, t * P:(t + 1) * P], sel[:, t, :].bitcast(F32R), exact("ident"), start=True, stop=True)
                    for c in range(CHUNKS):
                        for t in range(TILES):
                            ins = pe.matmul(TR[:, c * P:(c + 1) * P], hn[:, t, c * P:(c + 1) * P], sel[:, t, :],
                                            start=t == 0, stop=t == 1)
                        if c % 4 == 3:
                            ins.then_inc(gather_full, 1)

                def slot_weights(r, g):
                    q = pe.snap(r * GROUPS + g)
                    pe.wait_ge(gcomb_ready, q + 1)
                    for t in range(TILES):
                        ins = pe.matmul(SCOMB, sel[:, t, :], gcomb[:, t, :], start=t == 0, stop=t == 1)
                    ins.then_inc(scomb_full, 1)

                def gate_up(q, part, e):
                    v = MOE_SPLIT.index(f"{part}{e}")
                    w = tuple(w[:, 0:UNIT].rearrange("p (k n) -> p k n", n=2 * WIDTH) for w in moe_slot(v))
                    use((layer + 1) * MIX_UNITS + q * GROUP_UNITS + v)
                    i = "AB".index(part)
                    if e == 0:
                        pe.wait_ge(xg_ready, 2 * q + i + 1)
                    for k in range(4):
                        ins = product(GU[e % 2], at((xg_hi, xg_lo), 4 * i + k), at(w, k), (i, k) == (0, 0), (i, k) == (1, 3))
                    ins.then_inc(a_used if i == 0 else gu_full, 1)

                def group(r, g, last):
                    q = pe.snap(r * GROUPS + g)

                    def transposed_hidden(e):
                        pe.wait_ge(hid_ready, q * PER_GROUP + e + 1)
                        if e == 0:
                            pe.wait_ge(selT_ready, q + 1)
                        for f in range(2):
                            ins = pe.transpose(HT[e % 2][:, f * P:(f + 1) * P], hid[:, e % 2, f * P:(f + 1) * P],
                                               const("ident"))
                        ins.then_inc(ht_full, 1)

                    def down(e):
                        if e < 3:
                            pe.wait_ge(hidT_lo_ready, 3 * q + e + 1)
                        else:
                            pe.wait_ge(hidT_ready, q + 1)
                        if e < 3:
                            for who, ready in (("pool", pool_down_ready), ("dve", dve_down_ready)):
                                shares = DOWN_LOW[who]
                                if any(share[0] == e for share in shares):
                                    pe.wait_ge(ready, len(shares) * q + sum(share[0] <= e for share in shares))
                        else:
                            pe.wait_ge(down_landed[e], 16 * (q + 1))
                        order = [(f, n) for n in range(2) for f in range(2)]
                        for i, (f, n) in enumerate(order if e == 3 else sorted(order)):
                            cols = slice(n * 512, (n + 1) * 512)
                            rows = slice(f * D_MODEL + n * 512, f * D_MODEL + (n + 1) * 512)
                            start, stop = (e, f) == (0, 0), (e, f) == (3, 1)
                            if e < 3:
                                ins = product(SC[:, cols], (hidT_hi[:, f, :], hidT_lo[:, f, :]),
                                              (down_hi[f][:, cols], down_lo[:, e, rows]), start, stop)
                            else:
                                ins = pe.matmul(SC[:, cols], hidT[:, f, :], w_down[:, e, rows], start=start, stop=stop)
                            if (e, i) == (2, 1):
                                transposed_hidden(3)
                            if (e, i) == (3, 1):
                                ins.then_inc(y_half_full, 1)
                        ins.then_inc(d_used if e < 3 else y_full, 1)

                    for e in range(1, PER_GROUP):
                        gate_up(q, "A", e)
                        transposed_hidden(e - 1)
                        gate_up(q, "B", e)
                        down(e - 1)
                        if e == 2 and not last:
                            gather(r, g + 1)
                            slot_weights(r, g + 1)
                    down(PER_GROUP - 1)
                    if not last:
                        gate_up(q + 1, "A", 0)
                    for n in range(2):
                        pe.wait_ge(y_ready, 2 * q + n + 1)
                        cols = slice(n * 512, (n + 1) * 512)
                        for t, acc in enumerate((TR, SC)):
                            pe.matmul(acc[:, cols], selT[:, t, :], y_lo[:, cols], start=True, stop=False)
                            ins = pe.matmul(acc[:, cols], selT[:, t, :], y_hi[:, cols], start=False, stop=True)
                        ins.then_inc(scatter_full, 1)
                    if not last:
                        gate_up(q + 1, "B", 0)

                def one_pass(r, first_of_layer=False):
                    gather(r, 0)
                    for part in "AB":
                        gate_up(pe.snap(r * GROUPS), part, 0)
                    slot_weights(r, 0)
                    with pe.Fori(0, GROUPS - 1) as g:
                        group(r, g, False)
                    group(r, GROUPS - 1, True)

                one_pass(before, True)
                alone(pe, routed, layer + 2)
                end = pe.value_load(rounds[0:1, 0:1], min_val=0, max_val=2 * DEPTH)
                with pe.If(end - before - 1):
                    one_pass(pe.snap(before + 1))


def shape_constants():
    c = {}
    i = np.arange(P)
    c["ident"] = np.eye(P)
    c["before"] = i[:, None] < i[None, :]
    c["later"] = i[:, None] > i[None, :]
    c["ones"] = np.ones((P, P))
    swap = np.zeros((P, P))
    for f in range(P):
        swap[(f + 32 if f % 64 < 32 else f - 32), f] = -1 if f % 64 < 32 else 1
    c["swap64"] = swap
    swap = np.zeros((P, P))
    for f in range(NOPE, MLA_QK):
        swap[(f + 16 if f < NOPE + 16 else f - 16), f] = -1 if f < NOPE + 16 else 1
    c["swap96"] = swap
    c["iota"] = np.broadcast_to(i, (P, P))
    query, key = np.arange(SEQ), np.arange(SEQ)
    c["sb_mask"] = key[:P, None] < query[None, :]
    causal = np.where(key[None, :] <= query[:, None], 0.0, NEG)
    c["mla_mask"] = np.concatenate([causal[:P, :P], causal[P:, :]], 1)
    span = query[:, None] - key[None, :]
    dil = [np.where((span >= 0) & (span <= w) & (span % d == 0), 0.0, NEG) for w, d in DIL]
    c["dil_mask0"] = np.concatenate([m[:P, :P] for m in dil], 1)
    c["dil_mask1"] = np.concatenate([m[P:, :] for m in dil], 1)
    f32 = np.float32
    for dim, rows, lo in ((HEAD, P, 0), (ROPE, MLA_QK, NOPE)):
        inv = f32(THETA) ** (-np.arange(0, dim, 2, dtype=f32) / f32(dim))
        col = np.zeros((P, 1), f32)
        for f in range(lo, rows):
            col[f, 0] = inv[(f - lo) % (dim // 2)]
        c["freq64" if dim == HEAD else "freq96"] = col
    c["first4"] = np.broadcast_to(np.arange(4, 0, -1), (P, 4))
    c["first16"] = np.broadcast_to(np.arange(16, 0, -1), (P, 16))
    c["minus_half"] = np.full((P, 4), -0.5)
    out = np.zeros((P, CONST_COLS), f32)
    for name, (lo, hi) in CONST.items():
        out[:, lo:hi] = c[name]
    return out


def rows_of_chunks(w):
    n = w.shape[-1]
    return w.reshape(-1, P, n).transpose(1, 0, 2).reshape(P, -1)


def unit_of(parts):
    out = np.zeros((P, UNIT), np.float32)
    out[:, :parts.shape[1]] = parts
    return out


def lay_out(inputs):
    mix = np.zeros((DEPTH, MIX_UNITS, P, UNIT), np.float32)
    moe = np.zeros((DEPTH, GROUPS, len(MOE), P, UNIT), np.float32)
    params = np.zeros((DEPTH, P, PARAM_COLS), np.float32)
    col = {}
    at = 0
    for name, n in (("sbq", 256), ("sbk", 256), ("sbv", 256), ("cq", 256), ("ckv", 128), ("kr", 32)):
        col[name] = (at, n)
        at += n
    for g in range(3):
        for c in "qkv":
            col[f"d{g}{c}"] = (at, 256)
            at += 256
    for i in range(12):
        col[f"gate{i}"] = (at, 256)
        at += 256
    for layer in range(DEPTH):
        w_in = inputs["w_in"][layer]
        for u, name in enumerate(MIX):
            if name == "kr":
                lo, n = col[name]
                padded = np.zeros((D_MODEL, MLA_QK), np.float32)
                padded[:, NOPE:] = w_in[:, lo:lo + n]
                part = rows_of_chunks(padded)
            elif name in col:
                lo, n = col[name]
                part = rows_of_chunks(w_in[:, lo:lo + n])
            elif name == "uq":
                part = rows_of_chunks(inputs["w_uq"][layer])
            elif name == "ukv":
                by_head = inputs["w_ukv"][layer].reshape(P, HEADS, 2, NOPE)
                part = by_head.transpose(0, 2, 1, 3).reshape(P, 2 * WIDTH)
            elif name[:6] == "branch":
                part = rows_of_chunks(inputs["w_branch"][layer, int(name[6:])])
            else:
                i = int(name[3:])
                part = rows_of_chunks(inputs["w_out"][layer, 2 * i * P:(2 * i + 2) * P])
            mix[layer, u] = unit_of(part)
        for g in range(GROUPS):
            for u, name in enumerate(MOE):
                e = g * PER_GROUP + int(name[1])
                if name[0] == "D":
                    part = rows_of_chunks(inputs["w_down"][layer, e])
                else:
                    rows = slice(0, 512) if name[0] == "A" else slice(512, 1024)
                    part = rows_of_chunks(np.concatenate([inputs["w_gate"][layer, e, rows],
                                                          inputs["w_up"][layer, e, rows]], 1))
                moe[layer, g, u] = unit_of(part)
        by_name = {
            "g_mix": inputs["g_mix"][layer].reshape(CHUNKS, P).T, "g_ffn": inputs["g_ffn"][layer].reshape(CHUNKS, P).T,
            "g_q": inputs["g_q_lat"][layer].reshape(2, P).T, "g_kv": inputs["g_kv_lat"][layer].reshape(1, P).T,
            "router": rows_of_chunks(np.concatenate([inputs["w_group_router"][layer],
                                                     inputs["w_expert_router"][layer]], 1)),
            "bias": np.broadcast_to(np.concatenate([inputs["b_group_router"][layer],
                                                    inputs["b_expert_router"][layer]]), (P, 20)),
        }
        for name, (lo, hi) in PARAM.items():
            params[layer, :, lo:hi] = by_name[name]
    return mix, moe, params


def kernel(**inputs):
    import concourse.bacc as bacc
    from concourse import mybir
    from concourse.bass_utils import run_bass_kernel_spmd

    inputs = {name: np.ascontiguousarray(a) for name, a in inputs.items()}
    mix, moe, params = lay_out(inputs)
    arrays = {
        "x": inputs["x"][0], "positions": inputs["positions"], "mix_weights": mix, "moe_weights": moe,
        "params": params, "g_final": inputs["g_final"].reshape(1, D_MODEL), "constants": shape_constants(),
    }
    nc = bacc.Bacc("TRN2", target_bir_lowering=False, num_devices=1)
    args = [nc.dram_tensor(name, a.shape, mybir.dt.from_np(a.dtype), kind="ExternalInput").ap()
            for name, a in arrays.items()]
    out = nc.dram_tensor("out", (SEQ, D_MODEL), mybir.dt.float32, kind="ExternalOutput").ap()
    build(nc, *args, out)
    r = run_bass_kernel_spmd(nc, [arrays], core_ids=[0])
    return r.results[0]["out"].reshape(1, SEQ, D_MODEL)
```
